# Optimizing a Trainium2 kernel written in Bass

```python
import math
import jax
import jax.numpy as jnp
from jax import lax
import numpy as np

D_MODEL = 1024
BATCH = 1
SEQ = 256
DEPTH = 2
DEC_BATCH = 8
DEC_SEQ = 8
PAST_LEN = 256
PAGE_SIZE = 128

N_EVEN = (DEPTH + 1) // 2
N_ODD = DEPTH // 2
H_A = 8
HD_A = 64
ROT_DIM = HD_A // 4
ROPE_THETA = 500000.0
MOBA_BLOCK = 256
MOBA_TOPK = 3
Q_CHUNK = 64
H_R = 8
DK_R = 64
DV_R = 128
RET_CHUNK = 128
S5_GROUP = 16
S5_GROUPS = D_MODEL // S5_GROUP
S5_STATE = 64
MOE_GROUPS = 4
MOE_PER_GROUP = 8
N_EXPERTS = MOE_GROUPS * MOE_PER_GROUP
MOE_TOPK = 2
D_EXPERT = D_MODEL // 2
MOE_BLOCK = 128
A_W = H_A * HD_A
R_QK = H_R * DK_R
R_V = H_R * DV_R
IN_EVEN = 3 * A_W + 2 * R_QK + 2 * R_V
MIX_EVEN = A_W + R_V
SPLIT_EVEN = (A_W, 2 * A_W, 3 * A_W, 3 * A_W + R_QK, 3 * A_W + 2 * R_QK, 3 * A_W + 2 * R_QK + R_V)
NEG_INF = -1e30
EPS = 1e-6

kernel_name = 'hybrid_moba_retention_s5_hmoe_step'

def _rms(x, g):
    xf = x.astype(jnp.float32)
    y = xf * lax.rsqrt(jnp.mean(xf * xf, axis=-1, keepdims=True) + EPS)
    return (y * g.astype(jnp.float32)).astype(x.dtype)

def _partial_rope(x, pos):
    half = ROT_DIM // 2
    inv = ROPE_THETA ** (-jnp.arange(half, dtype=jnp.float32) / half)
    ang = pos.astype(jnp.float32)[:, None] * inv[None, :]
    cos = jnp.cos(ang)[None, :, None, :]
    sin = jnp.sin(ang)[None, :, None, :]
    xf = x.astype(jnp.float32)
    x1, x2, rest = xf[..., :half], xf[..., half:ROT_DIM], xf[..., ROT_DIM:]
    return jnp.concatenate([x1 * cos - x2 * sin, x2 * cos + x1 * sin, rest], axis=-1).astype(x.dtype)

def _retnet_rotate(x, pos):
    n = DK_R // 2
    inv = 1.0 / (10000.0 ** jnp.linspace(0.0, 1.0, n, dtype=jnp.float32))
    ang = pos.astype(jnp.float32)[:, None] * inv[None, :]
    cos = jnp.cos(ang)[None, :, None, :]
    sin = jnp.sin(ang)[None, :, None, :]
    xf = x.astype(jnp.float32).reshape(x.shape[:-1] + (n, 2))
    xe, xo = xf[..., 0], xf[..., 1]
    return jnp.stack([xe * cos - xo * sin, xo * cos + xe * sin], axis=-1).reshape(x.shape)

def _moba_attention(q, k, v, start):
    n, tq, h, hd = q.shape
    qc = min(Q_CHUNK, tq)
    n_qc = -(-tq // qc)
    tq_pad = n_qc * qc
    q = jnp.pad(q, ((0, 0), (0, tq_pad - tq), (0, 0), (0, 0)))
    pos = (start + jnp.arange(tq_pad)).reshape(n_qc, qc)
    seq_len = k.shape[1]
    n_blk = -(-seq_len // MOBA_BLOCK)
    pad = n_blk * MOBA_BLOCK - seq_len
    def blocks(a):
        a = jnp.pad(a, ((0, 0), (0, pad), (0, 0), (0, 0)))
        return a.reshape(n, n_blk, MOBA_BLOCK, h, hd).transpose(0, 3, 1, 2, 4)
    kb, vb = blocks(k), blocks(v)
    qs = q.reshape(n, n_qc, qc, h, hd)
    scale = hd ** -0.5
    n_cols_pad = max(0, MOBA_TOPK - n_blk)
    hidx = jnp.arange(h)[:, None, None]

    def per_seq(args):
        q_n, kb_n, vb_n = args
        kmean = jnp.mean(kb_n.astype(jnp.float32), axis=2)

        def per_chunk(cargs):
            qq, pp = cargs
            bq = pp // MOBA_BLOCK
            s = jnp.einsum('qhd,hjd->hqj', qq.astype(jnp.float32), kmean)
            s = jnp.pad(s, ((0, 0), (0, 0), (0, n_cols_pad)), constant_values=NEG_INF)
            j = jnp.arange(s.shape[-1])
            s = jnp.where(j[None, None, :] < bq[None, :, None], s, NEG_INF)
            _, top = lax.top_k(s, MOBA_TOPK)
            own = jnp.broadcast_to(jnp.minimum(bq, n_blk - 1)[None, :, None], (h, qc, 1))
            sel = jnp.concatenate([jnp.minimum(top, n_blk - 1), own], axis=-1)
            kg = kb_n[hidx, sel]
            vg = vb_n[hidx, sel]
            sc = jnp.einsum('qhd,hqrkd->hqrk', qq, kg, preferred_element_type=jnp.float32) * scale
            slot_ok = jnp.arange(MOBA_TOPK)[None, :] < bq[:, None]
            own_ok = jnp.arange(MOBA_BLOCK)[None, :] <= (pp - bq * MOBA_BLOCK)[:, None]
            mask = jnp.concatenate([jnp.broadcast_to(slot_ok[:, :, None], (qc, MOBA_TOPK, MOBA_BLOCK)),
                                    own_ok[:, None, :]], axis=1)
            sc = jnp.where(mask[None], sc, NEG_INF)
            p = jax.nn.softmax(sc.reshape(h, qc, -1), axis=-1).reshape(sc.shape)
            return jnp.einsum('hqrk,hqrke->qhe', p, vg.astype(jnp.float32))

        return lax.map(per_chunk, (q_n, pos))

    o = lax.map(per_seq, (qs, kb, vb))
    return o.reshape(n, tq_pad, h, hd)[:, :tq]

def _retention(q, k, v, s0):
    n, t, h, _ = q.shape
    c = min(RET_CHUNK, t)
    n_chunks = t // c
    log_g = jnp.log(1.0 - 2.0 ** (-5.0 - jnp.arange(H_R, dtype=jnp.float32)))
    i = jnp.arange(c, dtype=jnp.float32)
    diff = i[:, None] - i[None, :]
    dmat = jnp.where(diff >= 0, jnp.exp(jnp.maximum(diff, 0.0)[None] * log_g[:, None, None]), 0.0)
    dq = jnp.exp((i + 1.0)[:, None] * log_g[None, :])
    dk = jnp.exp((c - 1.0 - i)[:, None] * log_g[None, :])
    dc = jnp.exp(c * log_g)

    def step(s, chunk):
        qc, kc, vc = chunk
        att = jnp.einsum('nihd,njhd->nhij', qc, kc) * dmat[None]
        o = (jnp.einsum('nhij,njhe->nihe', att, vc)
             + jnp.einsum('nihd,nhde->nihe', qc * dq[None, :, :, None], s))
        s = s * dc[None, :, None, None] + jnp.einsum('njhd,njhe->nhde', kc * dk[None, :, :, None], vc)
        return s, o

    def to_chunks(a):
        return a.reshape(n, n_chunks, c, h, a.shape[-1]).transpose(1, 0, 2, 3, 4)

    s_fin, o = lax.scan(step, s0, (to_chunks(q), to_chunks(k), to_chunks(v)))
    return o.transpose(1, 0, 2, 3, 4).reshape(n, t, h, v.shape[-1]), s_fin

def _even_mixer(xn, start, past_k, past_v, s0, w_in, w_out):
    n, t, _ = xn.shape
    pos = start + jnp.arange(t)
    z = xn @ w_in
    q_a, k_a, v_a, q_r, k_r, v_r, g_r = jnp.split(z, SPLIT_EVEN, axis=-1)
    q_a = _partial_rope(q_a.reshape(n, t, H_A, HD_A), pos)
    k_a = _partial_rope(k_a.reshape(n, t, H_A, HD_A), pos)
    v_a = v_a.reshape(n, t, H_A, HD_A)
    k_all = k_a if past_k is None else jnp.concatenate([past_k.astype(k_a.dtype), k_a], axis=1)
    v_all = v_a if past_v is None else jnp.concatenate([past_v.astype(v_a.dtype), v_a], axis=1)
    o_a = _moba_attention(q_a, k_all, v_all, start)
    q_r = _retnet_rotate(q_r.reshape(n, t, H_R, DK_R), pos)
    k_r = _retnet_rotate(k_r.reshape(n, t, H_R, DK_R), pos) * (DK_R ** -0.5)
    v_r = v_r.reshape(n, t, H_R, DV_R).astype(jnp.float32)
    o_r, s_new = _retention(q_r, k_r, v_r, s0.astype(jnp.float32))
    o_r = o_r * lax.rsqrt(jnp.mean(o_r * o_r, axis=-1, keepdims=True) + EPS)
    o_r = o_r.reshape(n, t, R_V) * jax.nn.silu(g_r.astype(jnp.float32))
    mixed = jnp.concatenate([o_a.reshape(n, t, A_W), o_r], axis=-1).astype(xn.dtype)
    return mixed @ w_out, k_a, v_a, s_new

def _complex_affine_combine(e1, e2):
    a1r, a1i, b1r, b1i = e1
    a2r, a2i, b2r, b2i = e2
    return (a2r * a1r - a2i * a1i,
            a2r * a1i + a2i * a1r,
            a2r * b1r - a2i * b1i + b2r,
            a2r * b1i + a2i * b1r + b2i)

def _s5_mixer(u, s0_re, s0_im, lam_re, lam_im, log_dt, b_re, b_im, c_re, c_im, d_skip, w_glu, b_glu):
    n, t, _ = u.shape
    f32 = jnp.float32
    uf = u.astype(f32)
    ug = uf.reshape(n, t, S5_GROUPS, S5_GROUP)
    lr = lam_re.astype(f32)
    li = lam_im.astype(f32)
    dt = jnp.exp(log_dt.astype(f32))[:, None]
    mag = jnp.exp(lr * dt)
    ang = li * dt
    ab_re = mag * jnp.cos(ang)
    ab_im = mag * jnp.sin(ang)
    den = lr * lr + li * li
    nr = ab_re - 1.0
    co_re = (nr * lr + ab_im * li) / den
    co_im = (ab_im * lr - nr * li) / den
    br = b_re.astype(f32)
    bi = b_im.astype(f32)
    bb_re = co_re[..., None] * br - co_im[..., None] * bi
    bb_im = co_re[..., None] * bi + co_im[..., None] * br
    bu_re = jnp.einsum('ntgc,gpc->ntgp', ug, bb_re)
    bu_im = jnp.einsum('ntgc,gpc->ntgp', ug, bb_im)
    a_re = jnp.broadcast_to(ab_re, (1, t) + ab_re.shape)
    a_im = jnp.broadcast_to(ab_im, (1, t) + ab_im.shape)
    A_re, A_im, X_re, X_im = lax.associative_scan(_complex_affine_combine, (a_re, a_im, bu_re, bu_im), axis=1)
    sr = s0_re.astype(f32)[:, None]
    si = s0_im.astype(f32)[:, None]
    x_re = X_re + A_re * sr - A_im * si
    x_im = X_im + A_re * si + A_im * sr
    y = (jnp.einsum('gcp,ntgp->ntgc', c_re.astype(f32), x_re)
         - jnp.einsum('gcp,ntgp->ntgc', c_im.astype(f32), x_im)).reshape(n, t, D_MODEL)
    y = y + d_skip.astype(f32) * uf
    zg = jax.nn.gelu(y)
    hg = zg @ w_glu.astype(f32) + b_glu.astype(f32)
    out = hg[..., :D_MODEL] * jax.nn.sigmoid(hg[..., D_MODEL:])
    return out.astype(u.dtype), x_re[:, -1], x_im[:, -1]

def _hier_moe(x, w_group, b_group, w_expert, b_expert, w13, w2):
    n, t, d = x.shape
    xf = x.reshape(n * t, d)
    n_tok = n * t
    pg = jax.nn.softmax((xf @ w_group).astype(jnp.float32) + b_group.astype(jnp.float32), axis=-1)
    g = jnp.argmax(pg, axis=-1)
    wg = jnp.take_along_axis(pg, g[:, None], axis=1)[:, 0]
    le = ((xf @ w_expert).astype(jnp.float32) + b_expert.astype(jnp.float32)).reshape(n_tok, MOE_GROUPS, MOE_PER_GROUP)
    le_g = jnp.take_along_axis(le, g[:, None, None], axis=1)[:, 0]
    tv, ti = lax.top_k(le_g, MOE_TOPK)
    we = jax.nn.softmax(tv, axis=-1) * wg[:, None]
    eid = g[:, None] * MOE_PER_GROUP + ti
    n_assign = n_tok * MOE_TOPK
    e_flat = eid.reshape(-1)
    tok_flat = jnp.repeat(jnp.arange(n_tok), MOE_TOPK)
    w_flat = we.reshape(-1)
    order = jnp.argsort(e_flat)
    e_s, tok_s, w_s = e_flat[order], tok_flat[order], w_flat[order]
    counts = jnp.bincount(e_flat, length=N_EXPERTS)
    pc = (counts + MOE_BLOCK - 1) // MOE_BLOCK * MOE_BLOCK
    pend = jnp.cumsum(pc)
    pstart = pend - pc
    start = jnp.cumsum(counts) - counts
    dest = pstart[e_s] + jnp.arange(n_assign) - start[e_s]
    n_blocks = -(-n_assign // MOE_BLOCK) + N_EXPERTS
    rows = n_blocks * MOE_BLOCK
    buf_tok = jnp.zeros((rows,), jnp.int32).at[dest].set(tok_s.astype(jnp.int32))
    buf_w = jnp.zeros((rows,), jnp.float32).at[dest].set(w_s)
    blk_e = jnp.minimum(jnp.searchsorted(pend, jnp.arange(n_blocks) * MOE_BLOCK, side='right'), N_EXPERTS - 1)

    def run_block(args):
        toks, e = args
        hb = xf[toks] @ w13[e]
        return (jax.nn.silu(hb[:, :D_EXPERT]) * hb[:, D_EXPERT:]) @ w2[e]

    yb = lax.map(run_block, (buf_tok.reshape(n_blocks, MOE_BLOCK), blk_e))
    y = jnp.zeros((n_tok, d), jnp.float32).at[buf_tok].add(yb.reshape(rows, d).astype(jnp.float32) * buf_w[:, None])
    return y.astype(x.dtype).reshape(n, t, d)

def setup_inputs(seed: int = 0) -> dict:
    key = jax.random.key(seed)
    keys = jax.random.split(key, 32)
    f32 = jnp.float32
    n_pages = PAST_LEN // PAGE_SIZE
    n_pool = (DEC_BATCH * n_pages * 5) // 4

    def nrm(i, shape, scale):
        return jax.random.normal(keys[i], shape, f32) * scale

    page_table = jax.random.permutation(keys[7], n_pool)[: DEC_BATCH * n_pages].reshape(DEC_BATCH, n_pages).astype(jnp.int32)
    log_lo, log_hi = math.log(0.001), math.log(0.1)
    return {
        'x_prompt': nrm(0, (BATCH, SEQ, D_MODEL), 1.0),
        'x_sample': nrm(1, (DEC_BATCH, DEC_SEQ, D_MODEL), 1.0),
        'cache_k': nrm(2, (N_EVEN, n_pool, PAGE_SIZE, H_A, HD_A), 1.0),
        'cache_v': nrm(3, (N_EVEN, n_pool, PAGE_SIZE, H_A, HD_A), 1.0),
        'state_ret': nrm(4, (N_EVEN, DEC_BATCH, H_R, DK_R, DV_R), 0.5),
        'state_s5_re': nrm(5, (N_ODD, DEC_BATCH, S5_GROUPS, S5_STATE), 0.5),
        'state_s5_im': nrm(6, (N_ODD, DEC_BATCH, S5_GROUPS, S5_STATE), 0.5),
        'page_table': page_table,
        'norm1': 1.0 + nrm(8, (DEPTH, D_MODEL), 0.02),
        'norm2': 1.0 + nrm(9, (DEPTH, D_MODEL), 0.02),
        'norm_f': 1.0 + nrm(10, (D_MODEL,), 0.02),
        'w_in_even': nrm(11, (N_EVEN, D_MODEL, IN_EVEN), D_MODEL ** -0.5),
        'w_out_even': nrm(12, (N_EVEN, MIX_EVEN, D_MODEL), MIX_EVEN ** -0.5),
        's5_lam_re': -0.5 + nrm(13, (N_ODD, S5_GROUPS, S5_STATE), 0.01),
        's5_lam_im': math.pi * jnp.arange(S5_STATE, dtype=f32)[None, None, :] + nrm(14, (N_ODD, S5_GROUPS, S5_STATE), 0.01),
        's5_log_dt': log_lo + jax.random.uniform(keys[15], (N_ODD, S5_GROUPS), f32) * (log_hi - log_lo),
        's5_b_re': nrm(16, (N_ODD, S5_GROUPS, S5_STATE, S5_GROUP), (2.0 * S5_GROUP) ** -0.5),
        's5_b_im': nrm(17, (N_ODD, S5_GROUPS, S5_STATE, S5_GROUP), (2.0 * S5_GROUP) ** -0.5),
        's5_c_re': nrm(18, (N_ODD, S5_GROUPS, S5_GROUP, S5_STATE), (2.0 * S5_STATE) ** -0.5),
        's5_c_im': nrm(19, (N_ODD, S5_GROUPS, S5_GROUP, S5_STATE), (2.0 * S5_STATE) ** -0.5),
        's5_d': nrm(20, (N_ODD, D_MODEL), 1.0),
        's5_w_glu': nrm(21, (N_ODD, D_MODEL, 2 * D_MODEL), D_MODEL ** -0.5),
        's5_b_glu': nrm(22, (N_ODD, 2 * D_MODEL), 0.01),
        'moe_w_group': nrm(23, (DEPTH, D_MODEL, MOE_GROUPS), D_MODEL ** -0.5),
        'moe_b_group': nrm(24, (DEPTH, MOE_GROUPS), 0.01),
        'moe_w_expert': nrm(25, (DEPTH, D_MODEL, N_EXPERTS), D_MODEL ** -0.5),
        'moe_b_expert': nrm(26, (DEPTH, N_EXPERTS), 0.01),
        'moe_w13': nrm(27, (DEPTH, N_EXPERTS, D_MODEL, 2 * D_EXPERT), D_MODEL ** -0.5),
        'moe_w2': nrm(28, (DEPTH, N_EXPERTS, D_EXPERT, D_MODEL), D_EXPERT ** -0.5),
    }

def reference(x_prompt, x_sample, cache_k, cache_v, state_ret, state_s5_re, state_s5_im, page_table,
              norm1, norm2, norm_f, w_in_even, w_out_even,
              s5_lam_re, s5_lam_im, s5_log_dt, s5_b_re, s5_b_im, s5_c_re, s5_c_im, s5_d, s5_w_glu, s5_b_glu,
              moe_w_group, moe_b_group, moe_w_expert, moe_b_expert, moe_w13, moe_w2):
    n_p, seq, _ = x_prompt.shape
    n_s = x_sample.shape[0]
    page = cache_k.shape[2]
    past_len = page_table.shape[1] * page
    hp, hs = x_prompt, x_sample
    k_p, v_p, k_s, v_s, r_p, r_s = [], [], [], [], [], []
    sr_p, si_p, sr_s, si_s = [], [], [], []
    for li in range(DEPTH):
        xn_p = _rms(hp, norm1[li])
        xn_s = _rms(hs, norm1[li])
        if li % 2 == 0:
            e = li // 2
            past_k = cache_k[e, page_table].reshape(n_s, past_len, H_A, HD_A)
            past_v = cache_v[e, page_table].reshape(n_s, past_len, H_A, HD_A)
            zero_ret = jnp.zeros((n_p, H_R, DK_R, DV_R), jnp.float32)
            o_p, kk, vv, st = _even_mixer(xn_p, 0, None, None, zero_ret, w_in_even[e], w_out_even[e])
            k_p.append(kk.reshape(n_p, seq // page, page, H_A, HD_A))
            v_p.append(vv.reshape(n_p, seq // page, page, H_A, HD_A))
            r_p.append(st)
            o_s, kk, vv, st = _even_mixer(xn_s, past_len, past_k, past_v, state_ret[e], w_in_even[e], w_out_even[e])
            k_s.append(kk)
            v_s.append(vv)
            r_s.append(st)
        else:
            o = li // 2
            prm = (s5_lam_re[o], s5_lam_im[o], s5_log_dt[o], s5_b_re[o], s5_b_im[o], s5_c_re[o], s5_c_im[o],
                   s5_d[o], s5_w_glu[o], s5_b_glu[o])
            zero_s5 = jnp.zeros((n_p, S5_GROUPS, S5_STATE), jnp.float32)
            o_p, a_re, a_im = _s5_mixer(xn_p, zero_s5, zero_s5, *prm)
            sr_p.append(a_re)
            si_p.append(a_im)
            o_s, a_re, a_im = _s5_mixer(xn_s, state_s5_re[o], state_s5_im[o], *prm)
            sr_s.append(a_re)
            si_s.append(a_im)
        hp = hp + o_p
        hs = hs + o_s
        hp = hp + _hier_moe(_rms(hp, norm2[li]), moe_w_group[li], moe_b_group[li], moe_w_expert[li],
                            moe_b_expert[li], moe_w13[li], moe_w2[li])
        hs = hs + _hier_moe(_rms(hs, norm2[li]), moe_w_group[li], moe_b_group[li], moe_w_expert[li],
                            moe_b_expert[li], moe_w13[li], moe_w2[li])
    y_prompt = _rms(hp, norm_f)
    y_sample = _rms(hs, norm_f)
    return (y_prompt, y_sample, jnp.stack(k_p), jnp.stack(v_p), jnp.stack(k_s), jnp.stack(v_s),
            jnp.stack(r_p), jnp.stack(r_s), jnp.stack(sr_p), jnp.stack(si_p), jnp.stack(sr_s), jnp.stack(si_s))


_drawn_inputs = setup_inputs


def setup_inputs(seed=0):
    import zlib

    import numpy as np

    out = dict(_drawn_inputs(seed))
    spreads = {}
    factors = {'norm_f': 2.905, 's5_lam_re': 4.353, 'moe_b_group': 3.342}
    for name, (base, spread) in spreads.items():
        noise = np.random.default_rng([zlib.crc32(name.encode()), seed]).standard_normal(out[name].shape)
        drawn = base * np.exp(spread * noise) if base else spread * noise
        out[name] = jnp.asarray(drawn.astype(out[name].dtype))
    for name, factor in factors.items():
        out[name] = (out[name] * factor).astype(out[name].dtype)
    return out
```

```python
from contextlib import ExitStack, contextmanager

import concourse.bass as bass
import numpy as np
from concourse import mybir

F32 = mybir.dt.float32
I32 = mybir.dt.int32
U32 = mybir.dt.uint32
ALU = mybir.AluOpType
ACT = mybir.ActivationFunctionType
X = mybir.AxisListType.X

P = 128
D = 1024
KC = D // P
TILES = 3
ROWS = (128, 128, 64)
NTOK = sum(ROWS)
NSEQ, DSEQ = 8, 8
NS = NSEQ * DSEQ
H, HD = 8, 64
ROT = 8
DK, DV = 64, 128
PAGE = 128
IN_W = 4608
MIX_W = 1536
KM = MIX_W // P
QA, KA, VA, QR, KR, VR, GR = 0, 512, 1024, 1536, 2048, 2560, 3584
NEG = -1e30
EPS = 1e-6
GROUPS, PER, NE = 4, 8, 32
DE = 512
SLOT = 64
MAXB = NE + (2 * NTOK - NE) // SLOT
NBLK = MAXB + 3
MINB = 2 * NTOK // SLOT
G5, C5, S5 = 64, 16, 64
CH = 8
NCH = NTOK // CH
PCH = 256 // CH


def constants():
    f = np.float32
    pos = np.concatenate([np.arange(256), 256 + np.arange(NS) % DSEQ]).astype(f)
    out = {}

    def tiles(a):
        b = np.zeros((P, TILES) + a.shape[1:], f)
        b[:, 0], b[:, 1], b[:NS, 2] = a[:128], a[128:256], a[256:]
        return b

    inv = (f(500000.0) ** (-np.arange(ROT, dtype=f) / f(ROT))).astype(f)
    ang = pos[:, None] * inv[None]
    out["rope"] = tiles(np.stack([np.cos(ang), np.sin(ang)], 1).astype(f))
    inv = (f(1.0) / (f(10000.0) ** np.linspace(0.0, 1.0, DK // 2, dtype=f))).astype(f)
    ang = pos[:, None] * inv[None]
    cs = np.stack([np.cos(ang), np.sin(ang)], 1).astype(f)
    out["xpos"] = tiles(np.stack([cs, cs * f(DK ** -0.5)], 2))
    lg = np.log(f(1.0) - f(2.0) ** (f(-5.0) - np.arange(H, dtype=f))).astype(f)

    def decay(c):
        i = np.arange(c, dtype=f)
        diff = i[None, :] - i[:, None]
        return np.where(diff[:, None] >= 0, np.exp(np.maximum(diff, 0)[:, None] * lg[None, :, None]), 0).astype(f)

    order = [0, 2, 4, 6, 1, 3, 5, 7]
    out["dmat"] = decay(128)[:, order]
    same = (np.arange(NS)[:, None] // DSEQ == np.arange(NS)[None] // DSEQ)
    small = decay(DSEQ)
    i = np.arange(NS) % DSEQ
    out["dmat_s"] = (small[i][:, :, i] * same[:, None])[:, order].astype(f)
    i = np.concatenate([np.arange(256) % 128, np.arange(NS) % DSEQ]).astype(f)
    out["dq"] = tiles(np.exp((i + 1)[:, None] * lg[None]).astype(f))
    j = np.arange(128, dtype=f)
    out["dk"] = np.exp((127 - j)[:, None] * lg[None]).astype(f)
    j = (np.arange(NS) % DSEQ).astype(f)
    dks = np.exp((DSEQ - 1 - j)[:, None] * lg[None]).astype(f)
    seq = (np.arange(NS)[:, None] // DSEQ == np.arange(NSEQ)[None]).astype(f)
    out["dk_s"] = (dks[:, None, :] * seq[:, :, None]).astype(f)
    head = 2 * np.arange(4)[None] + np.arange(P)[:, None] // 64
    out["dc"] = np.stack([np.exp(f(128) * lg)[head], np.exp(f(DSEQ) * lg)[head]], 1).astype(f)
    q, k = np.arange(128)[:, None], np.arange(256)[None]
    out["causal"] = np.stack([np.where(k <= q, 0, NEG), np.where(k <= q + 128, 0, NEG)], 1).astype(f)
    t = np.arange(NS)[:, None, None] % DSEQ
    n, kk = np.arange(NSEQ)[None, :, None], np.arange(NS)[None, None]
    out["own"] = np.where((kk // DSEQ == n) & (kk % DSEQ <= t), 0, NEG).astype(f)
    out["ident"] = np.eye(P, dtype=f)
    out["before"] = np.triu(np.ones((P, P), f), 1)
    sw = np.zeros((P, P), f)
    for p in range(S5):
        sw[S5 + p, p], sw[p, S5 + p] = -1, 1
    out["swap"] = sw
    tok = np.arange(P, dtype=f)[:, None] + 128 * np.arange(TILES, dtype=f)[None]
    out["token"] = tok.astype(f)
    out["heads"] = np.broadcast_to((np.arange(NS)[:, None] // DSEQ == np.arange(H)[None])[:, :, None],
                                   (NS, H, HD)).astype(f)
    return out


class Own:

    def __init__(self, eng, sem):
        self.eng, self.sem, self.n = eng, sem, 0

    def inc(self, ins):
        ins.then_inc(self.sem, 1)
        self.n += 1

    def sync(self):
        self.eng.wait_ge(self.sem, self.n)

    def do(self, ins):
        self.inc(ins)
        self.sync()


class Core:

    def __init__(self, nc, ins, outs, consts, scratch):
        self.nc, self.i, self.o, self.c, self.d = nc, ins, outs, consts, scratch
        self.h = self.ident = self.xT = None

    def software_dma_semaphores(self, ctx):
        def sem(name):
            return ctx.enter_context(self.nc.semaphore(name))

        self.cleared = sem("yblk_cleared")
        self.gathered = [[sem(f"gathered{li}{b}") for b in range(2)] for li in range(2)]
        self.combined = [sem(f"yg_got{m}") for m in range(2 * TILES)]

    @contextmanager
    def phase(self):
        self.live = []
        with ExitStack() as ctx:
            self.ctx = ctx
            yield ctx
            nums = sorted(s.num for s in self.live)
            runs = [[nums[0], nums[0]]]
            for n in nums[1:]:
                if n == runs[-1][1] + 1:
                    runs[-1][1] = n
                else:
                    runs.append([n, n])
            with self.nc.Block() as block:
                @block.gpsimd
                def _(pool):
                    for lo, hi in runs:
                        pool.sem_clear(range(lo, hi + 1))

    def sem(self, name):
        s = self.ctx.enter_context(self.nc.semaphore(name))
        self.live.append(s)
        return s

    def sb(self, ctx, name, shape, dt=F32):
        return ctx.enter_context(self.nc.sbuf_tensor(name, shape, dt))

    def ps(self, ctx, name, shape):
        return ctx.enter_context(self.nc.psum_tensor(name, shape, F32))


def norm_phase(k, tag, gain, chunks, store):
    nc = k.nc
    with k.phase() as ctx:
        xn = k.sb(ctx, f"xn_{tag}", [P, TILES, D])
        g = k.sb(ctx, f"gain_{tag}", [P, D])
        ss = k.sb(ctx, f"ss_{tag}", [P, 4])
        ms = k.sb(ctx, f"ms_{tag}", [P, 4])
        rstd = k.sb(ctx, f"rstd_{tag}", [P, 4])
        turned_ps = k.ps(ctx, f"turned_ps_{tag}", [P, TILES, D])
        loaded, squares, cleared = k.sem(f"loaded_{tag}"), k.sem(f"squares_{tag}"), k.sem(f"cleared_{tag}")
        own, inv, root = k.sem(f"own_{tag}"), k.sem(f"inv_{tag}"), k.sem(f"root_{tag}")
        normed, turned, stored = k.sem(f"normed_{tag}"), k.sem(f"turned_{tag}"), k.sem(f"stored_{tag}")
        first = tag == "n10"
        s_h = k.sem(f"h_{tag}")
        with nc.Block() as block:
            @block.sync
            def _(sp):
                sp.dma_start(g[:], gain.partition_broadcast(P)).then_inc(loaded, 16)
                for t in range(TILES if store else 0):
                    sp.wait_ge(normed, t + 1)
                    sp.dma_start(store[t], xn[0:ROWS[t], t, :]).then_inc(stored, 16)
                if store:
                    sp.wait_ge(stored, 16 * TILES)

            @block.scalar
            def _(act):
                if first:
                    act.dma_start(k.h[:, 0:2, :], k.i["x_prompt"].rearrange("b (t p) d -> p (b t) d", p=P)
                                  ).then_inc(s_h, 16)
                    act.dma_start(k.h[0:NS, 2, :], k.i["x_sample"].rearrange("b t d -> (b t) d")
                                  ).then_inc(s_h, 16)
                    act.dma_start(k.ident[:], k.c["ident"]).then_inc(s_h, 16)
                    act.wait_ge(s_h, 48)
                act.wait_ge(cleared, 1)
                for t in range(TILES):
                    r = ROWS[t]
                    nc.scalar.activation(xn[0:r, t, :], k.h[0:r, t, :], ACT.Square,
                                         accum_out=ss[0:r, t:t + 1]).then_inc(squares, 1)
                act.wait_ge(inv, 1)
                nc.scalar.activation(rstd[:], ms[:], ACT.Sqrt).then_inc(root, 1)
                if chunks:
                    for t in range(TILES):
                        act.wait_ge(turned, 2 * t + 1)
                        nc.scalar.activation(k.xT[:, 0:4, P * t:P * t + ROWS[t]],
                                             turned_ps[:, t, 0:512].rearrange("p (c n) -> p c n", c=4)[:, :, 0:ROWS[t]],
                                             ACT.Copy)

            @block.vector
            def _(dve):
                nc.vector.memset(ss[:], 1.0).then_inc(cleared, 1)
                o = Own(dve, own)
                dve.wait_ge(squares, TILES)
                if first:
                    dve.wait_ge(s_h, 48)
                o.do(nc.vector.tensor_scalar(ss[:], ss[:], 1.0 / D, EPS, ALU.mult, ALU.add))
                nc.vector.reciprocal(ms[:], ss[:]).then_inc(inv, 1)
                dve.wait_ge(root, 1)
                dve.wait_ge(loaded, 16)
                for t in range(TILES):
                    r = ROWS[t]
                    nc.vector.scalar_tensor_tensor(out=xn[0:r, t, :], in0=k.h[0:r, t, :], scalar=rstd[0:r, t:t + 1],
                                                   in1=g[0:r, :], op0=ALU.mult, op1=ALU.mult).then_inc(normed, 1)
                if chunks:
                    for t in range(TILES):
                        dve.wait_ge(turned, 2 * t + 2)
                        nc.vector.tensor_copy(k.xT[:, 4:8, P * t:P * t + ROWS[t]],
                                              turned_ps[:, t, 512:1024].rearrange("p (c n) -> p c n", c=4)[:, :, 0:ROWS[t]])

            @block.tensor
            def _(pe):
                if not chunks:
                    return
                if first:
                    pe.wait_ge(s_h, 48)
                for t in range(TILES):
                    r = ROWS[t]
                    pe.wait_ge(normed, t + 1)
                    for c in range(KC):
                        src = xn[0:r, t, c:D:KC] if chunks == "pc" else xn[0:r, t, c * P:(c + 1) * P]
                        last = nc.tensor.transpose(turned_ps[:, t, c * P:c * P + r], src, k.ident[0:r, 0:r])
                        if c % 4 == 3:
                            last.then_inc(turned, 1)


def in_proj_phase(k, z):
    nc = k.nc
    NB, RING = 384, 4
    w = k.i["w_in_even"].rearrange("e (p c) n -> p (e c) n", c=KC)
    with k.phase() as ctx:
        wr = k.sb(ctx, "win_ring", [P, RING, KC, NB])
        zp = k.ps(ctx, "z_ps", [P, TILES, 2, 512])
        w_ready = [k.sem(f"win_ready{r}") for r in range(RING)]
        w_used = k.sem("win_used")
        zero = k.sb(ctx, "zero_rows", [P, D])
        zeroed, cleared = k.sem("zero_made"), k.cleared
        done = [k.sem(f"z_done{t}") for t in range(TILES)]
        copied = [k.sem(f"z_copied{t}") for t in range(TILES)]
        with nc.Block() as block:
            @block.sync
            def _(sp):
                with sp.Fori(0, IN_W // NB // RING) as j:
                    for r in range(RING):
                        n = j * RING + r
                        sp.wait_ge(w_used, n + 1)
                        sp.dma_start(wr[:, r], w[:, :, bass.ds(n * NB, NB)]).then_inc(w_ready[r], 16)

            @block.gpsimd
            def _(pool):
                nc.gpsimd.memset(zero[:], 0.0).then_inc(zeroed, 1)
                pool.wait_ge(zeroed, 1)
                lots = k.d["yblk"][(MINB + 2) * SLOT:NBLK * SLOT].rearrange("(n p) d -> n p d", p=P)
                for n in range(lots.shape[0]):
                    pool.dma_start(lots[n], zero[:]).then_inc(cleared, 16)
                pool.wait_ge(cleared, 16 * lots.shape[0])

            @block.tensor
            def _(pe):
                pe.sem_inc(w_used, RING)
                with pe.Fori(0, IN_W // NB // RING) as j:
                    for r in range(RING):
                        n = j * RING + r
                        pe.wait_ge(w_ready[r], 16 * j + 16)
                        for t in range(TILES):
                            pe.wait_ge(copied[t], n + 1)
                            for c in range(KC):
                                last = nc.tensor.matmul(zp[0:ROWS[t], t, r % 2, 0:NB], k.xT[:, c, P * t:P * t + ROWS[t]],
                                                        wr[:, r, c, :], start=c == 0, stop=c == KC - 1)
                            last.then_inc(done[t], 1)
                        pe.wait_ge(done[TILES - 1], n + 1)
                        pe.sem_inc(w_used, 1)

            def copies(eng, copy, tiles):
                for t in tiles:
                    eng.sem_inc(copied[t], 2)
                with eng.Fori(0, IN_W // NB // RING) as j:
                    for r in range(RING):
                        n = j * RING + r
                        for t in tiles:
                            eng.wait_ge(done[t], n + 1)
                            copy(z[0:ROWS[t], t, bass.ds(n * NB, NB)], zp[0:ROWS[t], t, r % 2, 0:NB]
                                 ).then_inc(copied[t], 1)

            @block.scalar
            def _(act):
                copies(act, nc.scalar.copy, (0,))

            @block.vector
            def _(dve):
                copies(dve, nc.vector.tensor_copy, (1, 2))




def even_mixer_phase(k, z, mix):
    nc, c = k.nc, k.c
    with k.phase() as ctx:
        def sb(name, shape, dt=F32):
            return k.sb(ctx, name, shape, dt)

        rope = sb("rope", [P, TILES, 2, ROT])
        xpos = sb("xpos", [P, TILES, 2, 2, DK // 2])
        dmat, dmat_s = sb("dmat", [P, H, P]), sb("dmat_s", [NS, H, NS])
        dq, dk, dk_s = sb("dq", [P, TILES, H]), sb("dk", [P, H]), sb("dk_s", [NS, NSEQ, H])
        dc = sb("dc", [P, 2, 4])
        causal, own_mask = sb("causal", [P, 2, 256]), sb("own", [NS, NSEQ, NS])
        heads = sb("heads", [NS, H * HD])
        tables = [(rope, "rope"), (xpos, "xpos"), (dmat, "dmat"), (dmat_s, "dmat_s"), (dq, "dq"), (dk, "dk"),
                  (dk_s, "dk_s"), (dc, "dc"), (causal, "causal"), (own_mask, "own")]
        pages = sb("pages", [1, 16], I32)
        KB = 2
        kv = sb("kv", [P, KB, 2, 2, 512])
        qt = sb("qt", [P, 16, NTOK])
        ra = sb("ra", [P, 4, 16, ROT])
        big = sb("big", [P, 2112])
        rb = big[:, 0:2048].rearrange("p (f n) -> p f n", f=4)
        soft = sb("soft", [P, 4096])
        sc = soft[:, 0:1024].rearrange("p (h n) -> p h n", h=4)
        pr = soft[:, 1024:2048].rearrange("p (h n) -> p h n", h=4)
        prt = soft[:, 2048:3072].rearrange("p (h n) -> p h n", h=8)
        km = soft[0:NS, :]
        mx, sm, rs = sb("mx", [P, 4]), sb("sm", [P, 4]), sb("rs", [P, 4])
        att = sb("att", [P, H * P])
        kd = sb("kd", [P, 2, H * DK])
        st = sb("st", [P, 4, DV])
        st_out = sb("st_out", [P, 4, DV])
        ss = sb("ss_state", [P, NSEQ, 4, DV])
        tmp = sb("tmp_o", [P, H * DV])
        nrm, nrm2 = sb("nrm", [P, TILES, H]), sb("nrm2", [P, TILES, H])
        qb = sb("qb", [P, NSEQ, 320])
        kT = soft[:, 0:1024].rearrange("p (c n) -> p c n", c=4)
        scs = soft[0:NS, 1024:1664].rearrange("p (a n) -> p a n", a=2)
        prs = soft[0:NS, 1664:2304].rearrange("p (a n) -> p a n", a=2)
        prst = soft[:, 2304:2688].rearrange("p (a b n) -> p a b n", a=2, b=3)
        so = soft[0:NS, 2688:3200].rearrange("p (n e) -> p n e", n=NSEQ)
        sml = sb("sml", [NS, 3, NSEQ])
        msk = tmp[0:NS].rearrange("p (a b) -> p a b", a=2)

        pt = k.ps(ctx, "mix_pt", [P, 2, 512])
        ps = k.ps(ctx, "mix_ps", [P, 2, 512])
        po = k.ps(ctx, "mix_po", [P, 2, 512])
        pd = k.ps(ctx, "mix_pd", [P, 2, 512])

        S = {n: k.sem("mx_" + n) for n in (
            "tables heads pages states own pool roped rotated qt_turned qt_copied kv_out scores scaled "
            "probs p_turned p_copied pv mixed ss_new "
            "att decayed ocross orr kd state st_copied st_final st_stored kvm qm "
            "qb kt_turned kt_copied s_scores s_scaled s_probs ps_turned ps_copied s_pv s_out s_stored s_loaded "
            "s_masked o_ready squares osq root osil gated ss_stored actown").split()}
        kv_ready = [k.sem(f"mx_kv_ready{b}") for b in range(KB)]
        flat_state = "h d e -> (h d) e"

        with nc.Block() as block:
            @block.sync
            def _(sp):
                for t, name in tables:
                    sp.dma_start(t[:], c[name]).then_inc(S["tables"], 16)
                sp.dma_start(heads[:], c["heads"].rearrange("p h d -> p (h d)")).then_inc(S["tables"], 16)
                sp.dma_start(pages[:], k.i["page_table"].rearrange("(a n) p -> a (n p)", a=1)).then_inc(S["pages"], 16)
                sp.dma_start(ss[:], k.i["state_ret"][0].rearrange("n h d e -> n (h d) e")
                             .rearrange("n (c p) e -> p n c e", p=P)).then_inc(S["states"], 16)
                sp.wait_ge(S["pages"], 16)
                for n in range(NSEQ):
                    if n >= KB:
                        sp.wait_ge(S["s_pv"], n - KB + 1)
                    for g in range(2):
                        page = sp.value_load(pages[0:1, 2 * n + g:2 * n + g + 1], min_val=0, max_val=19)
                        for v, cache in enumerate(("cache_k", "cache_v")):
                            sp.dma_start(kv[:, n % KB, g, v, :],
                                         k.i[cache][0].rearrange("n s h d -> n s (h d)")[bass.ds(page, 1)]
                                         .rearrange("a s f -> s (a f)")).then_inc(kv_ready[n % KB], 16)
                sp.wait_ge(S["s_out"], NSEQ)
                for h in range(H):
                    sp.dma_start(k.d["smix"][:, :, h, :].rearrange("n t e -> t n e"), so[h * DSEQ:(h + 1) * DSEQ]
                                 ).then_inc(S["s_stored"], 16)
                sp.wait_ge(S["s_stored"], 16 * H)
                sp.dma_start(mix[0:NS, 2, 0:512], k.d["smix"].rearrange("n t h e -> (n t) (h e)")
                             ).then_inc(S["s_loaded"], 16)
                sp.wait_ge(S["s_loaded"], 16)
                sp.wait_ge(S["ss_new"], NSEQ)
                sp.dma_start(k.o["ret_sample"][0].rearrange("n h d e -> n (h d) e")
                             .rearrange("n (c p) e -> p n c e", p=P), ss[:]).then_inc(S["ss_stored"], 16)
                sp.wait_ge(S["ss_stored"], 16)

            @block.gpsimd
            def _(pool):
                own = Own(pool, S["pool"])
                pool.wait_ge(S["tables"], 16 * 11)
                own.inc(nc.gpsimd.memset(qb[:], 0.0))
                for t in range(TILES):
                    r = ROWS[t]
                    qk = z[0:r, t, QA:VA].rearrange("p (h d) -> p h d", d=HD)
                    x1, x2 = qk[:, :, 0:ROT], qk[:, :, ROT:2 * ROT]
                    co, si = (rope[0:r, t, i].unsqueeze(1).broadcast_to([r, 16, ROT]) for i in range(2))
                    for i, (a, b) in enumerate(((x1, co), (x2, si), (x2, co), (x1, si))):
                        own.inc(nc.gpsimd.tensor_tensor(ra[0:r, i], a, b, ALU.mult))
                    own.sync()
                    own.inc(nc.gpsimd.tensor_tensor(x1, ra[0:r, 0], ra[0:r, 1], ALU.subtract))
                    own.do(nc.gpsimd.tensor_tensor(x2, ra[0:r, 2], ra[0:r, 3], ALU.add))
                    pool.sem_inc(S["roped"], 1)
                pool.wait_ge(S["rotated"], 2)
                for t in range(2):
                    nc.gpsimd.tensor_tensor(kd[:, t].rearrange("p (h d) -> p h d", d=DK),
                                            z[:, t, KR:VR].rearrange("p (h d) -> p h d", d=DK),
                                            dk[:].unsqueeze(2).broadcast_to([P, H, DK]), ALU.mult).then_inc(S["kd"], 1)

            @block.tensor
            def _(pe):
                for m in range(12):
                    t, g = m // 4, m % 4
                    r = ROWS[t]
                    pe.wait_ge(S["roped"], t + 1)
                    pe.wait_ge(S["rotated"], t + 1)
                    if m >= 2:
                        pe.wait_ge(S["qt_copied"], m - 1)
                    for i in range(4):
                        col = (0 if g < 2 else QR - 1024) + (4 * g + i) * P
                        last = nc.tensor.transpose(pt[:, m % 2, i * P:i * P + r], z[0:r, t, col:col + P], k.ident[0:r, 0:r])
                    last.then_inc(S["qt_turned"], 1)
                pe.wait_ge(S["qt_copied"], 12)

                def q_of(base, h, lo, n):
                    b = 64 * (h % 2)
                    return qt[b:b + 64, base + h // 2, lo:lo + n]

                def scores(u):
                    t, hg = u // 2, u % 2
                    if u:
                        pe.wait_ge(S["scaled"], u)
                    for i in range(4):
                        h = 4 * hg + i
                        last = nc.tensor.matmul(ps[:, i % 2, (i // 2) * 256:(i // 2) * 256 + P * (t + 1)],
                                                q_of(0, h, P * t, P), q_of(4, h, 0, P * (t + 1)), start=True, stop=True)
                    last.then_inc(S["scores"], 1)

                scores(0)
                for u in range(4):
                    t, hg = u // 2, u % 2
                    if u < 3:
                        scores(u + 1)
                    pe.wait_ge(S["probs"], u + 1)
                    if u:
                        pe.wait_ge(S["p_copied"], u)
                    for i in range(4):
                        for b in range(t + 1):
                            s = i * (t + 1) + b
                            last = nc.tensor.transpose(pt[:, s // 4, (s % 4) * P:(s % 4 + 1) * P],
                                                       pr[:, 2 * (i % 2) + i // 2, b * P:(b + 1) * P], k.ident[:])
                    last.then_inc(S["p_turned"], 1)
                    pe.wait_ge(S["p_copied"], u + 1)
                    if u:
                        pe.wait_ge(S["mixed"], u)
                    for i in range(4):
                        h = 4 * hg + i
                        for b in range(t + 1):
                            last = nc.tensor.matmul(po[:, 0, i * HD:(i + 1) * HD], prt[:, i * (t + 1) + b, :],
                                                    z[:, b, VA + h * HD:VA + (h + 1) * HD], start=b == 0, stop=b == t)
                    last.then_inc(S["pv"], 1)

                pe.wait_ge(S["kd"], 2)
                for t in range(TILES):
                    r = ROWS[t]
                    if t == 0:
                        pe.wait_ge(S["scaled"], 4)
                        pe.wait_ge(S["mixed"], 4)
                    else:
                        pe.wait_ge(S["decayed"], t)
                    for h in range(H):
                        last = nc.tensor.matmul(ps[0:r, h % 2, (h // 2) * r:(h // 2 + 1) * r],
                                                q_of(12, h, P * t, r), q_of(8, h, P * t, r), start=True, stop=True)
                    last.then_inc(S["att"], 1)
                    if t < 2:
                        if t == 0:
                            pe.wait_ge(S["p_copied"], 4)
                        else:
                            pe.wait_ge(S["st_copied"], 1)
                        for h in range(H):
                            last = nc.tensor.matmul(pt[64 * (h % 2):64 * (h % 2) + 64, 0, (h // 2) * DV:(h // 2 + 1) * DV],
                                                    kd[:, t, h * DK:(h + 1) * DK], z[:, t, VR + h * DV:VR + (h + 1) * DV],
                                                    start=True, stop=True)
                        last.then_inc(S["state"], 1)
                    if t:
                        pe.wait_ge(S["orr"], t)
                    if t == 1:
                        for h in range(H):
                            b = 64 * (h % 2)
                            last = nc.tensor.matmul(pd[:, h % 2, (h // 2) * DV:(h // 2 + 1) * DV], q_of(8, h, P, P),
                                                    st[b:b + 64, h // 2, :], start=True, stop=True)
                    if t == 2:
                        pe.wait_ge(S["qm"], 1)
                        pe.wait_ge(S["states"], 16)
                        for h in range(H):
                            b = 64 * (h % 2)
                            for n in range(NSEQ):
                                lo = n * 256 + (h // 2) * 64
                                last = nc.tensor.matmul(pd[0:NS, h % 2, (h // 2) * DV:(h // 2 + 1) * DV],
                                                        big[b:b + 64, lo:lo + 64], ss[b:b + 64, n, h // 2, :],
                                                        start=n == 0, stop=n == NSEQ - 1)
                    if t:
                        last.then_inc(S["ocross"], 1)
                    pe.wait_ge(S["decayed"], t + 1)
                    for h in range(H):
                        last = nc.tensor.matmul(po[0:r, h // 4, (h % 4) * DV:(h % 4 + 1) * DV], att[0:r, (4 * (h % 2) + h // 2) * r:(4 * (h % 2) + h // 2 + 1) * r],
                                                z[0:r, t, VR + h * DV:VR + (h + 1) * DV], start=True, stop=True)
                    last.then_inc(S["o_ready"], 1)
                pe.wait_ge(S["st_final"], 1)
                pe.wait_ge(S["kvm"], 1)
                for n in range(NSEQ):
                    if n >= 2:
                        pe.wait_ge(S["ss_new"], n - 1)
                    for h in range(H):
                        last = nc.tensor.matmul(pt[64 * (h % 2):64 * (h % 2) + 64, n % 2, (h // 2) * DV:(h // 2 + 1) * DV],
                                                km[:, n * 512 + h * DK:n * 512 + (h + 1) * DK],
                                                z[0:NS, 2, VR + h * DV:VR + (h + 1) * DV], start=True, stop=True)
                    last.then_inc(S["state"], 1)
                pe.wait_ge(S["ss_new"], NSEQ)
                pe.wait_ge(S["qb"], 1)
                pe.wait_ge(S["orr"], 3)
                def keys_and_scores(n):
                    pe.wait_ge(kv_ready[n % KB], 64 * (n // KB + 1))
                    if n:
                        pe.wait_ge(S["kt_copied"], n)
                    for ch in range(4):
                        for g in range(2):
                            last = nc.tensor.transpose(pt[:, ch // 2, ((ch % 2) * 2 + g) * P:((ch % 2) * 2 + g + 1) * P],
                                                       kv[:, n % KB, g, 0, ch * P:(ch + 1) * P], k.ident[:])
                    last.then_inc(S["kt_turned"], 1)
                    pe.wait_ge(S["kt_copied"], n + 1)
                    if n >= 2:
                        pe.wait_ge(S["s_scaled"], n - 1)
                    for lo, n_k in ((0, 256), (256, 64)):
                        for ch in range(4):
                            rhs = kT[:, ch, :] if lo == 0 else qt[:, 4 + ch, 256:320]
                            last = nc.tensor.matmul(ps[0:NS, n % 2, lo:lo + n_k], qb[:, n, ch * 64:(ch + 1) * 64], rhs,
                                                    start=ch == 0, stop=ch == 3)
                    last.then_inc(S["s_scores"], 1)

                def probs_and_values(n):
                    pe.wait_ge(S["s_probs"], n + 1)
                    if n >= 2:
                        pe.wait_ge(S["ps_copied"], n - 1)
                    for b in range(3):
                        w = (P, P, NS)[b]
                        last = nc.tensor.transpose(pd[0:w, n % 2, b * NS:(b + 1) * NS], prs[:, n % 2, b * P:b * P + w],
                                                   k.ident[0:NS, 0:NS])
                    last.then_inc(S["ps_turned"], 1)
                    pe.wait_ge(S["ps_copied"], n + 1)
                    if n >= 2:
                        pe.wait_ge(S["s_masked"], n - 1)
                    for b in range(3):
                        w = (P, P, NS)[b]
                        rhs = kv[:, n % KB, b, 1, :] if b < 2 else z[0:NS, 2, VA:VA + 512]
                        last = nc.tensor.matmul(po[0:NS, n % 2, :], prst[0:w, n % 2, b, :], rhs, start=b == 0, stop=b == 2)
                    last.then_inc(S["s_pv"], 1)

                keys_and_scores(0)
                for n in range(NSEQ):
                    if n + 1 < NSEQ:
                        keys_and_scores(n + 1)
                    probs_and_values(n)

            @block.scalar
            def _(act):
                own = Own(act, S["actown"])
                act.wait_ge(S["roped"], 3)
                for name, col in (("k", KA), ("v", VA)):
                    act.dma_start(k.o[name + "_prompt"].rearrange("e b g p h d -> p (e b g) (h d)"), z[:, 0:2, col:col + 512]
                                  ).then_inc(S["kv_out"], 16)
                    act.dma_start(k.o[name + "_sample"].rearrange("e n t h d -> (e n t) (h d)"), z[0:NS, 2, col:col + 512]
                                  ).then_inc(S["kv_out"], 16)
                for m in range(12):
                    t, g = m // 4, m % 4
                    act.wait_ge(S["qt_turned"], m + 1)
                    nc.scalar.copy(qt[:, 4 * g:4 * g + 4, P * t:P * t + ROWS[t]],
                                   pt[:, m % 2].rearrange("p (c n) -> p c n", c=4)[:, :, 0:ROWS[t]]).then_inc(S["qt_copied"], 1)
                for u in range(4):
                    t = u // 2
                    act.wait_ge(S["scaled"], u + 1)
                    if u:
                        act.wait_ge(S["p_turned"], u)
                    nc.scalar.activation(pr[:, :, 0:P * (t + 1)], sc[:, :, 0:P * (t + 1)], ACT.Exp).then_inc(S["probs"], 1)
                    act.wait_ge(S["p_turned"], u + 1)
                    if u:
                        act.wait_ge(S["pv"], u)
                    nc.scalar.copy(prt[:, 0:4 * (t + 1), :], pt[:].rearrange("p a (b n) -> p (a b) n", n=P)[:, 0:4 * (t + 1), :]
                                   ).then_inc(S["p_copied"], 1)
                act.wait_ge(S["st_final"], 1)
                act.dma_start(k.o["ret_prompt"][0, 0].rearrange("h d e -> (h d) e").rearrange("(c p) e -> p c e", p=P),
                              st_out[:]).then_inc(S["st_stored"], 16)

                def keys_copy(n):
                    act.wait_ge(S["kt_turned"], n + 1)
                    nc.scalar.copy(soft[:, 0:1024], pt[:].rearrange("p a b -> p (a b)")).then_inc(S["kt_copied"], 1)

                def exponentials(n):
                    act.wait_ge(S["s_scaled"], n + 1)
                    if n >= 2:
                        act.wait_ge(S["ps_turned"], n - 1)
                    nc.scalar.activation(prs[:, n % 2, :], scs[:, n % 2, :], ACT.Exp, bias=sml[:, 0, n:n + 1],
                                         accum_out=sml[:, 1, n:n + 1]).then_inc(S["s_probs"], 1)

                def probs_copy(n):
                    act.wait_ge(S["ps_turned"], n + 1)
                    if n >= 2:
                        act.wait_ge(S["s_pv"], n - 1)
                    own.inc(nc.scalar.copy(prst[:, n % 2, 0:2, :], pd[:, n % 2, 0:2 * NS].rearrange("p (a b) -> p a b", b=NS)))
                    own.do(nc.scalar.copy(prst[0:NS, n % 2, 2, :], pd[0:NS, n % 2, 2 * NS:3 * NS]))
                    act.sem_inc(S["ps_copied"], 1)

                keys_copy(0)
                exponentials(0)
                for n in range(NSEQ):
                    if n + 1 < NSEQ:
                        keys_copy(n + 1)
                        exponentials(n + 1)
                    probs_copy(n)
                act.wait_ge(S["osq"], 1)
                nc.scalar.activation(nrm2[:], nrm[:], ACT.Sqrt).then_inc(S["root"], 1)
                for t in range(TILES):
                    nc.scalar.activation(z[0:ROWS[t], t, GR:], z[0:ROWS[t], t, GR:], ACT.Silu).then_inc(S["osil"], 1)
                act.wait_ge(S["kv_out"], 64)
                act.wait_ge(S["st_stored"], 16)

            @block.vector
            def _(dve):
                own = Own(dve, S["own"])
                V = nc.vector
                dve.wait_ge(S["tables"], 16 * 11)
                for t in range(TILES):
                    r = ROWS[t]
                    for part in range(2):
                        qk = z[0:r, t, QR + 512 * part:QR + 512 * (part + 1)].rearrange("p (h n e) -> p h n e", h=H, e=2)
                        xe, xo = qk[:, :, :, 0], qk[:, :, :, 1]
                        f = [rb[0:r, i, 0:256].rearrange("p (h n) -> p h n", h=H) for i in range(4)]
                        co, si = (xpos[0:r, t, i, part].unsqueeze(1).broadcast_to([r, H, 32]) for i in range(2))
                        for i, (a, b) in enumerate(((xe, co), (xo, si), (xo, co), (xe, si))):
                            own.inc(V.tensor_tensor(f[i], a, b, ALU.mult))
                        own.sync()
                        own.inc(V.tensor_tensor(xe, f[0], f[1], ALU.subtract))
                        own.do(V.tensor_tensor(xo, f[2], f[3], ALU.add))
                    dve.sem_inc(S["rotated"], 1)
                own.do(V.memset(big[:], 0.0))

                for u in range(4):
                    t, hg = u // 2, u % 2
                    n_k = P * (t + 1)
                    s4 = ps[:].rearrange("p a (b n) -> p (a b) n", n=256)[:, :, 0:n_k]
                    dve.wait_ge(S["scores"], u + 1)
                    if u:
                        dve.wait_ge(S["probs"], u)
                    own.do(V.scalar_tensor_tensor(out=sc[:, :, 0:n_k], in0=s4, scalar=HD ** -0.5,
                                                  in1=causal[:, t, 0:n_k].unsqueeze(1).broadcast_to([P, 4, n_k]),
                                                  op0=ALU.mult, op1=ALU.add))
                    own.do(V.tensor_reduce(mx[:], sc[:, :, 0:n_k], X, ALU.max))
                    V.tensor_tensor(sc[:, :, 0:n_k], sc[:, :, 0:n_k], mx[:].unsqueeze(2).broadcast_to([P, 4, n_k]),
                                    ALU.subtract).then_inc(S["scaled"], 1)
                    dve.wait_ge(S["probs"], u + 1)
                    own.do(V.tensor_reduce(sm[:], pr[:, :, 0:n_k], X, ALU.add))
                    own.do(V.reciprocal(rs[:], sm[:]))
                    dve.wait_ge(S["pv"], u + 1)
                    V.tensor_tensor(mix[:, t, hg * 256:(hg + 1) * 256].rearrange("p (j b d) -> p j b d", b=2, d=HD),
                                    po[:, 0, 0:256].rearrange("p (j b d) -> p j b d", b=2, d=HD),
                                    rs[:].rearrange("p (b j) -> p j b", b=2).unsqueeze(3).broadcast_to([P, 2, 2, HD]), ALU.mult
                                    ).then_inc(S["mixed"], 1)
                    if u == 0:
                        dve.wait_ge(S["qt_copied"], 12)
                        dve.wait_ge(S["roped"], 3)
                        own.inc(V.tensor_copy(big[:].rearrange("p (n x) -> p n x", x=264)[:, :, 0:256]
                                              .rearrange("p n (c y) -> p n c y", y=64)[:, :, :, 0:DSEQ],
                                              qt[:, 8:12, 256:320].rearrange("p c (n t) -> p n c t", t=DSEQ)))
                        for b in range(2):
                            own.inc(V.tensor_copy(qb[64 * b:64 * b + 64].rearrange("p n (c x) -> p n c x", x=80)
                                                  [:, :, :, b * DSEQ:(b + 1) * DSEQ],
                                                  qt[64 * b:64 * b + 64, 0:4, 256:320].rearrange("p c (n t) -> p n c t", t=DSEQ)))
                        own.sync()
                        dve.sem_inc(S["qm"], 1)
                        dve.sem_inc(S["qb"], 1)

                for n in range(NSEQ):
                    own.inc(V.tensor_tensor(km[:, n * 512:(n + 1) * 512].rearrange("p (h d) -> p h d", h=H),
                                            z[0:NS, 2, KR:VR].rearrange("p (h d) -> p h d", h=H),
                                            dk_s[:, n].unsqueeze(2).broadcast_to([NS, H, DK]), ALU.mult))
                own.sync()
                dve.sem_inc(S["kvm"], 1)
                for t in range(TILES):
                    r = ROWS[t]
                    dve.wait_ge(S["att"], t + 1)
                    if t:
                        dve.wait_ge(S["o_ready"], t)
                    table = (dmat if t < 2 else dmat_s)[:].rearrange("p (a h) n -> p a (h n)", a=2)
                    V.tensor_tensor(att[0:r, 0:H * r].rearrange("p (a n) -> p a n", a=2), ps[0:r, :, 0:4 * r], table, ALU.mult
                                    ).then_inc(S["decayed"], 1)
                    if t < 2:
                        dve.wait_ge(S["state"], t + 1)
                        s_ps = pt[:, 0].rearrange("p (c e) -> p c e", e=DV)
                        if t == 0:
                            own.do(V.tensor_copy(st[:], s_ps))
                            dve.sem_inc(S["st_copied"], 1)
                        else:
                            own.do(V.tensor_tensor(st_out[:], st[:], dc[:, 0].unsqueeze(2).broadcast_to([P, 4, DV]), ALU.mult))
                            own.do(V.tensor_tensor(st_out[:], s_ps, st_out[:], ALU.add))
                            dve.sem_inc(S["st_final"], 1)
                    o_dst = mix[0:r, t, 512:MIX_W]
                    o_ps = po[0:r].rearrange("p a b -> p (a b)")
                    if t == 0:
                        dve.wait_ge(S["o_ready"], 1)
                        V.tensor_copy(o_dst, o_ps).then_inc(S["orr"], 1)
                    else:
                        dve.wait_ge(S["ocross"], t)
                        own.do(V.tensor_tensor(tmp[0:r].rearrange("p (j b e) -> p b j e", b=2, e=DV),
                                               pd[0:r].rearrange("p b (j e) -> p b j e", e=DV),
                                               dq[0:r, t].rearrange("p (j b) -> p b j", b=2).unsqueeze(3)
                                               .broadcast_to([r, 2, 4, DV]), ALU.mult))
                        dve.wait_ge(S["o_ready"], t + 1)
                        V.tensor_tensor(o_dst, o_ps, tmp[0:r], ALU.add).then_inc(S["orr"], 1)
                dve.wait_ge(S["orr"], 3)
                dve.wait_ge(S["states"], 16)
                own.do(V.tensor_tensor(ss[:].rearrange("p n c e -> p n (c e)").rearrange("p n (c e) -> p n c e", e=DV),
                                       ss[:], dc[:, 1].unsqueeze(1).unsqueeze(3).broadcast_to([P, NSEQ, 4, DV]), ALU.mult))
                for n in range(NSEQ):
                    dve.wait_ge(S["state"], n + 3)
                    V.tensor_tensor(ss[:, n].rearrange("p c e -> p (c e)"), pt[:, n % 2, :], ss[:, n].rearrange("p c e -> p (c e)"),
                                    ALU.add).then_inc(S["ss_new"], 1)

                def softmax_in(n):
                    dve.wait_ge(S["s_scores"], n + 1)
                    if n >= 2:
                        dve.wait_ge(S["s_probs"], n - 1)
                    own.inc(V.tensor_scalar(scs[:, n % 2, 0:256], ps[0:NS, n % 2, 0:256], HD ** -0.5, None, ALU.mult))
                    own.do(V.scalar_tensor_tensor(out=scs[:, n % 2, 256:320], in0=ps[0:NS, n % 2, 256:320], scalar=HD ** -0.5,
                                                  in1=own_mask[:, n, :], op0=ALU.mult, op1=ALU.add))
                    own.do(V.tensor_reduce(sml[:, 2, n:n + 1], scs[:, n % 2, :], X, ALU.max))
                    V.tensor_scalar(sml[:, 0, n:n + 1], sml[:, 2, n:n + 1], -1.0, None, ALU.mult).then_inc(S["s_scaled"], 1)

                def place(n):
                    dve.wait_ge(S["s_pv"], n + 1)
                    own.do(V.reciprocal(sml[:, 2, n:n + 1], sml[:, 1, n:n + 1]))
                    V.scalar_tensor_tensor(out=msk[:, n % 2, :], in0=po[0:NS, n % 2, :], scalar=sml[:, 2, n:n + 1],
                                           in1=heads[:], op0=ALU.mult, op1=ALU.mult).then_inc(S["s_masked"], 1)
                    dve.wait_ge(S["s_masked"], n + 1)
                    V.tensor_reduce(so[:, n, :], msk[:, n % 2, :].rearrange("p (h e) -> p e h", h=H), X, ALU.add
                                    ).then_inc(S["s_out"], 1)

                softmax_in(0)
                for n in range(NSEQ):
                    if n + 1 < NSEQ:
                        softmax_in(n + 1)
                    place(n)
                own.do(V.memset(nrm2[:], 1.0))
                for t in range(TILES):
                    r = ROWS[t]
                    o = mix[0:r, t, 512:MIX_W]
                    own.do(V.tensor_tensor(tmp[0:r], o, o, ALU.mult))
                    own.do(V.tensor_reduce(nrm2[0:r, t], tmp[0:r].rearrange("p (h e) -> p h e", e=DV), X, ALU.add))
                own.do(V.tensor_scalar(nrm2[:], nrm2[:], 1.0 / DV, EPS, ALU.mult, ALU.add))
                V.reciprocal(nrm[:], nrm2[:]).then_inc(S["osq"], 1)
                dve.wait_ge(S["osq"], 1)
                dve.wait_ge(S["root"], 1)
                for t in range(TILES):
                    r = ROWS[t]
                    dve.wait_ge(S["osil"], t + 1)
                    o = mix[0:r, t, 512:MIX_W].rearrange("p (h e) -> p h e", e=DV)
                    own.do(V.tensor_tensor(o, o, nrm2[0:r, t].unsqueeze(2).broadcast_to([r, H, DV]), ALU.mult))
                    own.inc(V.tensor_tensor(mix[0:r, t, 512:MIX_W], mix[0:r, t, 512:MIX_W], z[0:r, t, GR:], ALU.mult))


def out_proj_phase(k, mix):
    nc = k.nc
    w = k.i["w_out_even"].rearrange("e (p c) n -> p (e c) n", c=KM)
    LOTS = 4
    with k.phase() as ctx:
        wo = k.sb(ctx, "wo", [P, KM, D])
        mixT = k.sb(ctx, "mixT", [P, KM, NTOK])
        pt = k.ps(ctx, "op_pt", [P, 2, 512])
        acc = k.ps(ctx, "op_acc", [P, TILES, 2, 512])
        w_ready = [k.sem(f"wo_ready{n}") for n in range(LOTS)]
        turned, copied, done = k.sem("mix_turned"), k.sem("mix_copied"), k.sem("op_done")
        with nc.Block() as block:
            @block.sync
            def _(sp):
                for n in range(LOTS):
                    s = slice(n * KM // LOTS, (n + 1) * KM // LOTS)
                    sp.dma_start(wo[:, s], w[:, s]).then_inc(w_ready[n], 16)

            @block.tensor
            def _(pe):
                for m in range(9):
                    t, g = m // 3, m % 3
                    r = ROWS[t]
                    if m >= 2:
                        pe.wait_ge(copied, m - 1)
                    for i in range(4):
                        last = nc.tensor.transpose(pt[:, m % 2, i * P:i * P + r], mix[0:r, t, 4 * g + i:MIX_W:KM],
                                                   k.ident[0:r, 0:r])
                    last.then_inc(turned, 1)
                pe.wait_ge(copied, 9)
                for n in range(LOTS):
                    pe.wait_ge(w_ready[n], 16)
                for t in range(TILES):
                    for half in range(2):
                        for c in range(KM):
                            last = nc.tensor.matmul(acc[0:ROWS[t], t, half, :], mixT[:, c, P * t:P * t + ROWS[t]],
                                                    wo[:, c, half * 512:(half + 1) * 512], start=c == 0, stop=c == KM - 1)
                    last.then_inc(done, 1)

            @block.scalar
            def _(act):
                for m in range(9):
                    t, g = m // 3, m % 3
                    act.wait_ge(turned, m + 1)
                    nc.scalar.copy(mixT[:, 4 * g:4 * g + 4, P * t:P * t + ROWS[t]],
                                   pt[:, m % 2].rearrange("p (c n) -> p c n", c=4)[:, :, 0:ROWS[t]]).then_inc(copied, 1)

            @block.vector
            def _(dve):
                for t in range(TILES):
                    r = ROWS[t]
                    dve.wait_ge(done, t + 1)
                    nc.vector.tensor_tensor(k.h[0:r, t, :], acc[0:r, t].rearrange("p a b -> p (a b)"), k.h[0:r, t, :], ALU.add)


def moe_layer(k, li, rows):
    with ExitStack() as mc:
        route = {
            "slot_tok": k.sb(mc, f"slot_tok{li}", [SLOT, NBLK], U32),
            "dest": k.sb(mc, f"dest{li}", [P, TILES, 2], U32),
            "weight": k.sb(mc, f"weight{li}", [P, TILES, 2]),
            "experts": k.sb(mc, f"experts{li}", [1, NBLK], I32),
            "total": k.sb(mc, f"total{li}", [1, 1], I32),
        }
        with ExitStack() as xc:
            k.xT = k.sb(xc, f"xT_moe{li}", [P, KC, NTOK])
            norm_phase(k, f"n2{li}", k.i["norm2"][li], "pc", rows)
            routing_phase(k, li, route)
        experts_phase(k, li, route)
        combine_phase(k, li, route)


def routing_phase(k, li, route):
    nc = k.nc
    V = nc.vector
    NL = GROUPS + NE
    with k.phase() as ctx:
        def sb(name, shape, dt=F32):
            return k.sb(ctx, f"{name}_r{li}", shape, dt)

        w = sb("wr", [P, KC, NL])
        bias = sb("bias", [P, NL])
        before, token = sb("before", [P, P]), sb("token", [P, TILES])
        ones = sb("ones", [P, P])
        count_up = sb("count_up", [P, 64])
        lg = sb("lg", [P, TILES, NL])
        g8 = sb("g8", [P, TILES, 8])
        gmax, gidx = sb("gmax", [P, TILES, 8]), sb("gidx", [P, TILES, 8], U32)
        gf = sb("gf", [P, TILES])
        ge, gs, wg = sb("ge", [P, TILES, GROUPS]), sb("gs", [P, TILES]), sb("wg", [P, TILES])
        goh = sb("goh", [P, TILES, GROUPS])
        leg = sb("leg", [P, TILES, PER, GROUPS])
        le8, emax, eidx = sb("le8", [P, TILES, PER]), sb("emax", [P, TILES, 8]), sb("eidx", [P, TILES, 8], U32)
        ef = sb("ef", [P, TILES, 2])
        dd, ee, w0 = sb("dd", [P, TILES]), sb("ee", [P, TILES]), sb("w0", [P, TILES])
        oh = sb("oh", [P, TILES, 2, NE])
        both = sb("both", [P, TILES, NE])
        cnt, cmp = sb("cnt", [P, NE]), sb("cmp", [P, NE, NTOK // SLOT])
        limits = sb("limits", [P, NTOK // SLOT])
        nblk, incl, first = sb("nblk", [P, NE]), sb("incl", [P, NE]), sb("first", [P, NE])
        rank, blk, sel = sb("rank", [P, TILES, 2]), sb("blk", [P, TILES, 2]), sb("sel", [P, TILES, 2, NE])
        ahead = sb("ahead", [P, TILES, NE])
        q5, q = sb("q5", [P, TILES, 2, 4]), sb("q", [P, TILES, 2])
        slot, destf = sb("slot", [P, TILES, 2]), sb("destf", [P, TILES, 2])
        ohs, ohb = sb("ohs", [P, TILES, 2, SLOT]), sb("ohb", [P, TILES, 2, NBLK])
        bcmp, bexp = sb("bcmp", [1, NBLK, NE]), sb("bexp", [1, NBLK])
        lps = k.ps(ctx, f"lps{li}", [P, TILES, 512])
        cps = k.ps(ctx, f"cps{li}", [P, TILES, 512])
        tps = k.ps(ctx, f"tps{li}", [P, 512])
        aps = k.ps(ctx, f"aps{li}", [P, 512])
        loaded, own_s, made = k.sem("r_loaded"), k.sem("r_own"), k.sem("r_made")
        logits, shifted, exps, delta = k.sem("r_logits"), k.sem("r_shifted"), k.sem("r_exps"), k.sem("r_delta")
        chosen, counted, placed, listed = k.sem("r_chosen"), k.sem("r_counted"), k.sem("r_placed"), k.sem("r_listed")
        with nc.Block() as block:
            @block.sync
            def _(sp):
                sp.dma_start(w[:, :, 0:GROUPS], k.i["moe_w_group"][li].rearrange("(p c) n -> p c n", c=KC)).then_inc(loaded, 16)
                sp.dma_start(w[:, :, GROUPS:NL], k.i["moe_w_expert"][li].rearrange("(p c) n -> p c n", c=KC)).then_inc(loaded, 16)
                sp.dma_start(bias[:, 0:GROUPS], k.i["moe_b_group"][li].partition_broadcast(P)).then_inc(loaded, 16)
                sp.dma_start(bias[:, GROUPS:NL], k.i["moe_b_expert"][li].partition_broadcast(P)).then_inc(loaded, 16)
                sp.dma_start(before[:], k.c["before"]).then_inc(loaded, 16)
                sp.dma_start(token[:], k.c["token"]).then_inc(loaded, 16)

            @block.gpsimd
            def _(pool):
                nc.gpsimd.iota(count_up[:], pattern=[[1, 64]], base=0, channel_multiplier=0,
                               allow_small_or_imprecise_dtypes=True).then_inc(made, 1)
                nc.gpsimd.iota(limits[:], pattern=[[SLOT, NTOK // SLOT]], base=0, channel_multiplier=0,
                               allow_small_or_imprecise_dtypes=True).then_inc(made, 1)
                nc.gpsimd.memset(ones[:], 1.0).then_inc(made, 1)

            @block.tensor
            def _(pe):
                pe.wait_ge(loaded, 96)
                for t in range(TILES):
                    for c in range(KC):
                        last = nc.tensor.matmul(lps[0:ROWS[t], t, 0:NL], k.xT[:, c, P * t:P * t + ROWS[t]], w[:, c, :],
                                                start=c == 0, stop=c == KC - 1)
                last.then_inc(logits, 1)
                pe.wait_ge(chosen, 1)
                pe.wait_ge(made, 3)
                for t in range(TILES):
                    for s in range(t + 1):
                        r = ROWS[s]
                        lhs = before[0:r, 0:ROWS[t]] if s == t else ones[0:r, 0:ROWS[t]]
                        last = nc.tensor.matmul(cps[0:ROWS[t], t, 0:NE], lhs, both[0:r, s, :], start=s == 0, stop=s == t)
                for s in range(TILES):
                    last = nc.tensor.matmul(aps[:, 0:NE], ones[0:ROWS[s], :], both[0:ROWS[s], s, :], start=s == 0, stop=s == TILES - 1)
                last.then_inc(counted, 1)
                pe.wait_ge(placed, 1)
                for m in range(2 * TILES):
                    t, j = m // 2, m % 2
                    last = nc.tensor.matmul(tps[0:SLOT, 0:NBLK], ohs[0:ROWS[t], t, j, :], ohb[0:ROWS[t], t, j, :],
                                            start=m == 0, stop=m == 2 * TILES - 1)
                last.then_inc(listed, 1)

            @block.scalar
            def _(act):
                act.wait_ge(shifted, 1)
                nc.scalar.activation(ge[:], goh[:], ACT.Exp).then_inc(exps, 1)
                act.wait_ge(delta, 1)
                nc.scalar.activation(ee[:], dd[:], ACT.Exp).then_inc(exps, 1)

            @block.vector
            def _(dve):
                own = Own(dve, own_s)
                own.inc(V.memset(g8[:], NEG))
                own.inc(V.memset(lg[:], 0.0))
                own.do(V.memset(both[:], 0.0))
                dve.wait_ge(loaded, 96)
                dve.wait_ge(made, 3)
                dve.wait_ge(logits, 1)
                for t in range(TILES):
                    own.inc(V.tensor_tensor(lg[0:ROWS[t], t], lps[0:ROWS[t], t, 0:NL], bias[0:ROWS[t]], ALU.add))
                own.sync()
                own.do(V.tensor_copy(g8[:, :, 0:GROUPS], lg[:, :, 0:GROUPS]))
                for t in range(TILES):
                    own.do(V.max(gmax[:, t], g8[:, t]))
                    own.do(V.max_index(gidx[:, t], gmax[:, t], g8[:, t]))
                own.inc(V.tensor_copy(gf[:], gidx[:, :, 0]))
                V.tensor_tensor(goh[:], lg[:, :, 0:GROUPS], gmax[:, :, 0:1].broadcast_to([P, TILES, GROUPS]),
                                ALU.subtract).then_inc(shifted, 1)
                dve.wait_ge(exps, 1)
                own.do(V.tensor_reduce(gs[:], ge[:], X, ALU.add))
                own.do(V.reciprocal(wg[:], gs[:]))
                own.do(V.tensor_tensor(goh[:], count_up[:, 0:GROUPS].unsqueeze(1).broadcast_to([P, TILES, GROUPS]),
                                       gf[:].unsqueeze(2).broadcast_to([P, TILES, GROUPS]), ALU.is_equal))
                for t in range(TILES):
                    own.inc(V.tensor_tensor(leg[:, t], lg[:, t, GROUPS:NL].rearrange("p (g e) -> p e g", g=GROUPS),
                                            goh[:, t].unsqueeze(1).broadcast_to([P, PER, GROUPS]), ALU.mult))
                own.sync()
                own.do(V.tensor_reduce(le8[:], leg[:], X, ALU.add))
                for t in range(TILES):
                    own.do(V.max(emax[:, t], le8[:, t]))
                    own.do(V.max_index(eidx[:, t], emax[:, t], le8[:, t]))
                own.inc(V.tensor_copy(ef[:], eidx[:, :, 0:2]))
                V.tensor_tensor(dd[:], emax[:, :, 1], emax[:, :, 0], ALU.subtract).then_inc(delta, 1)
                own.sync()
                for j in range(2):
                    own.do(V.scalar_tensor_tensor(out=ef[:, :, j], in0=gf[:], scalar=float(PER), in1=ef[:, :, j],
                                                  op0=ALU.mult, op1=ALU.add))
                for t in range(TILES):
                    own.inc(V.tensor_tensor(oh[:, t], count_up[:, 0:NE].unsqueeze(1).broadcast_to([P, 2, NE]),
                                            ef[:, t].unsqueeze(2).broadcast_to([P, 2, NE]), ALU.is_equal))
                own.sync()
                V.tensor_tensor(both[:], oh[:, :, 0, :], oh[:, :, 1, :], ALU.add).then_inc(chosen, 1)
                dve.wait_ge(exps, 2)
                own.do(V.tensor_scalar(w0[:], ee[:], 1.0, None, ALU.add))
                own.do(V.reciprocal(w0[:], w0[:]))
                own.do(V.tensor_tensor(w0[:], w0[:], wg[:], ALU.mult))
                own.inc(V.tensor_copy(route["weight"][:, :, 0], w0[:]))
                own.inc(V.tensor_tensor(route["weight"][:, :, 1], w0[:], ee[:], ALU.mult))
                dve.wait_ge(counted, 1)
                own.do(V.tensor_copy(cnt[:], aps[:, 0:NE]))
                own.do(V.tensor_tensor(cmp[:], cnt[:].unsqueeze(2).broadcast_to([P, NE, NTOK // SLOT]),
                                       limits[:].unsqueeze(1).broadcast_to([P, NE, NTOK // SLOT]), ALU.is_gt))
                own.do(V.tensor_reduce(nblk[:], cmp[:], X, ALU.add))
                own.do(V.tensor_tensor_scan(incl[:], ones[:, 0:NE], nblk[:], 0.0, ALU.mult, ALU.add))
                own.do(V.tensor_tensor(first[:], incl[:], nblk[:], ALU.subtract))
                own.inc(V.tensor_copy(route["total"][:], incl[0:1, NE - 1:NE]))
                own.do(V.tensor_tensor(bcmp[:], incl[0:1].unsqueeze(1).broadcast_to([1, NBLK, NE]),
                                       count_up[0:1, 0:NBLK].unsqueeze(2).broadcast_to([1, NBLK, NE]), ALU.is_le))
                own.do(V.tensor_reduce(bexp[:], bcmp[:], X, ALU.add))
                own.do(V.tensor_scalar(bexp[:], bexp[:], float(NE - 1), None, ALU.min))
                own.inc(V.tensor_copy(route["experts"][:], bexp[:]))
                own.inc(V.memset(ahead[:], 0.0))
                own.sync()
                for t in range(TILES):
                    own.inc(V.tensor_copy(ahead[0:ROWS[t], t], cps[0:ROWS[t], t, 0:NE]))
                own.sync()
                for src, dst in ((ahead, rank), (first, blk)):
                    for t in range(TILES):
                        v = (src[:, t] if src is ahead else src[:]).unsqueeze(1).broadcast_to([P, 2, NE])
                        own.inc(V.tensor_tensor(sel[:, t], oh[:, t], v, ALU.mult))
                    own.sync()
                    own.do(V.tensor_reduce(dst[:], sel[:], X, ALU.add))
                for j in range(2):
                    own.inc(V.tensor_tensor(q5[:, :, j], rank[:, :, j].unsqueeze(2).broadcast_to([P, TILES, 4]),
                                            limits[:, 1:5].unsqueeze(1).broadcast_to([P, TILES, 4]), ALU.is_ge))
                own.sync()
                own.do(V.tensor_reduce(q[:], q5[:], X, ALU.add))
                own.do(V.scalar_tensor_tensor(out=slot[:], in0=q[:], scalar=-float(SLOT), in1=rank[:], op0=ALU.mult, op1=ALU.add))
                own.do(V.tensor_tensor(blk[:], blk[:], q[:], ALU.add))
                own.do(V.scalar_tensor_tensor(out=destf[:], in0=blk[:], scalar=float(SLOT), in1=slot[:], op0=ALU.mult, op1=ALU.add))
                own.do(V.tensor_scalar(destf[:], destf[:], 2.0 * SLOT, None, ALU.add))
                own.inc(V.tensor_copy(route["dest"][:], destf[:]))
                for t in range(TILES):
                    own.inc(V.tensor_tensor(ohs[:, t], count_up[:, 0:SLOT].unsqueeze(1).broadcast_to([P, 2, SLOT]),
                                            slot[:, t].unsqueeze(2).broadcast_to([P, 2, SLOT]), ALU.is_equal))
                    own.inc(V.tensor_tensor(ohb[:, t], count_up[:, 0:NBLK].unsqueeze(1).broadcast_to([P, 2, NBLK]),
                                            blk[:, t].unsqueeze(2).broadcast_to([P, 2, NBLK]), ALU.is_equal))
                own.sync()
                for t in range(TILES):
                    own.inc(V.tensor_scalar(ohb[:, t], ohb[:, t], token[:, t:t + 1], None, ALU.mult))
                own.sync()
                dve.sem_inc(placed, 1)
                dve.wait_ge(listed, 1)
                V.tensor_copy(route["slot_tok"][:], tps[0:SLOT, 0:NBLK])


def experts_phase(k, li, route):
    nc = k.nc
    PAIRS = NBLK // 2
    w13 = k.i["moe_w13"][li].rearrange("e (p c) n -> e p (c n)", c=KC)
    w2 = k.i["moe_w2"][li].rearrange("e (p c) n -> e p (c n)", c=4)
    yblk = k.d["yblk"].rearrange("(b s) d -> b s d", s=SLOT)
    HI = slice(SLOT, 2 * SLOT)
    with k.phase() as ctx:
        def sb(name, shape, dt=F32):
            return k.sb(ctx, f"{name}_e{li}", shape, dt)

        wa = [sb(f"w13_{b}", [P, KC, 2 * DE]) for b in range(2)]
        wb = [sb(f"w2_{b}", [P, 4, D]) for b in range(2)]
        xg = [sb(f"xg{b}", [SLOT, D]) for b in range(2)]
        idx = [sb(f"idx{b}", [SLOT, 1], U32) for b in range(2)]
        xgT = [sb(f"xgT{b}", [P, KC, SLOT]) for b in range(2)]
        act_g = sb("act_g", [P, DE])
        hid = sb("hid", [P, DE])
        hidT = sb("hidT", [P, 4, SLOT])
        y = [sb(f"y{b}", [P, D // 2]) for b in range(2)]
        xps = k.ps(ctx, f"xps{li}", [P, KC, SLOT])
        gu = [k.ps(ctx, f"gu{li}{b}", [P, DE]) for b in range(2)]
        hps = k.ps(ctx, f"hps{li}", [P, 2, 4 * SLOT])
        yps = [k.ps(ctx, f"yps{li}{b}", [P, D // 2]) for b in range(2)]
        w13_ready = [k.sem(f"w13_ready{b}") for b in range(2)]
        w2_ready = [k.sem(f"w2_ready{b}") for b in range(2)]
        gathered = k.gathered[li]
        stored = [k.sem(f"y_stored{b}") for b in range(2)]
        w13_used, w2_used, idx_copied = k.sem("w13_used"), k.sem("w2_used"), k.sem("idx_copied")
        passed = k.sem("passed")
        x_turned, x_copied, gate_up = k.sem("x_turned"), k.sem("x_copied"), k.sem("gate_up")
        silu, hidden, h_turned, h_copied = k.sem("silu"), k.sem("hidden"), k.sem("h_turned"), k.sem("h_copied")
        y_copied = k.sem("y_copied")

        def blocks(eng, body):
            total = eng.value_load(route["total"][:], min_val=1, max_val=MAXB)
            with eng.Fori(0, PAIRS) as i:
                for p in range(2):
                    with eng.If(2 * i + p < total):
                        body(i, p, 2 * i + p)

        with nc.Block() as block:
            @block.sync
            def _(sp):
                total = sp.value_load(route["total"][:], min_val=1, max_val=MAXB)
                with sp.Fori(0, PAIRS) as i:
                    for p in range(2):
                        b = 2 * i + p
                        with sp.If(b < total):
                            e = sp.value_load(route["experts"][0:1, bass.ds(b, 1)], min_val=0, max_val=NE - 1)
                            sp.wait_ge(w13_used, b + 1)
                            sp.dma_start(wa[p][:].rearrange("p c n -> p (c n)"), w13[bass.ds(e, 1)].rearrange("e p n -> p (e n)")
                                         ).then_inc(w13_ready[p], 16)
                            sp.wait_ge(w2_used, b + 1)
                            sp.dma_start(wb[p][:].rearrange("p c n -> p (c n)"), w2[bass.ds(e, 1)].rearrange("e p n -> p (e n)")
                                         ).then_inc(w2_ready[p], 16)
                        with sp.If(b < total + 2):
                            sp.wait_ge(y_copied, b + 1)
                            for half in range(2):
                                sp.dma_start(yblk[bass.ds(b, 1), :, half * 512:(half + 1) * 512].rearrange("b s d -> s (b d)"),
                                             y[p][half * SLOT:(half + 1) * SLOT, :]).then_inc(stored[p], 16)
                sp.wait_ge(stored[0], 32 * ((total + 3) // 2) + 32)
                sp.wait_ge(stored[1], 32 * ((total + 2) // 2) + 32)
                sp.sem_inc(passed, 1)

            @block.gpsimd
            def _(pool):
                def gather(i, p, b):
                    pool.wait_ge(x_turned, b + 1)
                    nc.gpsimd.tensor_copy(idx[p][:], route["slot_tok"][:, bass.ds(b, 1)]).then_inc(idx_copied, 1)
                    pool.wait_ge(idx_copied, b + 1)
                    pool.sem_inc(passed, 1)
                    nc.gpsimd.indirect_dma_start(xg[p][:], None, k.d["xn"], bass.IndirectOffsetOnAxis(ap=idx[p][:], axis=0)
                                                 ).then_inc(gathered[p], 16)

                blocks(pool, gather)

            @block.tensor
            def _(pe):
                pe.sem_inc(w13_used, 2)
                pe.sem_inc(w2_used, 2)
                pe.sem_inc(x_turned, 2)

                def expert(i, p, b):
                    pe.wait_ge(gathered[p], 16 * i + 16)
                    pe.wait_ge(x_copied, b + 1)
                    pe.sem_inc(passed, 1)
                    for c in range(KC):
                        last = nc.tensor.transpose(xps[:, c, :], xg[p][:, c:D:KC], k.ident[0:SLOT, 0:SLOT])
                    last.then_inc(x_turned, 1)
                    pe.wait_ge(x_copied, b + 2)
                    pe.wait_ge(w13_ready[p], 16 * i + 16)
                    for c in range(KC):
                        for half in range(2):
                            last = nc.tensor.matmul(gu[p][half * SLOT:(half + 1) * SLOT, :], xgT[p][:, c, :],
                                                    wa[p][:, c, half * DE:(half + 1) * DE], start=c == 0, stop=c == KC - 1)
                    last.then_inc(gate_up, 1)
                    pe.wait_ge(gate_up, b + 1)
                    pe.sem_inc(w13_used, 1)
                    pe.wait_ge(hidden, b + 1)
                    pe.sem_inc(passed, 1)
                    for j in range(4):
                        last = nc.tensor.transpose(hps[:, 0, j * SLOT:(j + 1) * SLOT], hid[HI, j:DE:4], k.ident[HI, HI])
                    last.then_inc(h_turned, 1)
                    pe.wait_ge(h_copied, b + 1)
                    pe.wait_ge(w2_ready[p], 16 * i + 16)
                    for j in range(4):
                        for half in range(2):
                            last = nc.tensor.matmul(yps[p][half * SLOT:(half + 1) * SLOT, :], hidT[:, j, :],
                                                    wb[p][:, j, half * 512:(half + 1) * 512], start=j == 0, stop=j == 3)
                    last.then_inc(w2_used, 1)

                blocks(pe, expert)

            @block.scalar
            def _(act):
                def step(i, p, b):
                    act.wait_ge(gate_up, b + 1)
                    nc.scalar.activation(act_g[HI, :], gu[p][0:SLOT, :], ACT.Silu).then_inc(silu, 1)

                blocks(act, step)

            @block.vector
            def _(dve):
                nc.vector.memset(y[0][:], 0.0).then_inc(y_copied, 1)
                nc.vector.memset(y[1][:], 0.0).then_inc(y_copied, 1)
                dve.sem_inc(x_copied, 1)
                dve.sem_inc(stored[0], 32)
                dve.sem_inc(stored[1], 32)

                def step(i, p, b):
                    dve.wait_ge(x_turned, b + 3)
                    nc.vector.tensor_copy(xgT[p][:], xps[:]).then_inc(x_copied, 1)
                    dve.wait_ge(silu, b + 1)
                    nc.vector.tensor_tensor(hid[HI, :], gu[p][HI, :], act_g[HI, :], ALU.mult).then_inc(hidden, 1)
                    dve.wait_ge(h_turned, b + 1)
                    nc.vector.tensor_copy(hidT[:].rearrange("p j n -> p (j n)"), hps[:, 0, :]).then_inc(h_copied, 1)
                    dve.wait_ge(w2_used, b + 3)
                    dve.wait_ge(stored[p], 32 * i + 64)
                    nc.vector.tensor_copy(y[p][:], yps[p][:]).then_inc(y_copied, 1)

                blocks(dve, step)


def combine_phase(k, li, route):
    nc = k.nc
    with k.phase() as ctx:
        yg = k.sb(ctx, f"yg{li}", [P, TILES, 2, D])
        got = k.combined
        added = k.sem("yg_added")
        with nc.Block() as block:
            @block.gpsimd
            def _(pool):
                for m in range(2 * TILES):
                    t, j = m // 2, m % 2
                    r = ROWS[t]
                    nc.gpsimd.indirect_dma_start(yg[0:r, t, j, :], None, k.d["yblk"],
                                                 bass.IndirectOffsetOnAxis(ap=route["dest"][0:r, t, j:j + 1], axis=0)
                                                 ).then_inc(got[m], 16)

            @block.vector
            def _(dve):
                for m in range(2 * TILES):
                    t, j = m // 2, m % 2
                    r = ROWS[t]
                    dve.wait_ge(got[m], 16 * (li + 1))
                    if j:
                        dve.wait_ge(added, m)
                    nc.vector.scalar_tensor_tensor(out=k.h[0:r, t, :], in0=yg[0:r, t, j, :], scalar=route["weight"][0:r, t, j:j + 1],
                                                   in1=k.h[0:r, t, :], op0=ALU.mult, op1=ALU.add).then_inc(added, 1)


def s5_layer(k, zT):
    with ExitStack() as sc:
        def sb(name, shape, dt=F32):
            return k.sb(sc, name, shape, dt)

        s = {
            "u": sb("s5_u", [P, G5, NCH]),
            "cs": sb("s5_cs", [P, G5, CH + 1, C5]),
            "fs": sb("s5_fs", [P, 7 * 1024 + 8 * 144]),
            "e": sb("s5_e", [P, G5 * P]),
            "xs": sb("s5_xs", [P, G5, NCH + 1]),
            "pb": sb("s5_pb", [P, 2, C5, G5]),
            "pc": sb("s5_pc", [P, 2, C5, G5]),
            "ar": sb("s5_ar", [P, CH + 1, G5]), "ai": sb("s5_ai", [P, CH + 1, G5]),
            "work": sb("s5_work", [P, 4096]),
            "s0": sb("s5_s0", [P, 2, NSEQ, G5]),
            "d": sb("s5_dcol", [P, KC]),
            "sw": sb("s5_sw", [P, P]),
        }
        s5_prepare_phase(k, s)
        s5_matrices_phase(k, s)
        s5_scan_phase(k, s, zT)


def s5_prepare_phase(k, s):
    nc = k.nc
    V = nc.vector
    with k.phase() as ctx:
        def sb(name, shape, dt=F32):
            return k.sb(ctx, name, shape, dt)

        xc = s["e"][0:NCH, :]
        xg = s["fs"][0:NCH, 0:CH * D]
        raw = s["work"][0:G5, :].rearrange("g (a n) -> g a n", a=4)
        lam, ldt = sb("lam", [G5, 2, S5]), sb("ldt", [P, G5])
        spare = s["cs"][:].rearrange("p g j c -> p (g j c)")
        s0raw = spare[0:G5, 3072:3072 + NSEQ * P].rearrange("g (n a p) -> g n a p", n=NSEQ, a=2)
        names = "lr li dt x ang mag kf a1 a2 sn sh cs den rden nr t1 t2 cor coi ek er eq ep".split()
        e_int = sb("s5_eint", [P, G5], I32)
        v = {n: spare[:, G5 * i:G5 * (i + 1)] for i, n in enumerate(names)}
        pp = spare[:, 2048:2560].rearrange("p (a m g) -> p a m g", a=2, m=4)
        pb = k.ps(ctx, "s5p", [P, 8, 512])
        loaded, chunks, s0_loaded = k.sem("p_loaded"), k.sem("p_chunks"), k.sem("p_s0")
        raws = [k.sem(f"p_raw{i}") for i in range(4)]
        sorted_, turned, copied = k.sem("p_sorted"), k.sem("p_turned"), k.sem("p_copied")
        lam_ps, lam_got, b_ps, c_re_ps, c_im_ps = (k.sem("p_" + n) for n in "lam_ps lam_got b_ps c_re_ps c_im_ps".split())
        own_s, e2, a_ok, b_done, c_done, s0_ps, s0_got = (k.sem("p_" + n) for n in
            "own e2 a_ok b_done c_done s0_ps s0_got".split())
        with nc.Block() as block:
            @block.sync
            def _(sp):
                sp.dma_start(xc, k.d["xn"].rearrange("(q s) d -> q (s d)", s=CH)).then_inc(chunks, 16)
                sp.dma_start(lam[:, 0], k.i["s5_lam_re"][0]).then_inc(loaded, 16)
                sp.dma_start(lam[:, 1], k.i["s5_lam_im"][0]).then_inc(loaded, 16)
                sp.dma_start(ldt[:], k.i["s5_log_dt"][0].partition_broadcast(P)).then_inc(loaded, 16)
                sp.dma_start(s["sw"][:], k.c["swap"]).then_inc(loaded, 16)
                sp.dma_start(s["d"][:], k.i["s5_d"][0].rearrange("(c p) -> p c", p=P), allow_slow_non_contiguous=True
                             ).then_inc(loaded, 16)
                for i, n in enumerate(("s5_b_re", "s5_b_im")):
                    sp.dma_start(raw[:, i], k.i[n][0].rearrange("g p c -> g (p c)")).then_inc(raws[i], 16)
                for i, n in enumerate(("s5_c_re", "s5_c_im")):
                    sp.dma_start(raw[:, 2 + i], k.i[n][0].rearrange("g c p -> g (c p)")).then_inc(raws[2 + i], 16)
                for i, n in enumerate(("state_s5_re", "state_s5_im")):
                    sp.dma_start(s0raw[:, :, i, :], k.i[n][0].rearrange("n g p -> g n p")).then_inc(s0_loaded, 16)

            @block.gpsimd
            def _(pool):
                pool.wait_ge(chunks, 16)
                for i in range(0, CH, 2):
                    nc.gpsimd.tensor_copy(xg.rearrange("q (g s c) -> q g s c", s=CH, c=C5)[:, :, i, :],
                                          xc[:, i * D:(i + 1) * D].rearrange("q (g c) -> q g c", c=C5)).then_inc(sorted_, 1)

            @block.scalar
            def _(act):
                act.wait_ge(a_ok, 1)
                nc.scalar.activation(v["sn"], v["a2"], ACT.Sin).then_inc(e2, 1)
                nc.scalar.activation(v["sh"], v["a2"], ACT.Sin, scale=0.5).then_inc(e2, 1)
                act.wait_ge(chunks, 16)
                for i in range(1, CH, 2):
                    nc.scalar.copy(xg.rearrange("q (g s c) -> q g s c", s=CH, c=C5)[:, :, i, :],
                                   xc[:, i * D:(i + 1) * D].rearrange("q (g c) -> q g c", c=C5)).then_inc(b_done, 1)
                for m in range(8):
                    act.wait_ge(turned, m + 1)
                    nc.scalar.copy(s["u"][:, 8 * m:8 * m + 8, :].rearrange("p g q -> p (g q)"), pb[:, m % 2, 0:8 * NCH]
                                   ).then_inc(copied, 1)
                act.wait_ge(s0_ps, 1)
                nc.scalar.copy(s["s0"][:, 0].rearrange("p n g -> p (n g)"), pb[:, 2, :]).then_inc(s0_got, 1)
                act.wait_ge(s0_ps, 2)
                nc.scalar.copy(s["s0"][:, 1].rearrange("p n g -> p (n g)"), pb[:, 3, :]).then_inc(s0_got, 1)

            @block.tensor
            def _(pe):
                def both_halves(src, stop_bank, col):
                    last = None
                    for half in range(2):
                        last = nc.tensor.matmul(pb[64 * half:64 * half + 64, stop_bank, col:col + G5], src, k.ident[0:G5, 0:G5],
                                                start=True, stop=True)
                    return last

                pe.wait_ge(loaded, 80)
                for i in range(2):
                    last = both_halves(lam[:, i, :], 0, i * G5)
                last.then_inc(lam_ps, 1)
                for i in range(2):
                    pe.wait_ge(raws[i], 16)
                    for c in range(C5):
                        last = both_halves(raw[:, i, c:1024:C5], 2 + 2 * i + c // 8, (c % 8) * G5)
                last.then_inc(b_ps, 1)
                pe.wait_ge(raws[2], 16)
                for c in range(C5):
                    last = both_halves(raw[:, 2, c * S5:(c + 1) * S5], 6 + c // 8, (c % 8) * G5)
                last.then_inc(c_re_ps, 1)
                pe.wait_ge(raws[3], 16)
                pe.wait_ge(lam_got, 1)
                for c in range(C5):
                    last = both_halves(raw[:, 3, c * S5:(c + 1) * S5], c // 8, (c % 8) * G5)
                last.then_inc(c_im_ps, 1)
                pe.wait_ge(c_done, 1)
                pe.wait_ge(sorted_, CH // 2)
                pe.wait_ge(b_done, CH // 2)
                for m in range(8):
                    if m >= 2:
                        pe.wait_ge(copied, m - 1)
                    for i in range(8):
                        g = 8 * m + i
                        last = nc.tensor.transpose(pb[:, m % 2, i * NCH:(i + 1) * NCH], xg[:, g * P:(g + 1) * P], k.ident[0:NCH, 0:NCH])
                    last.then_inc(turned, 1)
                pe.wait_ge(s0_loaded, 32)
                pe.wait_ge(c_done, 2)
                for n in range(NSEQ):
                    last = nc.tensor.transpose(pb[:, 2, n * G5:(n + 1) * G5], s0raw[:, n].rearrange("g a p -> g (a p)"),
                                               k.ident[0:G5, 0:G5])
                last.then_inc(s0_ps, 1)
                pe.wait_ge(s0_got, 1)
                nc.tensor.matmul(pb[:, 3, :], s["sw"][:], s["s0"][:, 0].rearrange("p n g -> p (n g)"), start=True, stop=True
                                 ).then_inc(s0_ps, 1)

            @block.vector
            def _(dve):
                own = Own(dve, own_s)
                tt = V.tensor_tensor

                def st(o, a, scalar, b, op0=ALU.mult, op1=ALU.add):
                    own.do(V.scalar_tensor_tensor(out=v[o], in0=v[a], scalar=scalar, in1=v[b] if b else e_int[:].bitcast(F32),
                                                  op0=op0, op1=op1))

                def do(o, a, b, op):
                    own.do(tt(v[o], v[a], v[b], op))

                def exp(o, x):
                    own.do(V.tensor_scalar(v["ek"], x, 1.0 / np.log(2.0), None, ALU.mult))
                    own.do(V.tensor_scalar(v["ek"], v["ek"], big, None, ALU.add))
                    own.do(V.tensor_scalar(v["ek"], v["ek"], -big, None, ALU.add))
                    own.do(V.tensor_scalar(v["ek"], v["ek"], 127.0, -126.0, ALU.min, ALU.max))
                    own.do(V.scalar_tensor_tensor(out=v["er"], in0=v["ek"], scalar=-0.693359375, in1=x, op0=ALU.mult, op1=ALU.add))
                    st("er", "ek", 2.12194440e-4, "er")
                    own.do(V.tensor_scalar(v["eq"], v["er"], 1.0 / 5040, None, ALU.mult))
                    for f in (720, 120, 24, 6, 2, 1):
                        st("eq", "eq", 1.0 / f, "er", ALU.add, ALU.mult)
                    own.do(V.tensor_scalar(v["ep"], v["ek"], 127.0, None, ALU.add))
                    own.do(V.tensor_copy(e_int[:], v["ep"]))
                    own.do(V.tensor_scalar(e_int[:], e_int[:], 23, None, ALU.logical_shift_left))
                    st(o, "eq", 1.0, None, ALU.add, ALU.mult)

                big = 12582912.0
                dve.wait_ge(loaded, 80)
                exp("dt", ldt[:])
                dve.wait_ge(lam_ps, 1)
                own.inc(V.tensor_copy(v["lr"], pb[:, 0, 0:G5]))
                own.do(V.tensor_copy(v["li"], pb[:, 0, G5:2 * G5]))
                dve.sem_inc(lam_got, 1)
                do("x", "lr", "dt", ALU.mult)
                exp("mag", v["x"])
                do("ang", "li", "dt", ALU.mult)
                own.do(V.tensor_scalar(v["kf"], v["ang"], 1.0 / (2 * np.pi), None, ALU.mult))
                own.do(V.tensor_scalar(v["kf"], v["kf"], big, None, ALU.add))
                own.do(V.tensor_scalar(v["kf"], v["kf"], -big, None, ALU.add))
                st("a1", "kf", -6.28125, "ang")
                st("a2", "kf", -(2 * np.pi - 6.28125), "a1")
                V.tensor_scalar(v["a2"], v["a2"], 3.1415925, -3.1415925, ALU.min, ALU.max).then_inc(a_ok, 1)
                dve.wait_ge(e2, 2)
                do("cs", "sh", "sh", ALU.mult)
                own.do(V.tensor_scalar(v["cs"], v["cs"], -2.0, 1.0, ALU.mult, ALU.add))
                ar, ai = s["ar"], s["ai"]
                own.inc(V.memset(ar[:, 0], 1.0))
                own.inc(V.memset(ai[:, 0], 0.0))
                own.inc(tt(ar[:, 1], v["mag"], v["cs"], ALU.mult))
                own.do(tt(ai[:, 1], v["mag"], v["sn"], ALU.mult))
                for m in (1, 2, 4):
                    r, i = ar[:, 1:1 + m], ai[:, 1:1 + m]
                    br, bi = (a[:, m].unsqueeze(1).broadcast_to([P, m, G5]) for a in (ar, ai))
                    f = [pp[:, j, 0:m] for j in range(2)]
                    own.inc(tt(f[0], r, br, ALU.mult))
                    own.do(tt(f[1], i, bi, ALU.mult))
                    own.do(tt(ar[:, 1 + m:1 + 2 * m], f[0], f[1], ALU.subtract))
                    own.inc(tt(f[0], r, bi, ALU.mult))
                    own.do(tt(f[1], i, br, ALU.mult))
                    own.do(tt(ai[:, 1 + m:1 + 2 * m], f[0], f[1], ALU.add))
                do("t1", "lr", "lr", ALU.mult)
                do("t2", "li", "li", ALU.mult)
                do("den", "t1", "t2", ALU.add)
                own.inc(V.reciprocal(v["rden"], v["den"]))
                own.do(V.tensor_scalar(v["nr"], ar[:, 1], -1.0, None, ALU.add))
                do("t1", "nr", "lr", ALU.mult)
                own.do(tt(v["t2"], ai[:, 1], v["li"], ALU.mult))
                do("t1", "t1", "t2", ALU.add)
                do("cor", "t1", "rden", ALU.mult)
                own.do(tt(v["t1"], ai[:, 1], v["lr"], ALU.mult))
                do("t2", "nr", "li", ALU.mult)
                do("t1", "t1", "t2", ALU.subtract)
                do("coi", "t1", "rden", ALU.mult)
                pc, lo, hi = s["pc"], slice(0, 64), slice(64, 128)
                dve.wait_ge(c_re_ps, 1)
                dve.wait_ge(c_im_ps, 1)
                dve.wait_ge(b_ps, 1)

                def flat(x):
                    return x.rearrange("p c g -> p (c g)")

                def bank(i):
                    return pb[:, i:i + 2, :].rearrange("p a b -> p (a b)")

                own.inc(V.tensor_copy(flat(pc[lo, 0]), bank(6)[lo]))
                own.inc(V.tensor_scalar(flat(pc[hi, 0]), bank(0)[hi], -1.0, None, ALU.mult))
                own.inc(V.tensor_scalar(flat(pc[lo, 1]), bank(0)[lo], -1.0, None, ALU.mult))
                own.do(V.tensor_scalar(flat(pc[hi, 1]), bank(6)[hi], -1.0, None, ALU.mult))
                dve.sem_inc(c_done, 1)
                pbk = s["pb"]
                w = s["work"][:].rearrange("p (a c g) -> p a c g", a=4, c=C5)
                cor, coi = (v[n].unsqueeze(1).broadcast_to([P, C5, G5]) for n in ("cor", "coi"))
                b_re, b_im = (bank(i).rearrange("p (c g) -> p c g", c=C5) for i in (2, 4))
                for j, (a, b) in enumerate(((b_re, cor), (b_im, coi), (b_im, cor), (b_re, coi))):
                    own.inc(tt(w[:, j], a, b, ALU.mult))
                own.sync()
                dve.sem_inc(c_done, 1)
                own.inc(tt(pbk[lo, 0], w[lo, 0], w[lo, 1], ALU.subtract))
                own.inc(tt(pbk[hi, 0], w[hi, 2], w[hi, 3], ALU.add))
                own.inc(tt(pbk[hi, 1], w[hi, 0], w[hi, 1], ALU.subtract))
                own.do(tt(pbk[lo, 1], w[lo, 2], w[lo, 3], ALU.add))
                own.do(V.tensor_scalar(pbk[lo, 1], pbk[lo, 1], -1.0, None, ALU.mult))


def s5_matrices_phase(k, s):
    nc = k.nc
    V, G = nc.vector, nc.gpsimd
    with k.phase() as ctx:
        fs = s["fs"][:, 0:G5 * P].rearrange("p (g s c) -> p g s c", s=CH, c=C5)
        prod = s["work"][:].rearrange("p (a c g) -> p a c g", a=4, c=C5)
        cc = s["work"][:, 0:G5 * NCH]
        pt = k.ps(ctx, "s5m_pt", [P, 2, 512])
        pc = k.ps(ctx, "s5m_pc", [P, 6, 512])
        own_s, pool_s, made, cs_made = (k.sem("m_" + n) for n in "own pool made cs_made".split())
        turned, copied, contrib, taken = (k.sem("m_" + n) for n in "turned copied contrib taken".split())

        def power(eng, own, out, base, j, buf):
            t = [prod[:, buf + i] for i in range(2)]
            for i, a in enumerate((s["ar"], s["ai"])):
                own.inc(eng.tensor_tensor(t[i], base[:, i], a[:, j].unsqueeze(1).broadcast_to([P, C5, G5]), ALU.mult))
            own.sync()
            own.do(eng.tensor_tensor(out, t[0], t[1], ALU.add))

        with nc.Block() as block:
            @block.gpsimd
            def _(pool):
                own = Own(pool, pool_s)
                for i in range(4):
                    power(G, own, fs[:, :, i, :].rearrange("p g c -> p c g"), s["pb"], CH - 1 - i, 0)
                pool.sem_inc(made, 1)

            @block.vector
            def _(dve):
                own = Own(dve, own_s)
                for i in range(4, CH):
                    power(V, own, fs[:, :, i, :].rearrange("p g c -> p c g"), s["pb"], CH - 1 - i, 2)
                dve.sem_inc(made, 1)
                for j in range(CH + 1):
                    power(V, own, s["cs"][:, :, j, :].rearrange("p g c -> p c g"), s["pc"], j, 2)
                dve.sem_inc(cs_made, 1)

            @block.tensor
            def _(pe):
                pe.wait_ge(made, 2)
                for m in range(16):
                    if m >= 2:
                        pe.wait_ge(copied, m - 1)
                    for i in range(4):
                        g = 4 * m + i
                        last = nc.tensor.transpose(pt[:, m % 2, i * P:(i + 1) * P], s["fs"][:, g * P:(g + 1) * P], k.ident[:])
                    last.then_inc(turned, 1)
                pe.wait_ge(copied, 16)
                for g in range(G5):
                    last = nc.tensor.matmul(pc[:, g // 12, (g % 12) * NCH:(g % 12 + 1) * NCH], s["e"][:, g * P:(g + 1) * P],
                                            s["u"][:, g, :], start=True, stop=True)
                last.then_inc(contrib, 1)

            @block.scalar
            def _(act):
                for m in range(16):
                    act.wait_ge(turned, m + 1)
                    nc.scalar.copy(s["e"][:, 512 * m:512 * (m + 1)], pt[:, m % 2, :]).then_inc(copied, 1)
                act.wait_ge(contrib, 1)
                act.wait_ge(cs_made, 1)
                for b in range(6):
                    n = min(12, G5 - 12 * b)
                    nc.scalar.copy(cc[:, b * 12 * NCH:(b * 12 + n) * NCH], pc[:, b, 0:n * NCH])


def s5_scan_phase(k, s, zT):
    nc = k.nc
    V = nc.vector
    NC2 = G5 * NCH
    with k.phase() as ctx:
        def sb(name, shape, dt=F32):
            return k.sb(ctx, name, shape, dt)

        cc = s["work"][:, 0:NC2].rearrange("p (g q) -> p g q", q=NCH)
        icc = s["u"][:].rearrange("p g q -> p (g q)")
        icv = icc.rearrange("p (g q) -> p g q", q=NCH)
        pad = s["fs"]
        kk = s["e"][:].rearrange("p (t j n) -> p t j n", t=KC, j=CH)
        yc = s["fs"][0:NCH, 0:CH * D]
        v3 = sb("s5_v3", [P, 2, 3, G5])
        t1, t2, t3 = sb("s5_t1", [P, 2, G5]), sb("s5_t2", [P, 2, G5]), sb("s5_t3", [P, 2, G5])
        ai2 = sb("s5_ai2", [P, 2, G5])
        fin = sb("s5_fin", [P, NSEQ + 1, G5])
        fout = s["work"][0:G5, 2560:2560 + (NSEQ + 1) * P].rearrange("g (n p) -> g n p", p=P)
        f1 = sb("s5_f1", [P, NSEQ, G5])
        yt = sb("s5_yt", [P, 2, NTOK])
        ps_b = k.ps(ctx, "s5s_b", [P, 8, 512])
        swapped, icc_ok, padded, kk_ps, kk_ok = (k.sem("q_" + n) for n in "swapped icc_ok padded kk_ps kk_ok".split())
        zeroed, own_s, state, saved, xs_ok = (k.sem("q_" + n) for n in "zeroed own state saved xs_ok".split())
        cross, cross_ok, y_ps, y_ok, gelu_ok = (k.sem("q_" + n) for n in "cross cross_ok y_ps y_ok gelu_ok".split())
        fin_ok, fin_ps, fout_ok, out_s, act_s = (k.sem("q_" + n) for n in "fin_ok fin_ps fout_ok out act".split())
        with nc.Block() as block:
            @block.gpsimd
            def _(pool):
                G = nc.gpsimd
                G.memset(pad[:], 0.0).then_inc(zeroed, 1)
                pool.wait_ge(zeroed, 1)
                for t in range(KC):
                    G.tensor_copy(pad[:, 1024 * t:1024 * t + 8 * 144].rearrange("p (i x) -> p i x", x=144)[:, :, 0:C5],
                                  s["pb"][:, 0, :, 8 * t:8 * t + 8].rearrange("p c g -> p g c")).then_inc(padded, 1)

            @block.tensor
            def _(pe):
                for b in range(5):
                    nc.tensor.matmul(ps_b[:, b, :], s["sw"][:], s["work"][:, 512 * b:512 * (b + 1)], start=True, stop=True
                                     ).then_inc(swapped, 1)
                pe.wait_ge(padded, KC)
                pe.wait_ge(icc_ok, 5)
                for t in range(KC):
                    if t >= 2:
                        pe.wait_ge(kk_ok, t - 1)
                    for i in range(8):
                        g = 8 * t + i
                        for half in range(2):
                            out = ps_b[:, 2 * (t % 2) + half, :].rearrange("p (j n) -> p j n", j=4)[:, :, C5 * i:C5 * (i + 1)]
                            last = nc.tensor.matmul(out, pad[:, g * P:(g + 1) * P], s["cs"][:, g, 4 * half:4 * half + 4, :],
                                                    start=True, stop=True)
                    last.then_inc(kk_ps, 1)
                pe.wait_ge(xs_ok, 1)
                for m in range(16):
                    if m >= 4:
                        pe.wait_ge(cross_ok, m - 3)
                    for i in range(4):
                        g = 4 * m + i
                        last = nc.tensor.matmul(ps_b[0:NCH, 4 + m % 4, i * P:(i + 1) * P], s["xs"][:, g, 0:NCH],
                                                s["cs"][:, g, 1:CH + 1, :].rearrange("p s c -> p (s c)"), start=True, stop=True)
                    last.then_inc(cross, 1)
                pe.wait_ge(cross_ok, 16)
                pe.wait_ge(kk_ok, KC)
                for t in range(KC):
                    if t >= 2:
                        pe.wait_ge(y_ok, t - 1)
                    y = ps_b[:, t % 2, 0:NTOK].rearrange("p (q s) -> p q s", s=CH)
                    u = k.xT[:, t, :].rearrange("p (q s) -> p q s", s=CH)
                    for j in range(CH):
                        nc.tensor.matmul(y[:, :, j:CH], kk[:, t, j, :], u[:, :, 0:CH - j], start=j == 0, stop=False)
                    for i in range(CH):
                        last = nc.tensor.matmul(y[:, :, i], yc[:, i * D + t * P:i * D + (t + 1) * P], k.ident[0:NCH, 0:NCH],
                                                start=False, stop=i == CH - 1)
                    last.then_inc(y_ps, 1)
                pe.wait_ge(fin_ok, 1)
                for n in range(NSEQ + 1):
                    last = nc.tensor.transpose(ps_b[0:G5, 4 + n // 4, (n % 4) * P:(n % 4 + 1) * P], fin[:, n, :], k.ident[:])
                last.then_inc(fin_ps, 1)

            @block.scalar
            def _(act):
                S = nc.scalar
                for b in range(5):
                    act.wait_ge(swapped, b + 1)
                    S.copy(icc[:, 512 * b:512 * (b + 1)], ps_b[:, b, :]).then_inc(icc_ok, 1)
                for t in range(KC):
                    act.wait_ge(kk_ps, t + 1)
                    S.copy(kk[:, t].rearrange("p j n -> p (j n)"), ps_b[:, 2 * (t % 2):2 * (t % 2) + 2, :].rearrange("p a b -> p (a b)")
                           ).then_inc(kk_ok, 1)
                for m in range(16):
                    act.wait_ge(cross, m + 1)
                    S.copy(yc.rearrange("q (s g c) -> q g s c", s=CH, c=C5)[:, 4 * m:4 * m + 4],
                           ps_b[0:NCH, 4 + m % 4, :].rearrange("q (g s c) -> q g s c", g=4, c=C5)).then_inc(cross_ok, 1)
                for t in range(KC):
                    act.wait_ge(y_ok, t + 1)
                    S.activation(zT[:, t, :], yt[:, t % 2, :], ACT.Gelu_apprx_tanh).then_inc(gelu_ok, 1)
                act.wait_ge(fin_ps, 1)
                S.copy(fout.rearrange("g n p -> g (n p)"), ps_b[0:G5, 4:7, :].rearrange("g a b -> g (a b)")[:, 0:(NSEQ + 1) * P]
                       ).then_inc(fout_ok, 1)
                act.wait_ge(fout_ok, 1)
                for i, n in enumerate(("re", "im")):
                    act.dma_start(k.o[f"s5_{n}_prompt"][0, 0], fout[:, 0, i * S5:(i + 1) * S5]).then_inc(out_s, 16)
                    act.dma_start(k.o[f"s5_{n}_sample"][0].rearrange("n g p -> g n p"), fout[:, 1:, i * S5:(i + 1) * S5]
                                  ).then_inc(out_s, 16)
                act.wait_ge(out_s, 64)

            @block.vector
            def _(dve):
                own = Own(dve, own_s)
                tt = V.tensor_tensor
                ar8 = s["ar"][:, CH]
                ar2 = ar8.unsqueeze(1).broadcast_to([P, 2, G5])
                own.inc(V.memset(v3[:, 0], 0.0))
                own.inc(V.tensor_copy(ai2[:, 0], s["ai"][:, CH]))
                own.inc(V.tensor_scalar(ai2[:, 1], s["ai"][:, CH], -1.0, None, ALU.mult))
                own.inc(V.memset(s["xs"][:, :, 0], 0.0))
                own.inc(V.tensor_copy(s["xs"][:, :, PCH:NCH].rearrange("p g n -> p n g"), s["s0"][:, 0]))
                own.sync()
                dve.wait_ge(icc_ok, 5)
                for q in range(PCH):
                    a, b = v3[:, q % 2], v3[:, (q + 1) % 2]
                    own.inc(tt(t1[:], a[:, 0:2], ar2, ALU.mult))
                    own.do(tt(t2[:], a[:, 1:3], ai2[:], ALU.mult))
                    own.inc(tt(t1[:, 0], t1[:, 0], cc[:, :, q], ALU.add))
                    own.do(tt(t1[:, 1], t1[:, 1], icv[:, :, q], ALU.add))
                    own.inc(tt(b[:, 0:2], t1[:], t2[:], ALU.add))
                    own.inc(tt(b[:, 2], t1[:, 0], t2[:, 0], ALU.add))
                    dst = s["xs"][:, :, q + 1] if q + 1 < PCH else fin[:, 0]
                    own.do(tt(dst, t1[:, 0], t2[:, 0], ALU.add))
                dve.sem_inc(xs_ok, 1)
                ai8 = s["ai"][:, CH]
                own.inc(tt(f1[:], s["s0"][:, 0], ar8.unsqueeze(1).broadcast_to([P, NSEQ, G5]), ALU.mult))
                own.do(tt(fin[:, 1:], s["s0"][:, 1], ai8.unsqueeze(1).broadcast_to([P, NSEQ, G5]), ALU.mult))
                own.do(tt(f1[:], f1[:], fin[:, 1:], ALU.add))
                own.do(tt(fin[:, 1:], f1[:], cc[:, :, PCH:NCH].rearrange("p g n -> p n g"), ALU.add))
                dve.sem_inc(fin_ok, 1)
                for t in range(KC):
                    dve.wait_ge(y_ps, t + 1)
                    if t >= 2:
                        dve.wait_ge(gelu_ok, t - 1)
                    V.scalar_tensor_tensor(out=yt[:, t % 2, :], in0=k.xT[:, t, :], scalar=s["d"][:, t:t + 1],
                                           in1=ps_b[:, t % 2, 0:NTOK], op0=ALU.mult, op1=ALU.add).then_inc(y_ok, 1)


def glu_phase(k, zT):
    nc = k.nc
    V = nc.vector
    w = k.i["s5_w_glu"][0].rearrange("(c p) n -> p c n", p=P)
    with k.phase() as ctx:
        wg = k.sb(ctx, "wg", [P, KC, 2 * D])
        bias = k.sb(ctx, "bglu", [P, 2 * D])
        a = k.sb(ctx, "glu_a", [P, 2, 512])
        b = k.sb(ctx, "glu_b", [P, 2, 512])
        acc = k.ps(ctx, "glu_ps", [P, 4, 2, 512])
        ready = [k.sem(f"glu_w{n}") for n in range(4)]
        bias_in, done, linear, sig, own_s = (k.sem("glu_" + n) for n in "bias done linear sig own".split())
        units = [(t, half) for half in range(2) for t in range(TILES)]
        with nc.Block() as block:
            @block.sync
            def _(sp):
                for n, col in enumerate((0, 1024, 512, 1536)):
                    sp.dma_start(wg[:, :, col:col + 512], w[:, :, col:col + 512]).then_inc(ready[n], 16)
                sp.dma_start(bias[:], k.i["s5_b_glu"][0].partition_broadcast(P)).then_inc(bias_in, 16)

            @block.tensor
            def _(pe):
                for m, (t, half) in enumerate(units):
                    if m >= 4:
                        pe.wait_ge(linear, m - 3)
                    for part in range(2):
                        pe.wait_ge(ready[2 * half + part], 16)
                        col = part * D + half * 512
                        for c in range(KC):
                            last = nc.tensor.matmul(acc[0:ROWS[t], m % 4, part, :], zT[:, c, P * t:P * t + ROWS[t]],
                                                    wg[:, c, col:col + 512], start=c == 0, stop=c == KC - 1)
                    last.then_inc(done, 1)

            @block.scalar
            def _(act):
                for m, (t, half) in enumerate(units):
                    act.wait_ge(linear, m + 1)
                    nc.scalar.activation(b[0:ROWS[t], m % 2, :], b[0:ROWS[t], m % 2, :], ACT.Sigmoid).then_inc(sig, 1)

            @block.vector
            def _(dve):
                own = Own(dve, own_s)
                dve.wait_ge(bias_in, 16)

                def gate(m):
                    t, half = units[m]
                    r = ROWS[t]
                    dve.wait_ge(sig, m + 1)
                    own.do(V.tensor_tensor(a[0:r, m % 2], a[0:r, m % 2], b[0:r, m % 2], ALU.mult))
                    h = k.h[0:r, t, half * 512:(half + 1) * 512]
                    own.do(V.tensor_tensor(h, h, a[0:r, m % 2], ALU.add))

                for m, (t, half) in enumerate(units):
                    r = ROWS[t]
                    dve.wait_ge(done, m + 1)
                    own.do(V.tensor_tensor(a[0:r, m % 2], acc[0:r, m % 4, 0], bias[0:r, half * 512:(half + 1) * 512], ALU.add))
                    V.tensor_tensor(b[0:r, m % 2], acc[0:r, m % 4, 1], bias[0:r, D + half * 512:D + (half + 1) * 512],
                                    ALU.add).then_inc(linear, 1)
                    if m:
                        gate(m - 1)
                gate(len(units) - 1)


def final_norm(k):
    yp = k.o["y_prompt"].rearrange("b (t p) d -> t p (b d)", p=P)
    norm_phase(k, "nf", k.i["norm_f"], None, [yp[0], yp[1], k.o["y_sample"].rearrange("n t d -> (n t) d")])


def program(nc, ins, outs, consts, scratch):
    k = Core(nc, ins, outs, consts, scratch)
    with ExitStack() as ctx:
        k.software_dma_semaphores(ctx)
        k.h = k.sb(ctx, "h", [P, TILES, D])
        k.ident = k.sb(ctx, "ident", [P, P])
        rows = [scratch["xn"][P * t:P * t + ROWS[t], :] for t in range(TILES)]
        with ExitStack() as zc:
            z = k.sb(zc, "z", [P, TILES, IN_W])
            with ExitStack() as xc:
                k.xT = k.sb(xc, "xT0", [P, KC, NTOK])
                norm_phase(k, "n10", ins["norm1"][0], "pc", None)
                in_proj_phase(k, z)
            mix = k.sb(zc, "mix", [P, TILES, MIX_W])
            even_mixer_phase(k, z, mix)
            out_proj_phase(k, mix)
        moe_layer(k, 0, rows)
        with ExitStack() as zc:
            zT = k.sb(zc, "zT", [P, KC, NTOK])
            with ExitStack() as xc:
                k.xT = k.sb(xc, "xT1", [P, KC, NTOK])
                norm_phase(k, "n11", ins["norm1"][1], "cp", rows)
                s5_layer(k, zT)
            glu_phase(k, zT)
        moe_layer(k, 1, rows)
        final_norm(k)


INPUTS = ("x_prompt", "x_sample", "cache_k", "cache_v", "state_ret", "state_s5_re", "state_s5_im", "page_table",
          "norm1", "norm2", "norm_f", "w_in_even", "w_out_even", "s5_lam_re", "s5_lam_im", "s5_log_dt", "s5_b_re",
          "s5_b_im", "s5_c_re", "s5_c_im", "s5_d", "s5_w_glu", "s5_b_glu", "moe_w_group", "moe_b_group",
          "moe_w_expert", "moe_b_expert", "moe_w13", "moe_w2")
OUTPUTS = (("y_prompt", (1, 256, D)), ("y_sample", (NSEQ, DSEQ, D)),
           ("k_prompt", (1, 1, 2, PAGE, H, HD)), ("v_prompt", (1, 1, 2, PAGE, H, HD)),
           ("k_sample", (1, NSEQ, DSEQ, H, HD)), ("v_sample", (1, NSEQ, DSEQ, H, HD)),
           ("ret_prompt", (1, 1, H, DK, DV)), ("ret_sample", (1, NSEQ, H, DK, DV)),
           ("s5_re_prompt", (1, 1, G5, S5)), ("s5_im_prompt", (1, 1, G5, S5)),
           ("s5_re_sample", (1, NSEQ, G5, S5)), ("s5_im_sample", (1, NSEQ, G5, S5)))
SCRATCH = (("xn", (NTOK, D)), ("smix", (NSEQ, DSEQ, H, HD)), ("yblk", (NBLK * SLOT, D)))


def kernel(**inputs):
    from concourse import bacc
    from concourse.bass_utils import run_bass_kernel_spmd

    nc = bacc.Bacc("TRN2", target_bir_lowering=False, num_devices=1)
    arrays, ins, consts = {}, {}, {}
    for name in INPUTS:
        a = np.ascontiguousarray(inputs[name])
        arrays["in_" + name] = a
        ins[name] = nc.dram_tensor("in_" + name, a.shape, mybir.dt.from_np(a.dtype), kind="ExternalInput").ap()
    for name, a in constants().items():
        arrays["table_" + name] = np.ascontiguousarray(a)
        consts[name] = nc.dram_tensor("table_" + name, a.shape, F32, kind="ExternalInput").ap()
    outs = {n: nc.dram_tensor("out_" + n, s, F32, kind="ExternalOutput").ap() for n, s in OUTPUTS}
    scratch = {n: nc.dram_tensor("scratch_" + n, s, F32).ap() for n, s in SCRATCH}
    program(nc, ins, outs, consts, scratch)
    r = run_bass_kernel_spmd(nc, [arrays], core_ids=[0])
    return tuple(r.results[0]["out_" + n] for n, _ in OUTPUTS)
```

```python
from contextlib import ExitStack, contextmanager

import concourse.bass as bass
import numpy as np
from concourse import mybir

F32 = mybir.dt.float32
I32 = mybir.dt.int32
U32 = mybir.dt.uint32
ALU = mybir.AluOpType
ACT = mybir.ActivationFunctionType
X = mybir.AxisListType.X

P = 128
D = 1024
KC = D // P
TILES = 3
ROWS = (128, 128, 64)
NTOK = sum(ROWS)
NSEQ, DSEQ = 8, 8
NS = NSEQ * DSEQ
H, HD = 8, 64
ROT = 8
DK, DV = 64, 128
PAGE = 128
IN_W = 4608
MIX_W = 1536
KM = MIX_W // P
QA, KA, VA, QR, KR, VR, GR = 0, 512, 1024, 1536, 2048, 2560, 3584
NEG = -1e30
SEMAPHORES, LARGEST_PHASE = 140, 62
EPS = 1e-6
GROUPS, PER, NE = 4, 8, 32
DE = 512
SLOT = 64
MAXB = NE + (2 * NTOK - NE) // SLOT
MINB = 2 * NTOK // SLOT
BUFS = 3
NBLK = -(-(MAXB + BUFS) // BUFS) * BUFS
G5, C5, S5 = 64, 16, 64
CH = 8
NCH = NTOK // CH
PCH = 256 // CH


def constants():
    f = np.float32
    pos = np.concatenate([np.arange(256), 256 + np.arange(NS) % DSEQ]).astype(f)
    out = {}

    def tiles(a):
        b = np.zeros((P, TILES) + a.shape[1:], f)
        b[:, 0], b[:, 1], b[:NS, 2] = a[:128], a[128:256], a[256:]
        return b

    inv = (f(500000.0) ** (-np.arange(ROT, dtype=f) / f(ROT))).astype(f)
    ang = pos[:, None] * inv[None]
    out["rope"] = tiles(np.stack([np.cos(ang), np.sin(ang)], 1).astype(f))
    inv = (f(1.0) / (f(10000.0) ** np.linspace(0.0, 1.0, DK // 2, dtype=f))).astype(f)
    ang = pos[:, None] * inv[None]
    cs = np.stack([np.cos(ang), np.sin(ang)], 1).astype(f)
    out["xpos"] = tiles(np.stack([cs, cs * f(DK ** -0.5)], 2))
    lg = np.log(f(1.0) - f(2.0) ** (f(-5.0) - np.arange(H, dtype=f))).astype(f)

    def decay(c):
        i = np.arange(c, dtype=f)
        diff = i[None, :] - i[:, None]
        return np.where(diff[:, None] >= 0, np.exp(np.maximum(diff, 0)[:, None] * lg[None, :, None]), 0).astype(f)

    order = [0, 2, 4, 6, 1, 3, 5, 7]
    out["dmat"] = decay(128)[:, order]
    same = (np.arange(NS)[:, None] // DSEQ == np.arange(NS)[None] // DSEQ)
    small = decay(DSEQ)
    i = np.arange(NS) % DSEQ
    out["dmat_s"] = (small[i][:, :, i] * same[:, None])[:, order].astype(f)
    i = np.concatenate([np.arange(256) % 128, np.arange(NS) % DSEQ]).astype(f)
    out["dq"] = tiles(np.exp((i + 1)[:, None] * lg[None]).astype(f))
    j = np.arange(128, dtype=f)
    out["dk"] = np.exp((127 - j)[:, None] * lg[None]).astype(f)
    j = (np.arange(NS) % DSEQ).astype(f)
    dks = np.exp((DSEQ - 1 - j)[:, None] * lg[None]).astype(f)
    seq = (np.arange(NS)[:, None] // DSEQ == np.arange(NSEQ)[None]).astype(f)
    out["dk_s"] = (dks[:, None, :] * seq[:, :, None]).astype(f)
    head = 2 * np.arange(4)[None] + np.arange(P)[:, None] // 64
    out["dc"] = np.stack([np.exp(f(128) * lg)[head], np.exp(f(DSEQ) * lg)[head]], 1).astype(f)
    q, k = np.arange(128)[:, None], np.arange(256)[None]
    out["causal"] = np.stack([np.where(k <= q, 0, NEG), np.where(k <= q + 128, 0, NEG)], 1).astype(f)
    t = np.arange(NS)[:, None, None] % DSEQ
    n, kk = np.arange(NSEQ)[None, :, None], np.arange(NS)[None, None]
    own = np.where((kk // DSEQ == n) & (kk % DSEQ <= t), 0, NEG).astype(f)
    out["own"] = own.reshape(NS, NSEQ // 2, 2, NS).transpose(2, 0, 1, 3).reshape(P, NSEQ // 2, NS)
    out["ident"] = np.eye(P, dtype=f)
    out["before"] = np.triu(np.ones((P, P), f), 1)
    sw = np.zeros((P, P), f)
    for p in range(S5):
        sw[S5 + p, p], sw[p, S5 + p] = -1, 1
    out["swap"] = sw
    tok = np.arange(P, dtype=f)[:, None] + 128 * np.arange(TILES, dtype=f)[None]
    out["token"] = tok.astype(f)
    out["heads"] = np.broadcast_to((np.arange(P)[:, None] % NS // DSEQ == np.arange(H)[None])[:, :, None],
                                   (P, H, HD)).astype(f)
    return out


class Own:

    def __init__(self, eng, sem):
        self.eng, self.sem, self.n = eng, sem, 0

    def inc(self, ins):
        ins.then_inc(self.sem, 1)
        self.n += 1

    def sync(self):
        self.eng.wait_ge(self.sem, self.n)

    def do(self, ins):
        self.inc(ins)
        self.sync()


class Core:

    def __init__(self, nc, ins, outs, consts, scratch):
        self.nc, self.i, self.o, self.c, self.d = nc, ins, outs, consts, scratch
        self.h = self.ident = self.xT = None
        self.nest, self.ctx, self.dirty = [], [], []

    def software_dma_semaphores(self, ctx):
        def sem(name):
            return ctx.enter_context(self.nc.semaphore(name))

        self.cleared = sem("yblk_cleared")
        self.gathered = [[sem(f"gathered{li}{b}") for b in range(BUFS)] for li in range(2)]
        self.combined = [sem(f"yg_got{m}") for m in range(2 * TILES)]

    @contextmanager
    def phase(self):
        self.nest.append([])
        with ExitStack() as ctx:
            self.ctx.append(ctx)
            yield ctx
            self.ctx.pop()
        self.dirty += self.nest.pop()
        if len(self.nest) == 0 and len(self.dirty) > SEMAPHORES - LARGEST_PHASE:
            self.clear()

    def clear(self):
        runs = []
        for n in sorted(set(self.dirty)):
            if runs and n == runs[-1][1] + 1:
                runs[-1][1] = n
            else:
                runs.append([n, n])
        self.dirty = []
        with self.nc.Block() as block:
            @block.gpsimd
            def _(pool):
                for lo, hi in runs:
                    pool.sem_clear(range(lo, hi + 1))

    def sem(self, name):
        s = self.ctx[-1].enter_context(self.nc.semaphore(name))
        self.nest[-1].append(s.num)
        return s

    def sb(self, ctx, name, shape, dt=F32):
        return ctx.enter_context(self.nc.sbuf_tensor(name, shape, dt))

    def ps(self, ctx, name, shape):
        return ctx.enter_context(self.nc.psum_tensor(name, shape, F32))


def norm_phase(k, tag, gain, chunks, store, ahead=None, later=None, behind=None):
    nc = k.nc
    with k.phase() as ctx:
        xn = later[0] if later else k.sb(ctx, f"xn_{tag}", [P, TILES, D])
        g = k.sb(ctx, f"gain_{tag}", [P, D])
        ss = k.sb(ctx, f"ss_{tag}", [P, 4])
        ms = k.sb(ctx, f"ms_{tag}", [P, 4])
        rstd = k.sb(ctx, f"rstd_{tag}", [P, 4])
        turned_ps = k.ps(ctx, f"turned_ps_{tag}", [P, TILES, D])
        loaded, squares, cleared = k.sem(f"loaded_{tag}"), k.sem(f"squares_{tag}"), k.sem(f"cleared_{tag}")
        own, inv, root = k.sem(f"own_{tag}"), k.sem(f"inv_{tag}"), k.sem(f"root_{tag}")
        normed, turned = k.sem(f"normed_{tag}"), k.sem(f"turned_{tag}")
        stored = later[1] if later else k.sem(f"stored_{tag}")
        first = tag == "n10"
        s_h = k.sem(f"h_{tag}")
        with nc.Block() as block:
            @block.sync
            def _(sp):
                sp.dma_start(g[:], gain.partition_broadcast(P)).then_inc(loaded, 16)
                if ahead:
                    ahead(sp)
                for t in range(TILES if store else 0):
                    sp.wait_ge(normed, t + 1)
                    sp.dma_start(store[t], xn[0:ROWS[t], t, :]).then_inc(stored, 16)
                if behind:
                    behind(sp)
                if store and not later:
                    sp.wait_ge(stored, 16 * TILES)

            @block.scalar
            def _(act):
                if first:
                    act.dma_start(k.h[:, 0:2, :], k.i["x_prompt"].rearrange("b (t p) d -> p (b t) d", p=P)
                                  ).then_inc(s_h, 16)
                    act.dma_start(k.h[0:NS, 2, :], k.i["x_sample"].rearrange("b t d -> (b t) d")
                                  ).then_inc(s_h, 16)
                    act.dma_start(k.ident[:], k.c["ident"]).then_inc(s_h, 16)
                    act.wait_ge(s_h, 48)
                act.wait_ge(cleared, 1)
                for t in range(TILES):
                    r = ROWS[t]
                    nc.scalar.activation(xn[0:r, t, :], k.h[0:r, t, :], ACT.Square,
                                         accum_out=ss[0:r, t:t + 1]).then_inc(squares, 1)
                act.wait_ge(inv, 1)
                nc.scalar.activation(rstd[:], ms[:], ACT.Sqrt).then_inc(root, 1)
                if chunks:
                    for t in range(TILES):
                        act.wait_ge(turned, 2 * t + 1)
                        nc.scalar.activation(k.xT[:, 0:4, P * t:P * t + ROWS[t]],
                                             turned_ps[:, t, 0:512].rearrange("p (c n) -> p c n", c=4)[:, :, 0:ROWS[t]],
                                             ACT.Copy)

            @block.vector
            def _(dve):
                nc.vector.memset(ss[:], 1.0).then_inc(cleared, 1)
                o = Own(dve, own)
                dve.wait_ge(squares, TILES)
                if first:
                    dve.wait_ge(s_h, 48)
                o.do(nc.vector.tensor_scalar(ss[:], ss[:], 1.0 / D, EPS, ALU.mult, ALU.add))
                nc.vector.reciprocal(ms[:], ss[:]).then_inc(inv, 1)
                dve.wait_ge(root, 1)
                dve.wait_ge(loaded, 16)
                for t in range(TILES):
                    r = ROWS[t]
                    nc.vector.scalar_tensor_tensor(out=xn[0:r, t, :], in0=k.h[0:r, t, :], scalar=rstd[0:r, t:t + 1],
                                                   in1=g[0:r, :], op0=ALU.mult, op1=ALU.mult).then_inc(normed, 1)
                if chunks:
                    for t in range(TILES):
                        dve.wait_ge(turned, 2 * t + 2)
                        nc.vector.tensor_copy(k.xT[:, 4:8, P * t:P * t + ROWS[t]],
                                              turned_ps[:, t, 512:1024].rearrange("p (c n) -> p c n", c=4)[:, :, 0:ROWS[t]])

            @block.tensor
            def _(pe):
                if not chunks:
                    return
                if first:
                    pe.wait_ge(s_h, 48)
                for t in range(TILES):
                    r = ROWS[t]
                    pe.wait_ge(normed, t + 1)
                    for c in range(KC):
                        src = xn[0:r, t, c:D:KC] if chunks == "pc" else xn[0:r, t, c * P:(c + 1) * P]
                        last = nc.tensor.transpose(turned_ps[:, t, c * P:c * P + r], src, k.ident[0:r, 0:r])
                        if c % 4 == 3:
                            last.then_inc(turned, 1)


def in_proj_phases(k, z, gain):
    nc = k.nc
    NB, RING = 384, 4
    w = k.i["w_in_even"].rearrange("e (p c) n -> p (e c) n", c=KC)
    with k.phase() as ctx:
        wr = k.sb(ctx, "win_ring", [P, RING, KC, NB])
        w_ready = [k.sem(f"win_ready{r}") for r in range(RING)]

        def ahead(sp):
            for r in range(RING):
                sp.dma_start(wr[:, r], w[:, :, r * NB:(r + 1) * NB]).then_inc(w_ready[r], 16)

        norm_phase(k, "n10", gain, "pc", None, ahead)
        zp = k.ps(ctx, "z_ps", [P, 2, 2, 512])
        zs = k.ps(ctx, "z_ps_s", [P, 2, 512])
        w_used = k.sem("win_used")
        zero = k.sb(ctx, "zero_rows", [P, D])
        zeroed, cleared = k.sem("zero_made"), k.cleared
        done = [k.sem(f"z_done{t}") for t in range(TILES)]
        copied = [k.sem(f"z_copied{t}") for t in range(TILES)]
        ROUNDS = IN_W // NB // RING
        with nc.Block() as block:
            @block.sync
            def _(sp):
                with sp.Fori(1, ROUNDS) as j:
                    for r in range(RING):
                        n = j * RING + r
                        sp.wait_ge(w_used, n - RING + (2 if r % 2 == 0 else 1))
                        sp.dma_start(wr[:, r], w[:, :, bass.ds(n * NB, NB)]).then_inc(w_ready[r], 16)

            @block.gpsimd
            def _(pool):
                nc.gpsimd.memset(zero[:], 0.0).then_inc(zeroed, 1)
                pool.wait_ge(zeroed, 1)
                lots = k.d["yblk"][MINB * SLOT:(NBLK - BUFS) * SLOT].rearrange("(n p) d -> n p d", p=P)
                for n in range(lots.shape[0]):
                    pool.dma_start(lots[n], zero[:]).then_inc(cleared, 16)
                pool.wait_ge(cleared, 16 * lots.shape[0])

            @block.tensor
            def _(pe):
                with pe.Fori(0, ROUNDS) as j:
                    for r in range(RING):
                        n = j * RING + r
                        pe.wait_ge(w_ready[r], 16 * j + 16)
                        for t in range(2):
                            pe.wait_ge(copied[t], n + 1)
                            for c in range(KC):
                                last = nc.tensor.matmul(zp[:, t, r % 2, 0:NB], k.xT[:, c, P * t:P * (t + 1)],
                                                        wr[:, r, c, :], start=c == 0, stop=c == KC - 1)
                            last.then_inc(done[t], 1)
                        if r % 2:
                            pair = j * (RING // 2) + r // 2
                            pe.wait_ge(copied[2], 2 * pair + 1)
                            for c in range(KC):
                                for half in range(2):
                                    last = nc.tensor.matmul(zs[64 * half:64 * half + 64, r // 2, 0:NB], k.xT[:, c, 256:320],
                                                            wr[:, r - 1 + half, c, :], start=c == 0, stop=c == KC - 1)
                            last.then_inc(done[2], 1)
                            pe.wait_ge(done[2], pair + 1)
                            pe.sem_inc(w_used, 2)

            @block.scalar
            def _(act):
                act.sem_inc(copied[0], 2)
                with act.Fori(0, ROUNDS) as j:
                    for r in range(RING):
                        n = j * RING + r
                        act.wait_ge(done[0], n + 1)
                        nc.scalar.copy(z[:, 0, bass.ds(n * NB, NB)], zp[:, 0, r % 2, 0:NB]).then_inc(copied[0], 1)

            @block.vector
            def _(dve):
                dve.sem_inc(copied[1], 2)
                dve.sem_inc(copied[2], 4)
                with dve.Fori(0, ROUNDS) as j:
                    for r in range(RING):
                        n = j * RING + r
                        dve.wait_ge(done[1], n + 1)
                        nc.vector.tensor_copy(z[:, 1, bass.ds(n * NB, NB)], zp[:, 1, r % 2, 0:NB]).then_inc(copied[1], 1)
                        if r % 2:
                            dve.wait_ge(done[2], j * (RING // 2) + r // 2 + 1)
                            for half in range(2):
                                nc.vector.tensor_copy(z[0:NS, 2, bass.ds((n - 1 + half) * NB, NB)],
                                                      zs[64 * half:64 * half + 64, r // 2, 0:NB]).then_inc(copied[2], 1)


def even_mixer_phase(k, z, mix):
    nc, c = k.nc, k.c
    PAIRS = NSEQ // 2
    with k.phase() as ctx:
        def sb(name, shape, dt=F32):
            return k.sb(ctx, name, shape, dt)

        rope = sb("rope", [P, TILES, 2, ROT])
        xpos = sb("xpos", [P, TILES, 2, 2, DK // 2])
        dmat, dmat_s = sb("dmat", [P, H, P]), sb("dmat_s", [NS, H, NS])
        dq, dk, dk_s = sb("dq", [P, TILES, H]), sb("dk", [P, H]), sb("dk_s", [NS, NSEQ, H])
        dc = sb("dc", [P, 2, 4])
        causal, own_mask = sb("causal", [P, 2, 256]), sb("own", [P, PAIRS, NS])
        heads = sb("heads", [P, H * HD])
        turns = [(rope, "rope"), (xpos, "xpos")]
        tables = [(dmat, "dmat"), (dmat_s, "dmat_s"), (dq, "dq"), (dk, "dk"),
                  (dk_s, "dk_s"), (dc, "dc"), (causal, "causal"), (own_mask, "own")]
        pages = sb("pages", [1, 16], I32)
        qt = sb("qt", [P, 16, NTOK])
        ra = sb("ra", [P, 4, 16, ROT])
        big = sb("big", [P, 2112])
        rb = big[:, 0:2048].rearrange("p (f n) -> p f n", f=4)
        soft = sb("soft", [P, 4096])
        sc = soft[:, 0:1024].rearrange("p (h n) -> p h n", h=4)
        pr = soft[:, 1024:2048].rearrange("p (h n) -> p h n", h=4)
        prt = soft[:, 2048:3072].rearrange("p (h n) -> p h n", h=8)
        km = soft[0:NS, :]
        mx, sm, rs = sb("mx", [P, 4]), sb("sm", [P, 4]), sb("rs", [P, 4])
        attkd = sb("attkd", [P, 2 * H * P])
        att = attkd[:, 0:H * P]
        kd = attkd[:, H * P:].rearrange("p (t x) -> p t x", t=2)
        sq = sb("sq", [P, 2, 4 * DV])
        st = sb("st", [P, 4, DV])
        st_out = sb("st_out", [P, 4, DV])
        ss = sb("ss_state", [P, NSEQ, 4, DV])
        tmp = sb("tmp_o", [P, H * DV])
        nrm, nrm2 = sb("nrm", [P, TILES, H]), sb("nrm2", [P, TILES, H])
        qb = sb("qb", [P, NSEQ, 320])
        kv01 = sb("kv", [P, 2, 2048])
        kv = [a.rearrange("p (g v x) -> p g v x", g=2, v=2) for a in (kv01[:, 0], kv01[:, 1], attkd[:], big[:, 0:2048])]
        kT = soft[:, 0:2048].rearrange("p (j c n) -> p j c n", j=2, c=4)
        scs = soft[:, 2048:2688].rearrange("p (a n) -> p a n", a=2)
        prs = soft[:, 2688:3328].rearrange("p (a n) -> p a n", a=2)
        prst = soft[:, 3328:4096].rearrange("p (a b n) -> p a b n", a=2, b=3)
        so = sb("so", [P, PAIRS, HD])
        sml = sb("sml", [P, 3, PAIRS])
        msk = tmp[:].rearrange("p (a b) -> p a b", a=2)

        pt = k.ps(ctx, "mix_pt", [P, 2, 512])
        ps = k.ps(ctx, "mix_ps", [P, 2, 512])
        po = k.ps(ctx, "mix_po", [P, 2, 512])
        pd = k.ps(ctx, "mix_pd", [P, 2, 512])

        S = {n: k.sem("mx_" + n) for n in (
            "turns tables pages states own pool roped rotated qt_turned qt_copied kv_out scores scaled "
            "probs p_turned p_copied pv mixed ss_new "
            "att decayed ocross orr kd state st_copied st_final st_stored kvm qm "
            "qb kt_turned kt_copied s_scores s_scaled s_probs ps_turned ps_copied s_pv s_out s_stored s_loaded "
            "s_masked o_ready squares osq root osil gated squared ss_stored actown").split()}
        kv_ready = [k.sem(f"mx_kv_ready{b}") for b in range(2)]
        flat_state = "h d e -> (h d) e"

        with nc.Block() as block:
            @block.sync
            def _(sp):
                for t, name in turns:
                    sp.dma_start(t[:], c[name]).then_inc(S["turns"], 16)
                sp.dma_start(pages[:], k.i["page_table"].rearrange("(a n) p -> a (n p)", a=1)).then_inc(S["pages"], 16)
                for t, name in tables:
                    sp.dma_start(t[:], c[name]).then_inc(S["tables"], 16)
                sp.dma_start(heads[:], c["heads"].rearrange("p h d -> p (h d)")).then_inc(S["tables"], 16)
                sp.dma_start(ss[:], k.i["state_ret"][0].rearrange("n h d e -> n (h d) e")
                             .rearrange("n (c p) e -> p n c e", p=P)).then_inc(S["states"], 16)
                sp.wait_ge(S["pages"], 16)

                def attention_leaves(m):
                    sp.wait_ge(S["s_out"], m + 1)
                    sp.dma_start(k.d["smix"][m], so[:, m]).then_inc(S["s_stored"], 16)
                    sp.wait_ge(S["s_stored"], 16 * (m + 1))
                    for j in range(2):
                        n = 2 * m + j
                        sp.dma_start(mix[DSEQ * n:DSEQ * (n + 1), 2, 0:512].rearrange("t (h e) -> t h e", h=H),
                                     k.d["smix"][m, NS * j:NS * (j + 1)].rearrange("(h t) e -> t h e", t=DSEQ)
                                     ).then_inc(S["s_loaded"], 16)

                for m in range(PAIRS):
                    if m == 1:
                        sp.wait_ge(S["o_ready"], 3)
                    elif m:
                        sp.wait_ge(S["s_pv"], m - 1)
                    for j in range(2):
                        n = 2 * m + j
                        for g in range(2):
                            page = sp.value_load(pages[0:1, 2 * n + g:2 * n + g + 1], min_val=0, max_val=19)
                            for v, cache in enumerate(("cache_k", "cache_v")):
                                sp.dma_start(kv[n % 4][:, g, v, :],
                                             k.i[cache][0].rearrange("n s h d -> n s (h d)")[bass.ds(page, 1)]
                                             .rearrange("a s f -> s (a f)")).then_inc(kv_ready[m % 2], 16)
                    if m == 1:
                        sp.wait_ge(S["ss_new"], NSEQ)
                        sp.dma_start(k.o["ret_sample"][0].rearrange("n h d e -> n (h d) e")
                                     .rearrange("n (c p) e -> p n c e", p=P), ss[:]).then_inc(S["ss_stored"], 16)
                    if m >= 2:
                        attention_leaves(m - 2)
                for m in (PAIRS - 2, PAIRS - 1):
                    attention_leaves(m)
                sp.wait_ge(S["s_loaded"], 32 * PAIRS)
                sp.wait_ge(S["ss_stored"], 16)

            @block.gpsimd
            def _(pool):
                own = Own(pool, S["pool"])
                own.inc(nc.gpsimd.memset(qb[:], 0.0))
                pool.wait_ge(S["turns"], 32)
                for t in range(TILES):
                    r = ROWS[t]
                    qk = z[0:r, t, QA:VA].rearrange("p (h d) -> p h d", d=HD)
                    x1, x2 = qk[:, :, 0:ROT], qk[:, :, ROT:2 * ROT]
                    co, si = (rope[0:r, t, i].unsqueeze(1).broadcast_to([r, 16, ROT]) for i in range(2))
                    for i, (a, b) in enumerate(((x1, co), (x2, si), (x2, co), (x1, si))):
                        own.inc(nc.gpsimd.tensor_tensor(ra[0:r, i], a, b, ALU.mult))
                    own.sync()
                    own.inc(nc.gpsimd.tensor_tensor(x1, ra[0:r, 0], ra[0:r, 1], ALU.subtract))
                    own.do(nc.gpsimd.tensor_tensor(x2, ra[0:r, 2], ra[0:r, 3], ALU.add))
                    pool.sem_inc(S["roped"], 1)
                pool.wait_ge(S["tables"], 16 * 9)
                pool.wait_ge(S["rotated"], 2)
                for t in range(2):
                    nc.gpsimd.tensor_tensor(kd[:, t].rearrange("p (h d) -> p h d", d=DK),
                                            z[:, t, KR:VR].rearrange("p (h d) -> p h d", d=DK),
                                            dk[:].unsqueeze(2).broadcast_to([P, H, DK]), ALU.mult).then_inc(S["kd"], 1)
                for t in range(TILES):
                    r = ROWS[t]
                    pool.wait_ge(S["osil"], t + 1)
                    pool.wait_ge(S["squared"], t + 1)
                    nc.gpsimd.tensor_tensor(mix[0:r, t, 512:MIX_W], mix[0:r, t, 512:MIX_W], z[0:r, t, GR:], ALU.mult
                                            ).then_inc(S["gated"], 1)

            @block.tensor
            def _(pe):
                for m in range(12):
                    t, g = m // 4, m % 4
                    r = ROWS[t]
                    pe.wait_ge(S["roped"], t + 1)
                    pe.wait_ge(S["rotated"], t + 1)
                    if m >= 2:
                        pe.wait_ge(S["qt_copied"], m - 1)
                    for i in range(4):
                        col = (0 if g < 2 else QR - 1024) + (4 * g + i) * P
                        last = nc.tensor.transpose(pt[:, m % 2, i * P:i * P + r], z[0:r, t, col:col + P], k.ident[0:r, 0:r])
                    last.then_inc(S["qt_turned"], 1)
                pe.wait_ge(S["qt_copied"], 12)

                def q_of(base, h, lo, n):
                    b = 64 * (h % 2)
                    return qt[b:b + 64, base + h // 2, lo:lo + n]

                def scores(u):
                    t, hg = u // 2, u % 2
                    if u:
                        pe.wait_ge(S["scaled"], u)
                    for i in range(4):
                        h = 4 * hg + i
                        last = nc.tensor.matmul(ps[:, i % 2, (i // 2) * 256:(i // 2) * 256 + P * (t + 1)],
                                                q_of(0, h, P * t, P), q_of(4, h, 0, P * (t + 1)), start=True, stop=True)
                    last.then_inc(S["scores"], 1)

                scores(0)
                for u in range(4):
                    t, hg = u // 2, u % 2
                    if u < 3:
                        scores(u + 1)
                    pe.wait_ge(S["probs"], u + 1)
                    if u:
                        pe.wait_ge(S["p_copied"], u)
                    for i in range(4):
                        for b in range(t + 1):
                            s = i * (t + 1) + b
                            last = nc.tensor.transpose(pt[:, s // 4, (s % 4) * P:(s % 4 + 1) * P],
                                                       pr[:, 2 * (i % 2) + i // 2, b * P:(b + 1) * P], k.ident[:])
                    last.then_inc(S["p_turned"], 1)
                    pe.wait_ge(S["p_copied"], u + 1)
                    if u:
                        pe.wait_ge(S["mixed"], u)
                    for i in range(4):
                        h = 4 * hg + i
                        for b in range(t + 1):
                            last = nc.tensor.matmul(po[:, 0, i * HD:(i + 1) * HD], prt[:, i * (t + 1) + b, :],
                                                    z[:, b, VA + h * HD:VA + (h + 1) * HD], start=b == 0, stop=b == t)
                    last.then_inc(S["pv"], 1)

                pe.wait_ge(S["kd"], 2)
                for t in range(TILES):
                    r = ROWS[t]
                    if t == 0:
                        pe.wait_ge(S["scaled"], 4)
                        pe.wait_ge(S["mixed"], 4)
                    else:
                        pe.wait_ge(S["decayed"], t)
                    for h in range(H):
                        last = nc.tensor.matmul(ps[0:r, h % 2, (h // 2) * r:(h // 2 + 1) * r],
                                                q_of(12, h, P * t, r), q_of(8, h, P * t, r), start=True, stop=True)
                    last.then_inc(S["att"], 1)
                    if t < 2:
                        if t == 0:
                            pe.wait_ge(S["p_copied"], 4)
                        else:
                            pe.wait_ge(S["st_copied"], 1)
                        for h in range(H):
                            last = nc.tensor.matmul(pt[64 * (h % 2):64 * (h % 2) + 64, 0, (h // 2) * DV:(h // 2 + 1) * DV],
                                                    kd[:, t, h * DK:(h + 1) * DK], z[:, t, VR + h * DV:VR + (h + 1) * DV],
                                                    start=True, stop=True)
                        last.then_inc(S["state"], 1)
                    if t:
                        pe.wait_ge(S["orr"], t)
                    if t == 1:
                        for h in range(H):
                            b = 64 * (h % 2)
                            last = nc.tensor.matmul(pd[:, h % 2, (h // 2) * DV:(h // 2 + 1) * DV], q_of(8, h, P, P),
                                                    st[b:b + 64, h // 2, :], start=True, stop=True)
                    if t == 2:
                        pe.wait_ge(S["qm"], 1)
                        pe.wait_ge(S["states"], 16)
                        for h in range(H):
                            b = 64 * (h % 2)
                            for n in range(NSEQ):
                                lo = n * 256 + (h // 2) * 64
                                last = nc.tensor.matmul(pd[0:NS, h % 2, (h // 2) * DV:(h // 2 + 1) * DV],
                                                        big[b:b + 64, lo:lo + 64], ss[b:b + 64, n, h // 2, :],
                                                        start=n == 0, stop=n == NSEQ - 1)
                    if t:
                        last.then_inc(S["ocross"], 1)
                    pe.wait_ge(S["decayed"], t + 1)
                    for h in range(H):
                        last = nc.tensor.matmul(po[0:r, h // 4, (h % 4) * DV:(h % 4 + 1) * DV], att[0:r, (4 * (h % 2) + h // 2) * r:(4 * (h % 2) + h // 2 + 1) * r],
                                                z[0:r, t, VR + h * DV:VR + (h + 1) * DV], start=True, stop=True)
                    last.then_inc(S["o_ready"], 1)
                pe.wait_ge(S["st_final"], 1)
                pe.wait_ge(S["kvm"], 1)
                for n in range(NSEQ):
                    if n >= 2:
                        pe.wait_ge(S["ss_new"], n - 1)
                    for h in range(H):
                        last = nc.tensor.matmul(pt[64 * (h % 2):64 * (h % 2) + 64, n % 2, (h // 2) * DV:(h // 2 + 1) * DV],
                                                km[:, n * 512 + h * DK:n * 512 + (h + 1) * DK],
                                                z[0:NS, 2, VR + h * DV:VR + (h + 1) * DV], start=True, stop=True)
                    last.then_inc(S["state"], 1)
                pe.wait_ge(S["ss_new"], NSEQ)
                pe.wait_ge(S["qb"], 1)
                pe.wait_ge(S["orr"], 3)

                def keys(n):
                    if n % 2 == 0:
                        pe.wait_ge(kv_ready[n // 2 % 2], 128 * (n // 4 + 1))
                    if n:
                        pe.wait_ge(S["kt_copied"], 2 * n)
                    for ch in range(4):
                        for g in range(2):
                            last = nc.tensor.transpose(pt[:, ch // 2, ((ch % 2) * 2 + g) * P:((ch % 2) * 2 + g + 1) * P],
                                                       kv[n % 4][:, g, 0, ch * P:(ch + 1) * P], k.ident[:])
                    last.then_inc(S["kt_turned"], 1)

                def pair_scores(m):
                    pe.wait_ge(S["kt_copied"], 4 * (m + 1))
                    if m >= 2:
                        pe.wait_ge(S["s_scaled"], m - 1)
                    for lo, n_k in ((0, 256), (256, 64)):
                        for ch in range(4):
                            for j in range(2):
                                rhs = kT[:, j, ch, :] if lo == 0 else qt[:, 4 + ch, 256:320]
                                last = nc.tensor.matmul(ps[NS * j:NS * (j + 1), m % 2, lo:lo + n_k],
                                                        qb[:, 2 * m + j, ch * 64:(ch + 1) * 64], rhs, start=ch == 0, stop=ch == 3)
                    last.then_inc(S["s_scores"], 1)

                def turn_probs(m):
                    pe.wait_ge(S["s_probs"], m + 1)
                    if m >= 2:
                        pe.wait_ge(S["ps_copied"], m - 1)
                    for b in range(3):
                        w = (P, P, NS)[b]
                        last = nc.tensor.transpose(pd[0:w, m % 2, b * P:(b + 1) * P], prs[:, m % 2, b * P:b * P + w], k.ident[:])
                    last.then_inc(S["ps_turned"], 1)

                def values(m):
                    pe.wait_ge(S["ps_copied"], m + 1)
                    if m >= 2:
                        pe.wait_ge(S["s_masked"], m - 1)
                    for b in range(3):
                        w = (P, P, NS)[b]
                        for j in range(2):
                            rhs = kv[(2 * m + j) % 4][:, b, 1, :] if b < 2 else z[0:NS, 2, VA:VA + 512]
                            last = nc.tensor.matmul(po[NS * j:NS * (j + 1), m % 2, :], prst[0:w, m % 2, b, NS * j:NS * (j + 1)],
                                                    rhs, start=b == 0, stop=b == 2)
                    last.then_inc(S["s_pv"], 1)

                keys(0)
                keys(1)
                pair_scores(0)
                for m in range(PAIRS):
                    if m + 1 < PAIRS:
                        keys(2 * m + 2)
                    turn_probs(m)
                    if m + 1 < PAIRS:
                        keys(2 * m + 3)
                    values(m)
                    if m + 1 < PAIRS:
                        pair_scores(m + 1)

            @block.scalar
            def _(act):
                own = Own(act, S["actown"])
                for t in range(TILES):
                    nc.scalar.activation(z[0:ROWS[t], t, GR:], z[0:ROWS[t], t, GR:], ACT.Silu).then_inc(S["osil"], 1)
                act.wait_ge(S["roped"], 3)
                for name, col in (("k", KA), ("v", VA)):
                    act.dma_start(k.o[name + "_prompt"].rearrange("e b g p h d -> p (e b g) (h d)"), z[:, 0:2, col:col + 512]
                                  ).then_inc(S["kv_out"], 16)
                    act.dma_start(k.o[name + "_sample"].rearrange("e n t h d -> (e n t) (h d)"), z[0:NS, 2, col:col + 512]
                                  ).then_inc(S["kv_out"], 16)
                for m in range(12):
                    t, g = m // 4, m % 4
                    act.wait_ge(S["qt_turned"], m + 1)
                    nc.scalar.copy(qt[:, 4 * g:4 * g + 4, P * t:P * t + ROWS[t]],
                                   pt[:, m % 2].rearrange("p (c n) -> p c n", c=4)[:, :, 0:ROWS[t]]).then_inc(S["qt_copied"], 1)
                for u in range(4):
                    t = u // 2
                    act.wait_ge(S["scaled"], u + 1)
                    if u:
                        act.wait_ge(S["p_turned"], u)
                    nc.scalar.activation(pr[:, :, 0:P * (t + 1)], sc[:, :, 0:P * (t + 1)], ACT.Exp).then_inc(S["probs"], 1)
                    act.wait_ge(S["p_turned"], u + 1)
                    if u:
                        act.wait_ge(S["pv"], u)
                    nc.scalar.copy(prt[:, 0:4 * (t + 1), :], pt[:].rearrange("p a (b n) -> p (a b) n", n=P)[:, 0:4 * (t + 1), :]
                                   ).then_inc(S["p_copied"], 1)
                act.wait_ge(S["st_final"], 1)
                act.dma_start(k.o["ret_prompt"][0, 0].rearrange("h d e -> (h d) e").rearrange("(c p) e -> p c e", p=P),
                              st_out[:]).then_inc(S["st_stored"], 16)

                def keys_copy(n):
                    act.wait_ge(S["kt_turned"], n + 1)
                    if n >= 2:
                        act.wait_ge(S["s_scores"], n // 2)
                    nc.scalar.copy(kT[:, n % 2, 0:2].rearrange("p c n -> p (c n)"), pt[:, 0]).then_inc(S["kt_copied"], 1)

                def probs_copy(m):
                    act.wait_ge(S["ps_turned"], m + 1)
                    if m >= 2:
                        act.wait_ge(S["s_pv"], m - 1)
                    own.inc(nc.scalar.copy(prst[:, m % 2, 0:2, :], pd[:, m % 2, 0:2 * P].rearrange("p (a b) -> p a b", b=P)))
                    own.do(nc.scalar.copy(prst[0:NS, m % 2, 2, :], pd[0:NS, m % 2, 2 * P:3 * P]))
                    act.sem_inc(S["ps_copied"], 1)

                keys_copy(0)
                keys_copy(1)
                for m in range(PAIRS):
                    act.wait_ge(S["s_scaled"], m + 1)
                    if m >= 2:
                        act.wait_ge(S["ps_turned"], m - 1)
                    nc.scalar.activation(prs[:, m % 2, :], scs[:, m % 2, :], ACT.Exp, bias=sml[:, 0, m:m + 1],
                                         accum_out=sml[:, 1, m:m + 1]).then_inc(S["s_probs"], 1)
                    if m + 1 < PAIRS:
                        keys_copy(2 * m + 2)
                    probs_copy(m)
                    if m + 1 < PAIRS:
                        keys_copy(2 * m + 3)
                act.wait_ge(S["osq"], 1)
                nc.scalar.activation(nrm2[:], nrm[:], ACT.Sqrt).then_inc(S["root"], 1)
                act.wait_ge(S["kv_out"], 64)
                act.wait_ge(S["st_stored"], 16)

            @block.vector
            def _(dve):
                own = Own(dve, S["own"])
                V = nc.vector
                dve.wait_ge(S["turns"], 32)
                for t in range(TILES):
                    r = ROWS[t]
                    for part in range(2):
                        qk = z[0:r, t, QR + 512 * part:QR + 512 * (part + 1)].rearrange("p (h n e) -> p h n e", h=H, e=2)
                        xe, xo = qk[:, :, :, 0], qk[:, :, :, 1]
                        f = [rb[0:r, i, 0:256].rearrange("p (h n) -> p h n", h=H) for i in range(4)]
                        co, si = (xpos[0:r, t, i, part].unsqueeze(1).broadcast_to([r, H, 32]) for i in range(2))
                        for i, (a, b) in enumerate(((xe, co), (xo, si), (xo, co), (xe, si))):
                            own.inc(V.tensor_tensor(f[i], a, b, ALU.mult))
                        own.sync()
                        own.inc(V.tensor_tensor(xe, f[0], f[1], ALU.subtract))
                        own.do(V.tensor_tensor(xo, f[2], f[3], ALU.add))
                    dve.sem_inc(S["rotated"], 1)
                own.do(V.memset(big[:], 0.0))
                dve.wait_ge(S["tables"], 16 * 9)

                for u in range(4):
                    t, hg = u // 2, u % 2
                    n_k = P * (t + 1)
                    s4 = ps[:].rearrange("p a (b n) -> p (a b) n", n=256)[:, :, 0:n_k]
                    dve.wait_ge(S["scores"], u + 1)
                    if u:
                        dve.wait_ge(S["probs"], u)
                    own.do(V.scalar_tensor_tensor(out=sc[:, :, 0:n_k], in0=s4, scalar=HD ** -0.5,
                                                  in1=causal[:, t, 0:n_k].unsqueeze(1).broadcast_to([P, 4, n_k]),
                                                  op0=ALU.mult, op1=ALU.add))
                    own.do(V.tensor_reduce(mx[:], sc[:, :, 0:n_k], X, ALU.max))
                    V.tensor_tensor(sc[:, :, 0:n_k], sc[:, :, 0:n_k], mx[:].unsqueeze(2).broadcast_to([P, 4, n_k]),
                                    ALU.subtract).then_inc(S["scaled"], 1)
                    dve.wait_ge(S["probs"], u + 1)
                    own.do(V.tensor_reduce(sm[:], pr[:, :, 0:n_k], X, ALU.add))
                    own.do(V.reciprocal(rs[:], sm[:]))
                    dve.wait_ge(S["pv"], u + 1)
                    V.tensor_tensor(mix[:, t, hg * 256:(hg + 1) * 256].rearrange("p (j b d) -> p j b d", b=2, d=HD),
                                    po[:, 0, 0:256].rearrange("p (j b d) -> p j b d", b=2, d=HD),
                                    rs[:].rearrange("p (b j) -> p j b", b=2).unsqueeze(3).broadcast_to([P, 2, 2, HD]), ALU.mult
                                    ).then_inc(S["mixed"], 1)
                    if u == 0:
                        dve.wait_ge(S["qt_copied"], 12)
                        dve.wait_ge(S["roped"], 3)
                        own.inc(V.tensor_copy(big[:].rearrange("p (n x) -> p n x", x=264)[:, :, 0:256]
                                              .rearrange("p n (c y) -> p n c y", y=64)[:, :, :, 0:DSEQ],
                                              qt[:, 8:12, 256:320].rearrange("p c (n t) -> p n c t", t=DSEQ)))
                        for b in range(2):
                            own.inc(V.tensor_copy(qb[64 * b:64 * b + 64].rearrange("p n (c x) -> p n c x", x=80)
                                                  [:, :, :, b * DSEQ:(b + 1) * DSEQ],
                                                  qt[64 * b:64 * b + 64, 0:4, 256:320].rearrange("p c (n t) -> p n c t", t=DSEQ)))
                        own.sync()
                        dve.sem_inc(S["qm"], 1)
                        dve.sem_inc(S["qb"], 1)

                for n in range(NSEQ):
                    own.inc(V.tensor_tensor(km[:, n * 512:(n + 1) * 512].rearrange("p (h d) -> p h d", h=H),
                                            z[0:NS, 2, KR:VR].rearrange("p (h d) -> p h d", h=H),
                                            dk_s[:, n].unsqueeze(2).broadcast_to([NS, H, DK]), ALU.mult))
                own.sync()
                dve.sem_inc(S["kvm"], 1)
                for t in range(TILES):
                    r = ROWS[t]
                    dve.wait_ge(S["att"], t + 1)
                    if t:
                        dve.wait_ge(S["o_ready"], t)
                    table = (dmat if t < 2 else dmat_s)[:].rearrange("p (a h) n -> p a (h n)", a=2)
                    V.tensor_tensor(att[0:r, 0:H * r].rearrange("p (a n) -> p a n", a=2), ps[0:r, :, 0:4 * r], table, ALU.mult
                                    ).then_inc(S["decayed"], 1)
                    if t < 2:
                        dve.wait_ge(S["state"], t + 1)
                        s_ps = pt[:, 0].rearrange("p (c e) -> p c e", e=DV)
                        if t == 0:
                            own.do(V.tensor_copy(st[:], s_ps))
                            dve.sem_inc(S["st_copied"], 1)
                        else:
                            own.do(V.tensor_tensor(st_out[:], st[:], dc[:, 0].unsqueeze(2).broadcast_to([P, 4, DV]), ALU.mult))
                            own.do(V.tensor_tensor(st_out[:], s_ps, st_out[:], ALU.add))
                            dve.sem_inc(S["st_final"], 1)
                    o_dst = mix[0:r, t, 512:MIX_W]
                    o_ps = po[0:r].rearrange("p a b -> p (a b)")
                    if t == 0:
                        dve.wait_ge(S["o_ready"], 1)
                        V.tensor_copy(o_dst, o_ps).then_inc(S["orr"], 1)
                    else:
                        dve.wait_ge(S["ocross"], t)
                        own.do(V.tensor_tensor(tmp[0:r].rearrange("p (j b e) -> p b j e", b=2, e=DV),
                                               pd[0:r].rearrange("p b (j e) -> p b j e", e=DV),
                                               dq[0:r, t].rearrange("p (j b) -> p b j", b=2).unsqueeze(3)
                                               .broadcast_to([r, 2, 4, DV]), ALU.mult))
                        dve.wait_ge(S["o_ready"], t + 1)
                        V.tensor_tensor(o_dst, o_ps, tmp[0:r], ALU.add).then_inc(S["orr"], 1)
                dve.wait_ge(S["orr"], 3)
                dve.wait_ge(S["states"], 16)
                own.do(V.tensor_tensor(ss[:].rearrange("p n c e -> p n (c e)").rearrange("p n (c e) -> p n c e", e=DV),
                                       ss[:], dc[:, 1].unsqueeze(1).unsqueeze(3).broadcast_to([P, NSEQ, 4, DV]), ALU.mult))
                for n in range(NSEQ):
                    dve.wait_ge(S["state"], n + 3)
                    V.tensor_tensor(ss[:, n].rearrange("p c e -> p (c e)"), pt[:, n % 2, :], ss[:, n].rearrange("p c e -> p (c e)"),
                                    ALU.add).then_inc(S["ss_new"], 1)

                def keys_copy(n):
                    dve.wait_ge(S["kt_turned"], n + 1)
                    if n >= 2:
                        dve.wait_ge(S["s_scores"], n // 2)
                    V.tensor_copy(kT[:, n % 2, 2:4].rearrange("p c n -> p (c n)"), pt[:, 1]).then_inc(S["kt_copied"], 1)

                def softmax_in(m):
                    dve.wait_ge(S["s_scores"], m + 1)
                    if m >= 2:
                        dve.wait_ge(S["s_probs"], m - 1)
                    own.inc(V.tensor_scalar(scs[:, m % 2, 0:256], ps[:, m % 2, 0:256], HD ** -0.5, None, ALU.mult))
                    own.do(V.scalar_tensor_tensor(out=scs[:, m % 2, 256:320], in0=ps[:, m % 2, 256:320], scalar=HD ** -0.5,
                                                  in1=own_mask[:, m, :], op0=ALU.mult, op1=ALU.add))
                    own.do(V.tensor_reduce(sml[:, 2, m:m + 1], scs[:, m % 2, :], X, ALU.max))
                    V.tensor_scalar(sml[:, 0, m:m + 1], sml[:, 2, m:m + 1], -1.0, None, ALU.mult).then_inc(S["s_scaled"], 1)

                def place(m):
                    dve.wait_ge(S["s_pv"], m + 1)
                    own.do(V.reciprocal(sml[:, 2, m:m + 1], sml[:, 1, m:m + 1]))
                    V.scalar_tensor_tensor(out=msk[:, m % 2, :], in0=po[:, m % 2, :], scalar=sml[:, 2, m:m + 1],
                                           in1=heads[:], op0=ALU.mult, op1=ALU.mult).then_inc(S["s_masked"], 1)
                    dve.wait_ge(S["s_masked"], m + 1)
                    V.tensor_reduce(so[:, m, :], msk[:, m % 2, :].rearrange("p (h e) -> p e h", h=H), X, ALU.add
                                    ).then_inc(S["s_out"], 1)

                def squares(t):
                    r = ROWS[t]
                    for half in range(2):
                        o = mix[0:r, t, 512 + 512 * half:1024 + 512 * half]
                        own.do(V.tensor_tensor(sq[0:r, half], o, o, ALU.mult))
                    for half in range(2):
                        own.inc(V.tensor_reduce(nrm2[0:r, t, 4 * half:4 * half + 4],
                                                sq[0:r, half].rearrange("p (h e) -> p h e", e=DV), X, ALU.add))
                    own.sync()
                    dve.sem_inc(S["squared"], 1)

                own.do(V.memset(nrm2[:], 1.0))
                keys_copy(0)
                keys_copy(1)
                for m in range(PAIRS):
                    softmax_in(m)
                    if m < TILES:
                        squares(m)
                    if m + 1 < PAIRS:
                        keys_copy(2 * m + 2)
                        keys_copy(2 * m + 3)
                    else:
                        own.do(V.tensor_scalar(nrm2[:], nrm2[:], 1.0 / DV, EPS, ALU.mult, ALU.add))
                        V.reciprocal(nrm[:], nrm2[:]).then_inc(S["osq"], 1)
                    place(m)
                dve.wait_ge(S["root"], 1)
                for t in range(TILES):
                    r = ROWS[t]
                    dve.wait_ge(S["gated"], t + 1)
                    o = mix[0:r, t, 512:MIX_W].rearrange("p (h e) -> p h e", e=DV)
                    own.inc(V.tensor_tensor(o, o, nrm2[0:r, t].unsqueeze(2).broadcast_to([r, H, DV]), ALU.mult))


def out_proj_phase(k, mix):
    nc = k.nc
    w = k.i["w_out_even"].rearrange("e (p c) n -> p (e c) n", c=KM)
    LOTS = 4
    with k.phase() as ctx:
        wo = k.sb(ctx, "wo", [P, KM, D])
        mixT = k.sb(ctx, "mixT", [P, KM, NTOK])
        pt = k.ps(ctx, "op_pt", [P, 2, 512])
        acc = k.ps(ctx, "op_acc", [P, TILES, 2, 512])
        w_ready = [k.sem(f"wo_ready{n}") for n in range(LOTS)]
        turned, copied, done = k.sem("mix_turned"), k.sem("mix_copied"), k.sem("op_done")
        with nc.Block() as block:
            @block.sync
            def _(sp):
                for n in range(LOTS):
                    s = slice(n * KM // LOTS, (n + 1) * KM // LOTS)
                    sp.dma_start(wo[:, s], w[:, s]).then_inc(w_ready[n], 16)

            @block.tensor
            def _(pe):
                def product(t, c):
                    for half in range(2):
                        out = acc[64 * half:64 * half + 64, 2, 0, :] if t == 2 else acc[:, t, half, :]
                        last = nc.tensor.matmul(out, mixT[:, c, P * t:P * t + ROWS[t]],
                                                wo[:, c, half * 512:(half + 1) * 512], start=c == 0, stop=c == KM - 1)
                    return last

                for m in range(9):
                    t, g = m // 3, m % 3
                    r = ROWS[t]
                    if m >= 2:
                        pe.wait_ge(copied, m - 1)
                    for i in range(4):
                        last = nc.tensor.transpose(pt[:, m % 2, i * P:i * P + r], mix[0:r, t, 4 * g + i:MIX_W:KM],
                                                   k.ident[0:r, 0:r])
                    last.then_inc(turned, 1)
                pe.wait_ge(copied, 9)
                for n in range(LOTS - 1):
                    pe.wait_ge(w_ready[n], 16)
                    for c in range(KM // LOTS * n, KM // LOTS * (n + 1)):
                        for t in range(TILES):
                            product(t, c)
                pe.wait_ge(w_ready[LOTS - 1], 16)
                for t in range(TILES):
                    for c in range(KM // LOTS * (LOTS - 1), KM):
                        last = product(t, c)
                    last.then_inc(done, 1)

            @block.scalar
            def _(act):
                for m in range(9):
                    t, g = m // 3, m % 3
                    act.wait_ge(turned, m + 1)
                    nc.scalar.copy(mixT[:, 4 * g:4 * g + 4, P * t:P * t + ROWS[t]],
                                   pt[:, m % 2].rearrange("p (c n) -> p c n", c=4)[:, :, 0:ROWS[t]]).then_inc(copied, 1)

            @block.vector
            def _(dve):
                for t in range(2):
                    dve.wait_ge(done, t + 1)
                    nc.vector.tensor_tensor(k.h[:, t, :], acc[:, t].rearrange("p a b -> p (a b)"), k.h[:, t, :], ALU.add)
                dve.wait_ge(done, 3)
                for half in range(2):
                    h = k.h[0:NS, 2, half * 512:(half + 1) * 512]
                    nc.vector.tensor_tensor(h, acc[64 * half:64 * half + 64, 2, 0, :], h, ALU.add)


def moe_layer(k, li, rows):
    with k.phase() as mc:
        route = {
            "slot_tok": k.sb(mc, f"slot_tok{li}", [SLOT, NBLK], U32),
            "dest": k.sb(mc, f"dest{li}", [P, TILES, 2], U32),
            "weight": k.sb(mc, f"weight{li}", [P, TILES, 2]),
            "experts": k.sb(mc, f"experts{li}", [1, NBLK], I32),
            "total": k.sb(mc, f"total{li}", [1, 1], I32),
        }
        with k.phase() as wc:
            weights = {
                "w13": [k.sb(wc, f"w13_{li}{b}", [P, KC, 2 * DE]) for b in range(BUFS)],
                "w2": [k.sb(wc, f"w2_{li}{b}", [P, 4, D]) for b in range(BUFS)],
                "w13_ready": [k.sem(f"w13_ready{b}") for b in range(BUFS)],
                "w2_ready": [k.sem(f"w2_ready{b}") for b in range(BUFS)],
            }

            with ExitStack() as xc:
                k.xT = k.sb(xc, f"xT_moe{li}", [P, KC, NTOK])
                xn = k.sb(xc, f"xn_moe{li}", [P, TILES, D])
                stored = k.sem(f"xn_stored{li}")
                r = {
                    "w": k.sb(xc, f"wr{li}", [P, KC, GROUPS + NE]), "bias": k.sb(xc, f"br{li}", [P, GROUPS + NE]),
                    "before": k.sb(xc, f"before{li}", [P, P]), "token": k.sb(xc, f"token{li}", [P, TILES]),
                    "loaded": k.sem(f"router_loaded{li}"),
                }

                def ahead(sp):
                    for dst, src in (
                            (r["w"][:, :, 0:GROUPS], k.i["moe_w_group"][li].rearrange("(p c) n -> p c n", c=KC)),
                            (r["w"][:, :, GROUPS:], k.i["moe_w_expert"][li].rearrange("(p c) n -> p c n", c=KC)),
                            (r["bias"][:, 0:GROUPS], k.i["moe_b_group"][li].partition_broadcast(P)),
                            (r["bias"][:, GROUPS:], k.i["moe_b_expert"][li].partition_broadcast(P)),
                            (r["before"][:], k.c["before"]), (r["token"][:], k.c["token"])):
                        sp.dma_start(dst, src).then_inc(r["loaded"], 16)
                    load_expert(k, li, weights, sp, "w13", 0, 0)

                def behind(sp):
                    load_expert(k, li, weights, sp, "w2", 0, 0)
                    for b in range(1, BUFS):
                        load_expert(k, li, weights, sp, "w13", b, b)
                        load_expert(k, li, weights, sp, "w2", b, b)

                norm_phase(k, f"n2{li}", k.i["norm2"][li], "pc", rows, ahead, (xn, stored), behind)
                routing_phase(k, li, route, r, stored)
            experts_phase(k, li, route, weights)
        combine_phase(k, li, route)


def load_expert(k, li, weights, sp, which, e, b):
    w = k.i["moe_" + which][li].rearrange("e (p c) n -> e p (c n)", p=P)
    sp.dma_start(weights[which][b][:].rearrange("p c n -> p (c n)"), w[bass.ds(e, 1)].rearrange("e p n -> p (e n)")
                 ).then_inc(weights[which + "_ready"][b], 16)


def routing_phase(k, li, route, r, stored):
    nc = k.nc
    V = nc.vector
    NL = GROUPS + NE
    with k.phase() as ctx:
        def sb(name, shape, dt=F32):
            return k.sb(ctx, f"{name}_r{li}", shape, dt)

        w, bias, before, token, loaded = (r[n] for n in "w bias before token loaded".split())
        ones = sb("ones", [P, P])
        count_up = sb("count_up", [P, 64])
        lg = sb("lg", [P, TILES, NL])
        g8 = sb("g8", [P, TILES, 8])
        gmax, gidx = sb("gmax", [P, TILES, 8]), sb("gidx", [P, TILES, 8], U32)
        gf = sb("gf", [P, TILES])
        ge, gs, wg = sb("ge", [P, TILES, GROUPS]), sb("gs", [P, TILES]), sb("wg", [P, TILES])
        goh = sb("goh", [P, TILES, GROUPS])
        leg = sb("leg", [P, TILES, PER, GROUPS])
        le8, emax, eidx = sb("le8", [P, TILES, PER]), sb("emax", [P, TILES, 8]), sb("eidx", [P, TILES, 8], U32)
        ef = sb("ef", [P, TILES, 2])
        dd, ee, w0 = sb("dd", [P, TILES]), sb("ee", [P, TILES]), sb("w0", [P, TILES])
        oh = sb("oh", [P, TILES, 2, NE])
        both = sb("both", [P, TILES, NE])
        cnt, cmp = sb("cnt", [P, NE]), sb("cmp", [P, NE, NTOK // SLOT])
        limits = sb("limits", [P, NTOK // SLOT])
        nblk, incl, first = sb("nblk", [P, NE]), sb("incl", [P, NE]), sb("first", [P, NE])
        rank, blk, sel = sb("rank", [P, TILES, 2]), sb("blk", [P, TILES, 2]), sb("sel", [P, TILES, 2, NE])
        ahead = sb("ahead", [P, TILES, NE])
        q5, q = sb("q5", [P, TILES, 2, 4]), sb("q", [P, TILES, 2])
        slot, destf = sb("slot", [P, TILES, 2]), sb("destf", [P, TILES, 2])
        ohs, ohb = sb("ohs", [P, TILES, 2, SLOT]), sb("ohb", [P, TILES, 2, NBLK])
        bcmp, bexp = sb("bcmp", [1, NBLK, NE]), sb("bexp", [1, NBLK])
        lps = k.ps(ctx, f"lps{li}", [P, TILES, 512])
        cps = k.ps(ctx, f"cps{li}", [P, TILES, 512])
        tps = k.ps(ctx, f"tps{li}", [P, 512])
        aps = k.ps(ctx, f"aps{li}", [P, 512])
        own_s, made = k.sem("r_own"), k.sem("r_made")
        logits, shifted, exps, delta = k.sem("r_logits"), k.sem("r_shifted"), k.sem("r_exps"), k.sem("r_delta")
        chosen, counted, placed, listed = k.sem("r_chosen"), k.sem("r_counted"), k.sem("r_placed"), k.sem("r_listed")
        with nc.Block() as block:
            @block.sync
            def _(sp):
                sp.wait_ge(stored, 16 * TILES)
            @block.gpsimd
            def _(pool):
                nc.gpsimd.iota(count_up[:], pattern=[[1, 64]], base=0, channel_multiplier=0,
                               allow_small_or_imprecise_dtypes=True).then_inc(made, 1)
                nc.gpsimd.iota(limits[:], pattern=[[SLOT, NTOK // SLOT]], base=0, channel_multiplier=0,
                               allow_small_or_imprecise_dtypes=True).then_inc(made, 1)
                nc.gpsimd.memset(ones[:], 1.0).then_inc(made, 1)

            @block.tensor
            def _(pe):
                pe.wait_ge(loaded, 96)
                for t in range(TILES):
                    for c in range(KC):
                        last = nc.tensor.matmul(lps[0:ROWS[t], t, 0:NL], k.xT[:, c, P * t:P * t + ROWS[t]], w[:, c, :],
                                                start=c == 0, stop=c == KC - 1)
                last.then_inc(logits, 1)
                pe.wait_ge(chosen, 1)
                pe.wait_ge(made, 3)
                for t in range(TILES):
                    for s in range(t + 1):
                        r = ROWS[s]
                        lhs = before[0:r, 0:ROWS[t]] if s == t else ones[0:r, 0:ROWS[t]]
                        last = nc.tensor.matmul(cps[0:ROWS[t], t, 0:NE], lhs, both[0:r, s, :], start=s == 0, stop=s == t)
                for s in range(TILES):
                    last = nc.tensor.matmul(aps[:, 0:NE], ones[0:ROWS[s], :], both[0:ROWS[s], s, :], start=s == 0, stop=s == TILES - 1)
                last.then_inc(counted, 1)
                pe.wait_ge(placed, 1)
                for m in range(2 * TILES):
                    t, j = m // 2, m % 2
                    last = nc.tensor.matmul(tps[0:SLOT, 0:NBLK], ohs[0:ROWS[t], t, j, :], ohb[0:ROWS[t], t, j, :],
                                            start=m == 0, stop=m == 2 * TILES - 1)
                last.then_inc(listed, 1)

            @block.scalar
            def _(act):
                act.wait_ge(shifted, 1)
                nc.scalar.activation(ge[:], goh[:], ACT.Exp).then_inc(exps, 1)
                act.wait_ge(delta, 1)
                nc.scalar.activation(ee[:], dd[:], ACT.Exp).then_inc(exps, 1)

            @block.vector
            def _(dve):
                own = Own(dve, own_s)
                own.inc(V.memset(g8[:], NEG))
                own.inc(V.memset(lg[:], 0.0))
                own.do(V.memset(both[:], 0.0))
                dve.wait_ge(loaded, 96)
                dve.wait_ge(made, 3)
                dve.wait_ge(logits, 1)
                for t in range(TILES):
                    own.inc(V.tensor_tensor(lg[0:ROWS[t], t], lps[0:ROWS[t], t, 0:NL], bias[0:ROWS[t]], ALU.add))
                own.sync()
                own.do(V.tensor_copy(g8[:, :, 0:GROUPS], lg[:, :, 0:GROUPS]))
                for t in range(TILES):
                    own.do(V.max(gmax[:, t], g8[:, t]))
                    own.do(V.max_index(gidx[:, t], gmax[:, t], g8[:, t]))
                own.inc(V.tensor_copy(gf[:], gidx[:, :, 0]))
                V.tensor_tensor(goh[:], lg[:, :, 0:GROUPS], gmax[:, :, 0:1].broadcast_to([P, TILES, GROUPS]),
                                ALU.subtract).then_inc(shifted, 1)
                dve.wait_ge(exps, 1)
                own.do(V.tensor_reduce(gs[:], ge[:], X, ALU.add))
                own.do(V.reciprocal(wg[:], gs[:]))
                own.do(V.tensor_tensor(goh[:], count_up[:, 0:GROUPS].unsqueeze(1).broadcast_to([P, TILES, GROUPS]),
                                       gf[:].unsqueeze(2).broadcast_to([P, TILES, GROUPS]), ALU.is_equal))
                for t in range(TILES):
                    own.inc(V.tensor_tensor(leg[:, t], lg[:, t, GROUPS:NL].rearrange("p (g e) -> p e g", g=GROUPS),
                                            goh[:, t].unsqueeze(1).broadcast_to([P, PER, GROUPS]), ALU.mult))
                own.sync()
                own.do(V.tensor_reduce(le8[:], leg[:], X, ALU.add))
                for t in range(TILES):
                    own.do(V.max(emax[:, t], le8[:, t]))
                    own.do(V.max_index(eidx[:, t], emax[:, t], le8[:, t]))
                own.inc(V.tensor_copy(ef[:], eidx[:, :, 0:2]))
                V.tensor_tensor(dd[:], emax[:, :, 1], emax[:, :, 0], ALU.subtract).then_inc(delta, 1)
                own.sync()
                for j in range(2):
                    own.do(V.scalar_tensor_tensor(out=ef[:, :, j], in0=gf[:], scalar=float(PER), in1=ef[:, :, j],
                                                  op0=ALU.mult, op1=ALU.add))
                for t in range(TILES):
                    own.inc(V.tensor_tensor(oh[:, t], count_up[:, 0:NE].unsqueeze(1).broadcast_to([P, 2, NE]),
                                            ef[:, t].unsqueeze(2).broadcast_to([P, 2, NE]), ALU.is_equal))
                own.sync()
                V.tensor_tensor(both[:], oh[:, :, 0, :], oh[:, :, 1, :], ALU.add).then_inc(chosen, 1)
                dve.wait_ge(exps, 2)
                own.do(V.tensor_scalar(w0[:], ee[:], 1.0, None, ALU.add))
                own.do(V.reciprocal(w0[:], w0[:]))
                own.do(V.tensor_tensor(w0[:], w0[:], wg[:], ALU.mult))
                own.inc(V.tensor_copy(route["weight"][:, :, 0], w0[:]))
                own.inc(V.tensor_tensor(route["weight"][:, :, 1], w0[:], ee[:], ALU.mult))
                dve.wait_ge(counted, 1)
                own.do(V.tensor_copy(cnt[:], aps[:, 0:NE]))
                own.do(V.tensor_tensor(cmp[:], cnt[:].unsqueeze(2).broadcast_to([P, NE, NTOK // SLOT]),
                                       limits[:].unsqueeze(1).broadcast_to([P, NE, NTOK // SLOT]), ALU.is_gt))
                own.do(V.tensor_reduce(nblk[:], cmp[:], X, ALU.add))
                own.do(V.tensor_scalar(nblk[:, 0:BUFS], nblk[:, 0:BUFS], -1.0, 0.0, ALU.add, ALU.max))
                own.do(V.tensor_tensor_scan(incl[:], ones[:, 0:NE], nblk[:], 0.0, ALU.mult, ALU.add))
                own.do(V.tensor_tensor(first[:], incl[:], nblk[:], ALU.subtract))
                own.do(V.tensor_scalar(first[:], first[:], float(BUFS), None, ALU.add))
                own.do(V.tensor_scalar(first[:, 0:BUFS], first[:, 0:BUFS], -1.0, None, ALU.add))
                own.do(V.tensor_scalar(bexp[:, 0:1], incl[0:1, NE - 1:NE], float(BUFS), None, ALU.add))
                own.do(V.tensor_copy(route["total"][:], bexp[:, 0:1]))
                own.do(V.tensor_tensor(bcmp[:], incl[0:1].unsqueeze(1).broadcast_to([1, NBLK, NE]),
                                       count_up[0:1, 0:NBLK].unsqueeze(2).broadcast_to([1, NBLK, NE]), ALU.is_le))
                own.do(V.tensor_reduce(bexp[:], bcmp[:], X, ALU.add))
                own.do(V.tensor_scalar(bexp[:], bexp[:], float(NE - 1), None, ALU.min))
                own.inc(V.tensor_copy(route["experts"][:], bexp[:]))
                own.inc(V.memset(ahead[:], 0.0))
                own.sync()
                for t in range(TILES):
                    own.inc(V.tensor_copy(ahead[0:ROWS[t], t], cps[0:ROWS[t], t, 0:NE]))
                own.sync()
                for src, dst in ((ahead, rank), (first, blk)):
                    for t in range(TILES):
                        v = (src[:, t] if src is ahead else src[:]).unsqueeze(1).broadcast_to([P, 2, NE])
                        own.inc(V.tensor_tensor(sel[:, t], oh[:, t], v, ALU.mult))
                    own.sync()
                    own.do(V.tensor_reduce(dst[:], sel[:], X, ALU.add))
                for j in range(2):
                    own.inc(V.tensor_tensor(q5[:, :, j], rank[:, :, j].unsqueeze(2).broadcast_to([P, TILES, 4]),
                                            limits[:, 1:5].unsqueeze(1).broadcast_to([P, TILES, 4]), ALU.is_ge))
                own.sync()
                own.do(V.tensor_reduce(q[:], q5[:], X, ALU.add))
                own.do(V.scalar_tensor_tensor(out=slot[:], in0=q[:], scalar=-float(SLOT), in1=rank[:], op0=ALU.mult, op1=ALU.add))
                own.do(V.tensor_tensor(blk[:], blk[:], q[:], ALU.add))
                own.inc(V.tensor_scalar(sel[:, :, :, 0], ef[:], float(BUFS) - 0.5, None, ALU.is_le))
                own.inc(V.tensor_scalar(sel[:, :, :, 1], q[:], 0.5, None, ALU.is_le))
                own.inc(V.tensor_tensor(sel[:, :, :, 2], ef[:], blk[:], ALU.subtract))
                own.sync()
                own.do(V.tensor_tensor(sel[:, :, :, 0], sel[:, :, :, 0], sel[:, :, :, 1], ALU.mult))
                own.do(V.tensor_tensor(sel[:, :, :, 0], sel[:, :, :, 0], sel[:, :, :, 2], ALU.mult))
                own.do(V.tensor_tensor(blk[:], blk[:], sel[:, :, :, 0], ALU.add))
                own.do(V.scalar_tensor_tensor(out=destf[:], in0=blk[:], scalar=float(SLOT), in1=slot[:], op0=ALU.mult, op1=ALU.add))
                own.inc(V.tensor_copy(route["dest"][:], destf[:]))
                for t in range(TILES):
                    own.inc(V.tensor_tensor(ohs[:, t], count_up[:, 0:SLOT].unsqueeze(1).broadcast_to([P, 2, SLOT]),
                                            slot[:, t].unsqueeze(2).broadcast_to([P, 2, SLOT]), ALU.is_equal))
                    own.inc(V.tensor_tensor(ohb[:, t], count_up[:, 0:NBLK].unsqueeze(1).broadcast_to([P, 2, NBLK]),
                                            blk[:, t].unsqueeze(2).broadcast_to([P, 2, NBLK]), ALU.is_equal))
                own.sync()
                for t in range(TILES):
                    own.inc(V.tensor_scalar(ohb[:, t], ohb[:, t], token[:, t:t + 1], None, ALU.mult))
                own.sync()
                dve.sem_inc(placed, 1)
                dve.wait_ge(listed, 1)
                V.tensor_copy(route["slot_tok"][:], tps[0:SLOT, 0:NBLK])


def experts_phase(k, li, route, weights):
    nc = k.nc
    ROUNDS = NBLK // BUFS
    yblk = k.d["yblk"].rearrange("(b s) d -> b s d", s=SLOT)
    HI = slice(SLOT, 2 * SLOT)
    with k.phase() as ctx:
        def sb(name, shape, dt=F32):
            return k.sb(ctx, f"{name}_e{li}", shape, dt)

        wa, wb = weights["w13"], weights["w2"]
        xg = [sb(f"xg{b}", [SLOT, D]) for b in range(BUFS)]
        idx = [sb(f"idx{b}", [SLOT, 1], U32) for b in range(BUFS)]
        xgT = [sb(f"xgT{b}", [P, KC, SLOT]) for b in range(BUFS)]
        act_g = sb("act_g", [P, DE])
        hid = sb("hid", [P, DE])
        hidT = sb("hidT", [P, 4, SLOT])
        y = [sb(f"y{b}", [P, D // 2]) for b in range(BUFS)]
        xps = k.ps(ctx, f"xps{li}", [P, KC, SLOT])
        gu = [k.ps(ctx, f"gu{li}{b}", [P, DE]) for b in range(BUFS)]
        hps = k.ps(ctx, f"hps{li}", [P, 2, 4 * SLOT])
        yps = [k.ps(ctx, f"yps{li}{b}", [P, D // 2]) for b in range(BUFS)]
        w13_ready, w2_ready = weights["w13_ready"], weights["w2_ready"]
        gathered = k.gathered[li]
        stored = [k.sem(f"y_stored{b}") for b in range(BUFS)]
        w13_used, w2_used, idx_copied = k.sem("w13_used"), k.sem("w2_used"), k.sem("idx_copied")
        passed = k.sem("passed")
        x_turned, x_copied, gate_up = k.sem("x_turned"), k.sem("x_copied"), k.sem("gate_up")
        silu, hidden, h_turned, h_copied = k.sem("silu"), k.sem("hidden"), k.sem("h_turned"), k.sem("h_copied")
        y_copied = k.sem("y_copied")

        def blocks(eng, body):
            total = eng.value_load(route["total"][:], min_val=1, max_val=MAXB)
            with eng.Fori(0, ROUNDS) as i:
                with eng.If(BUFS * i < total):
                    for p in range(BUFS):
                        with eng.If(BUFS * i + p < total):
                            body(i, p, BUFS * i + p)

        with nc.Block() as block:
            @block.sync
            def _(sp):
                total = sp.value_load(route["total"][:], min_val=1, max_val=MAXB)
                with sp.Fori(1, ROUNDS) as i:
                    with sp.If(BUFS * (i - 1) < total):
                        for p in range(BUFS):
                            b = BUFS * i + p
                            with sp.If(b < total):
                                e = sp.value_load(route["experts"][0:1, bass.ds(b - BUFS, 1)], min_val=0, max_val=NE - 1)
                                sp.wait_ge(w13_used, b - BUFS + 1)
                                load_expert(k, li, weights, sp, "w13", e, p)
                                sp.wait_ge(w2_used, b - BUFS + 1)
                                load_expert(k, li, weights, sp, "w2", e, p)
                            with sp.If(b < total + BUFS):
                                sp.wait_ge(y_copied, b - BUFS + 1)
                                for half in range(2):
                                    sp.dma_start(yblk[bass.ds(b - BUFS, 1), :, half * 512:(half + 1) * 512].rearrange("b s d -> s (b d)"),
                                                 y[p][half * SLOT:(half + 1) * SLOT, :]).then_inc(stored[p], 16)
                for p in range(BUFS):
                    sp.wait_ge(stored[p], 32 * ((total + BUFS - 1 - p) // BUFS))
                sp.sem_inc(passed, 1)

            @block.gpsimd
            def _(pool):
                def gather(i, p, b):
                    pool.wait_ge(x_turned, b + 1)
                    nc.gpsimd.tensor_copy(idx[p][:], route["slot_tok"][:, bass.ds(b, 1)]).then_inc(idx_copied, 1)
                    pool.wait_ge(idx_copied, b + 1)
                    pool.sem_inc(passed, 1)
                    nc.gpsimd.indirect_dma_start(xg[p][:], None, k.d["xn"], bass.IndirectOffsetOnAxis(ap=idx[p][:], axis=0)
                                                 ).then_inc(gathered[p], 16)

                blocks(pool, gather)

            @block.tensor
            def _(pe):
                pe.sem_inc(x_turned, BUFS)

                def expert(i, p, b):
                    pe.wait_ge(gathered[p], 16 * i + 16)
                    pe.wait_ge(x_copied, b + 1)
                    pe.sem_inc(passed, 1)
                    for c in range(KC):
                        last = nc.tensor.transpose(xps[:, c, :], xg[p][:, c:D:KC], k.ident[0:SLOT, 0:SLOT])
                    last.then_inc(x_turned, 1)
                    pe.wait_ge(x_copied, b + 2)
                    pe.wait_ge(w13_ready[p], 16 * i + 16)
                    for c in range(KC):
                        for half in range(2):
                            last = nc.tensor.matmul(gu[p][half * SLOT:(half + 1) * SLOT, :], xgT[p][:, c, :],
                                                    wa[p][:, c, half * DE:(half + 1) * DE], start=c == 0, stop=c == KC - 1)
                    last.then_inc(gate_up, 1)
                    pe.wait_ge(gate_up, b + 1)
                    pe.sem_inc(w13_used, 1)
                    pe.wait_ge(hidden, b + 1)
                    pe.sem_inc(passed, 1)
                    for j in range(4):
                        last = nc.tensor.transpose(hps[:, 0, j * SLOT:(j + 1) * SLOT], hid[HI, j:DE:4], k.ident[HI, HI])
                    last.then_inc(h_turned, 1)
                    pe.wait_ge(h_copied, b + 1)
                    pe.wait_ge(w2_ready[p], 16 * i + 16)
                    for j in range(4):
                        for half in range(2):
                            last = nc.tensor.matmul(yps[p][half * SLOT:(half + 1) * SLOT, :], hidT[:, j, :],
                                                    wb[p][:, j, half * 512:(half + 1) * 512], start=j == 0, stop=j == 3)
                    last.then_inc(w2_used, 1)

                blocks(pe, expert)

            @block.scalar
            def _(act):
                def step(i, p, b):
                    act.wait_ge(gate_up, b + 1)
                    nc.scalar.activation(act_g[HI, :], gu[p][0:SLOT, :], ACT.Silu).then_inc(silu, 1)

                blocks(act, step)

            @block.vector
            def _(dve):
                dve.sem_inc(x_copied, 1)

                def step(i, p, b):
                    dve.wait_ge(x_turned, b + BUFS + 1)
                    nc.vector.tensor_copy(xgT[p][:], xps[:]).then_inc(x_copied, 1)
                    dve.wait_ge(silu, b + 1)
                    nc.vector.tensor_tensor(hid[HI, :], gu[p][HI, :], act_g[HI, :], ALU.mult).then_inc(hidden, 1)
                    dve.wait_ge(h_turned, b + 1)
                    nc.vector.tensor_copy(hidT[:].rearrange("p j n -> p (j n)"), hps[:, 0, :]).then_inc(h_copied, 1)
                    dve.wait_ge(w2_used, b + 1)
                    dve.wait_ge(stored[p], 32 * i)
                    nc.vector.tensor_copy(y[p][:], yps[p][:]).then_inc(y_copied, 1)

                blocks(dve, step)


def combine_phase(k, li, route):
    nc = k.nc
    with k.phase() as ctx:
        yg = k.sb(ctx, f"yg{li}", [P, TILES, 2, D])
        got = k.combined
        added = k.sem("yg_added")
        with nc.Block() as block:
            @block.gpsimd
            def _(pool):
                for m in range(2 * TILES):
                    t, j = m // 2, m % 2
                    r = ROWS[t]
                    nc.gpsimd.indirect_dma_start(yg[0:r, t, j, :], None, k.d["yblk"],
                                                 bass.IndirectOffsetOnAxis(ap=route["dest"][0:r, t, j:j + 1], axis=0)
                                                 ).then_inc(got[m], 16)

            @block.vector
            def _(dve):
                for m in range(2 * TILES):
                    t, j = m // 2, m % 2
                    r = ROWS[t]
                    dve.wait_ge(got[m], 16 * (li + 1))
                    if j:
                        dve.wait_ge(added, m)
                    nc.vector.scalar_tensor_tensor(out=k.h[0:r, t, :], in0=yg[0:r, t, j, :], scalar=route["weight"][0:r, t, j:j + 1],
                                                   in1=k.h[0:r, t, :], op0=ALU.mult, op1=ALU.add).then_inc(added, 1)


def s5_layer(k, zT):
    with ExitStack() as sc:
        def sb(name, shape, dt=F32):
            return k.sb(sc, name, shape, dt)

        s = {
            "u": sb("s5_u", [P, G5, NCH]),
            "cs": sb("s5_cs", [P, G5, CH + 1, C5]),
            "fs": sb("s5_fs", [P, 7 * 1024 + 8 * 144]),
            "e": sb("s5_e", [P, G5 * P]),
            "xs": sb("s5_xs", [P, G5, NCH + 1]),
            "pb": sb("s5_pb", [P, 2, C5, G5]),
            "pc": sb("s5_pc", [P, 2, C5, G5]),
            "ar": sb("s5_ar", [P, CH + 1, G5]), "ai": sb("s5_ai", [P, CH + 1, G5]),
            "work": sb("s5_work", [P, 4096]),
            "s0": sb("s5_s0", [P, 2, NSEQ, G5]),
            "d": sb("s5_dcol", [P, KC]),
            "sw": sb("s5_sw", [P, P]),
        }
        s5_prepare_phase(k, s)
        s5_matrices_phase(k, s)
        s5_scan_phase(k, s, zT)


def s5_prepare_phase(k, s):
    nc = k.nc
    V = nc.vector
    with k.phase() as ctx:
        def sb(name, shape, dt=F32):
            return k.sb(ctx, name, shape, dt)

        xc = s["e"][0:NCH, :]
        xg = s["fs"][0:NCH, 0:CH * D]
        raw = s["work"][0:G5, :].rearrange("g (a n) -> g a n", a=4)
        lam, ldt = sb("lam", [G5, 2, S5]), sb("ldt", [P, G5])
        spare = s["cs"][:].rearrange("p g j c -> p (g j c)")
        s0raw = spare[0:G5, 3072:3072 + NSEQ * P].rearrange("g (n a p) -> g n a p", n=NSEQ, a=2)
        names = "lr li dt x ang mag kf a1 a2 sn sh cs den rden nr t1 t2 cor coi ek er eq ep".split()
        e_int = sb("s5_eint", [P, G5], I32)
        v = {n: spare[:, G5 * i:G5 * (i + 1)] for i, n in enumerate(names)}
        pp = spare[:, 2048:2560].rearrange("p (a m g) -> p a m g", a=2, m=4)
        pb = k.ps(ctx, "s5p", [P, 8, 512])
        loaded, chunks, s0_loaded = k.sem("p_loaded"), k.sem("p_chunks"), k.sem("p_s0")
        raws = [k.sem(f"p_raw{i}") for i in range(4)]
        sorted_, turned, copied = k.sem("p_sorted"), k.sem("p_turned"), k.sem("p_copied")
        lam_ps, lam_got, b_ps, c_re_ps, c_im_ps = (k.sem("p_" + n) for n in "lam_ps lam_got b_ps c_re_ps c_im_ps".split())
        own_s, e2, a_ok, b_done, c_done, s0_ps, s0_got = (k.sem("p_" + n) for n in
            "own e2 a_ok b_done c_done s0_ps s0_got".split())
        with nc.Block() as block:
            @block.sync
            def _(sp):
                sp.dma_start(xc, k.d["xn"].rearrange("(q s) d -> q (s d)", s=CH)).then_inc(chunks, 16)
                sp.dma_start(lam[:, 0], k.i["s5_lam_re"][0]).then_inc(loaded, 16)
                sp.dma_start(lam[:, 1], k.i["s5_lam_im"][0]).then_inc(loaded, 16)
                sp.dma_start(ldt[:], k.i["s5_log_dt"][0].partition_broadcast(P)).then_inc(loaded, 16)
                sp.dma_start(s["sw"][:], k.c["swap"]).then_inc(loaded, 16)
                sp.dma_start(s["d"][:], k.i["s5_d"][0].rearrange("(c p) -> p c", p=P), allow_slow_non_contiguous=True
                             ).then_inc(loaded, 16)
                for i, n in enumerate(("s5_b_re", "s5_b_im")):
                    sp.dma_start(raw[:, i], k.i[n][0].rearrange("g p c -> g (p c)")).then_inc(raws[i], 16)
                for i, n in enumerate(("s5_c_re", "s5_c_im")):
                    sp.dma_start(raw[:, 2 + i], k.i[n][0].rearrange("g c p -> g (c p)")).then_inc(raws[2 + i], 16)
                for i, n in enumerate(("state_s5_re", "state_s5_im")):
                    sp.dma_start(s0raw[:, :, i, :], k.i[n][0].rearrange("n g p -> g n p")).then_inc(s0_loaded, 16)

            @block.gpsimd
            def _(pool):
                pool.wait_ge(chunks, 16)
                for i in range(0, CH, 2):
                    nc.gpsimd.tensor_copy(xg.rearrange("q (g s c) -> q g s c", s=CH, c=C5)[:, :, i, :],
                                          xc[:, i * D:(i + 1) * D].rearrange("q (g c) -> q g c", c=C5)).then_inc(sorted_, 1)

            @block.scalar
            def _(act):
                act.wait_ge(a_ok, 1)
                nc.scalar.activation(v["sn"], v["a2"], ACT.Sin).then_inc(e2, 1)
                nc.scalar.activation(v["sh"], v["a2"], ACT.Sin, scale=0.5).then_inc(e2, 1)
                act.wait_ge(chunks, 16)
                for i in range(1, CH, 2):
                    nc.scalar.copy(xg.rearrange("q (g s c) -> q g s c", s=CH, c=C5)[:, :, i, :],
                                   xc[:, i * D:(i + 1) * D].rearrange("q (g c) -> q g c", c=C5)).then_inc(b_done, 1)
                for m in range(8):
                    act.wait_ge(turned, m + 1)
                    nc.scalar.copy(s["u"][:, 8 * m:8 * m + 8, :].rearrange("p g q -> p (g q)"), pb[:, m % 2, 0:8 * NCH]
                                   ).then_inc(copied, 1)
                act.wait_ge(s0_ps, 1)
                nc.scalar.copy(s["s0"][:, 0].rearrange("p n g -> p (n g)"), pb[:, 2, :]).then_inc(s0_got, 1)
                act.wait_ge(s0_ps, 2)
                nc.scalar.copy(s["s0"][:, 1].rearrange("p n g -> p (n g)"), pb[:, 3, :]).then_inc(s0_got, 1)

            @block.tensor
            def _(pe):
                def both_halves(src, stop_bank, col):
                    last = None
                    for half in range(2):
                        last = nc.tensor.matmul(pb[64 * half:64 * half + 64, stop_bank, col:col + G5], src, k.ident[0:G5, 0:G5],
                                                start=True, stop=True)
                    return last

                pe.wait_ge(loaded, 80)
                for i in range(2):
                    last = both_halves(lam[:, i, :], 0, i * G5)
                last.then_inc(lam_ps, 1)
                for i in range(2):
                    pe.wait_ge(raws[i], 16)
                    for c in range(C5):
                        last = both_halves(raw[:, i, c:1024:C5], 2 + 2 * i + c // 8, (c % 8) * G5)
                last.then_inc(b_ps, 1)
                pe.wait_ge(raws[2], 16)
                for c in range(C5):
                    last = both_halves(raw[:, 2, c * S5:(c + 1) * S5], 6 + c // 8, (c % 8) * G5)
                last.then_inc(c_re_ps, 1)
                pe.wait_ge(raws[3], 16)
                pe.wait_ge(lam_got, 1)
                for c in range(C5):
                    last = both_halves(raw[:, 3, c * S5:(c + 1) * S5], c // 8, (c % 8) * G5)
                last.then_inc(c_im_ps, 1)
                pe.wait_ge(c_done, 1)
                pe.wait_ge(sorted_, CH // 2)
                pe.wait_ge(b_done, CH // 2)
                for m in range(8):
                    if m >= 2:
                        pe.wait_ge(copied, m - 1)
                    for i in range(8):
                        g = 8 * m + i
                        last = nc.tensor.transpose(pb[:, m % 2, i * NCH:(i + 1) * NCH], xg[:, g * P:(g + 1) * P], k.ident[0:NCH, 0:NCH])
                    last.then_inc(turned, 1)
                pe.wait_ge(s0_loaded, 32)
                pe.wait_ge(c_done, 2)
                for n in range(NSEQ):
                    last = nc.tensor.transpose(pb[:, 2, n * G5:(n + 1) * G5], s0raw[:, n].rearrange("g a p -> g (a p)"),
                                               k.ident[0:G5, 0:G5])
                last.then_inc(s0_ps, 1)
                pe.wait_ge(s0_got, 1)
                nc.tensor.matmul(pb[:, 3, :], s["sw"][:], s["s0"][:, 0].rearrange("p n g -> p (n g)"), start=True, stop=True
                                 ).then_inc(s0_ps, 1)

            @block.vector
            def _(dve):
                own = Own(dve, own_s)
                tt = V.tensor_tensor

                def st(o, a, scalar, b, op0=ALU.mult, op1=ALU.add):
                    own.do(V.scalar_tensor_tensor(out=v[o], in0=v[a], scalar=scalar, in1=v[b] if b else e_int[:].bitcast(F32),
                                                  op0=op0, op1=op1))

                def do(o, a, b, op):
                    own.do(tt(v[o], v[a], v[b], op))

                def exp(o, x):
                    own.do(V.tensor_scalar(v["ek"], x, 1.0 / np.log(2.0), None, ALU.mult))
                    own.do(V.tensor_scalar(v["ek"], v["ek"], big, None, ALU.add))
                    own.do(V.tensor_scalar(v["ek"], v["ek"], -big, None, ALU.add))
                    own.do(V.tensor_scalar(v["ek"], v["ek"], 127.0, -126.0, ALU.min, ALU.max))
                    own.do(V.scalar_tensor_tensor(out=v["er"], in0=v["ek"], scalar=-0.693359375, in1=x, op0=ALU.mult, op1=ALU.add))
                    st("er", "ek", 2.12194440e-4, "er")
                    own.do(V.tensor_scalar(v["eq"], v["er"], 1.0 / 5040, None, ALU.mult))
                    for f in (720, 120, 24, 6, 2, 1):
                        st("eq", "eq", 1.0 / f, "er", ALU.add, ALU.mult)
                    own.do(V.tensor_scalar(v["ep"], v["ek"], 127.0, None, ALU.add))
                    own.do(V.tensor_copy(e_int[:], v["ep"]))
                    own.do(V.tensor_scalar(e_int[:], e_int[:], 23, None, ALU.logical_shift_left))
                    st(o, "eq", 1.0, None, ALU.add, ALU.mult)

                big = 12582912.0
                dve.wait_ge(loaded, 80)
                exp("dt", ldt[:])
                dve.wait_ge(lam_ps, 1)
                own.inc(V.tensor_copy(v["lr"], pb[:, 0, 0:G5]))
                own.do(V.tensor_copy(v["li"], pb[:, 0, G5:2 * G5]))
                dve.sem_inc(lam_got, 1)
                do("x", "lr", "dt", ALU.mult)
                exp("mag", v["x"])
                do("ang", "li", "dt", ALU.mult)
                own.do(V.tensor_scalar(v["kf"], v["ang"], 1.0 / (2 * np.pi), None, ALU.mult))
                own.do(V.tensor_scalar(v["kf"], v["kf"], big, None, ALU.add))
                own.do(V.tensor_scalar(v["kf"], v["kf"], -big, None, ALU.add))
                st("a1", "kf", -6.28125, "ang")
                st("a2", "kf", -(2 * np.pi - 6.28125), "a1")
                V.tensor_scalar(v["a2"], v["a2"], 3.1415925, -3.1415925, ALU.min, ALU.max).then_inc(a_ok, 1)
                dve.wait_ge(e2, 2)
                do("cs", "sh", "sh", ALU.mult)
                own.do(V.tensor_scalar(v["cs"], v["cs"], -2.0, 1.0, ALU.mult, ALU.add))
                ar, ai = s["ar"], s["ai"]
                own.inc(V.memset(ar[:, 0], 1.0))
                own.inc(V.memset(ai[:, 0], 0.0))
                own.inc(tt(ar[:, 1], v["mag"], v["cs"], ALU.mult))
                own.do(tt(ai[:, 1], v["mag"], v["sn"], ALU.mult))
                for m in (1, 2, 4):
                    r, i = ar[:, 1:1 + m], ai[:, 1:1 + m]
                    br, bi = (a[:, m].unsqueeze(1).broadcast_to([P, m, G5]) for a in (ar, ai))
                    f = [pp[:, j, 0:m] for j in range(2)]
                    own.inc(tt(f[0], r, br, ALU.mult))
                    own.do(tt(f[1], i, bi, ALU.mult))
                    own.do(tt(ar[:, 1 + m:1 + 2 * m], f[0], f[1], ALU.subtract))
                    own.inc(tt(f[0], r, bi, ALU.mult))
                    own.do(tt(f[1], i, br, ALU.mult))
                    own.do(tt(ai[:, 1 + m:1 + 2 * m], f[0], f[1], ALU.add))
                do("t1", "lr", "lr", ALU.mult)
                do("t2", "li", "li", ALU.mult)
                do("den", "t1", "t2", ALU.add)
                own.inc(V.reciprocal(v["rden"], v["den"]))
                own.do(V.tensor_scalar(v["nr"], ar[:, 1], -1.0, None, ALU.add))
                do("t1", "nr", "lr", ALU.mult)
                own.do(tt(v["t2"], ai[:, 1], v["li"], ALU.mult))
                do("t1", "t1", "t2", ALU.add)
                do("cor", "t1", "rden", ALU.mult)
                own.do(tt(v["t1"], ai[:, 1], v["lr"], ALU.mult))
                do("t2", "nr", "li", ALU.mult)
                do("t1", "t1", "t2", ALU.subtract)
                do("coi", "t1", "rden", ALU.mult)
                pc, lo, hi = s["pc"], slice(0, 64), slice(64, 128)
                dve.wait_ge(c_re_ps, 1)
                dve.wait_ge(c_im_ps, 1)
                dve.wait_ge(b_ps, 1)

                def flat(x):
                    return x.rearrange("p c g -> p (c g)")

                def bank(i):
                    return pb[:, i:i + 2, :].rearrange("p a b -> p (a b)")

                own.inc(V.tensor_copy(flat(pc[lo, 0]), bank(6)[lo]))
                own.inc(V.tensor_scalar(flat(pc[hi, 0]), bank(0)[hi], -1.0, None, ALU.mult))
                own.inc(V.tensor_scalar(flat(pc[lo, 1]), bank(0)[lo], -1.0, None, ALU.mult))
                own.do(V.tensor_scalar(flat(pc[hi, 1]), bank(6)[hi], -1.0, None, ALU.mult))
                dve.sem_inc(c_done, 1)
                pbk = s["pb"]
                w = s["work"][:].rearrange("p (a c g) -> p a c g", a=4, c=C5)
                cor, coi = (v[n].unsqueeze(1).broadcast_to([P, C5, G5]) for n in ("cor", "coi"))
                b_re, b_im = (bank(i).rearrange("p (c g) -> p c g", c=C5) for i in (2, 4))
                for j, (a, b) in enumerate(((b_re, cor), (b_im, coi), (b_im, cor), (b_re, coi))):
                    own.inc(tt(w[:, j], a, b, ALU.mult))
                own.sync()
                dve.sem_inc(c_done, 1)
                own.inc(tt(pbk[lo, 0], w[lo, 0], w[lo, 1], ALU.subtract))
                own.inc(tt(pbk[hi, 0], w[hi, 2], w[hi, 3], ALU.add))
                own.inc(tt(pbk[hi, 1], w[hi, 0], w[hi, 1], ALU.subtract))
                own.do(tt(pbk[lo, 1], w[lo, 2], w[lo, 3], ALU.add))
                own.do(V.tensor_scalar(pbk[lo, 1], pbk[lo, 1], -1.0, None, ALU.mult))


def s5_matrices_phase(k, s):
    nc = k.nc
    V, G = nc.vector, nc.gpsimd
    with k.phase() as ctx:
        fs = s["fs"][:, 0:G5 * P].rearrange("p (g s c) -> p g s c", s=CH, c=C5)
        prod = s["work"][:].rearrange("p (a c g) -> p a c g", a=4, c=C5)
        cc = s["work"][:, 0:G5 * NCH]
        pt = k.ps(ctx, "s5m_pt", [P, 2, 512])
        pc = k.ps(ctx, "s5m_pc", [P, 6, 512])
        own_s, pool_s, made, cs_made = (k.sem("m_" + n) for n in "own pool made cs_made".split())
        turned, copied, contrib, taken = (k.sem("m_" + n) for n in "turned copied contrib taken".split())

        def power(eng, own, out, base, j, buf):
            t = [prod[:, buf + i] for i in range(2)]
            for i, a in enumerate((s["ar"], s["ai"])):
                own.inc(eng.tensor_tensor(t[i], base[:, i], a[:, j].unsqueeze(1).broadcast_to([P, C5, G5]), ALU.mult))
            own.sync()
            own.do(eng.tensor_tensor(out, t[0], t[1], ALU.add))

        with nc.Block() as block:
            @block.gpsimd
            def _(pool):
                own = Own(pool, pool_s)
                for i in range(4):
                    power(G, own, fs[:, :, i, :].rearrange("p g c -> p c g"), s["pb"], CH - 1 - i, 0)
                pool.sem_inc(made, 1)

            @block.vector
            def _(dve):
                own = Own(dve, own_s)
                for i in range(4, CH):
                    power(V, own, fs[:, :, i, :].rearrange("p g c -> p c g"), s["pb"], CH - 1 - i, 2)
                dve.sem_inc(made, 1)
                for j in range(CH + 1):
                    power(V, own, s["cs"][:, :, j, :].rearrange("p g c -> p c g"), s["pc"], j, 2)
                dve.sem_inc(cs_made, 1)

            @block.tensor
            def _(pe):
                pe.wait_ge(made, 2)
                for m in range(16):
                    if m >= 2:
                        pe.wait_ge(copied, m - 1)
                    for i in range(4):
                        g = 4 * m + i
                        last = nc.tensor.transpose(pt[:, m % 2, i * P:(i + 1) * P], s["fs"][:, g * P:(g + 1) * P], k.ident[:])
                    last.then_inc(turned, 1)
                pe.wait_ge(copied, 16)
                for g in range(G5):
                    last = nc.tensor.matmul(pc[:, g // 12, (g % 12) * NCH:(g % 12 + 1) * NCH], s["e"][:, g * P:(g + 1) * P],
                                            s["u"][:, g, :], start=True, stop=True)
                last.then_inc(contrib, 1)

            @block.scalar
            def _(act):
                for m in range(16):
                    act.wait_ge(turned, m + 1)
                    nc.scalar.copy(s["e"][:, 512 * m:512 * (m + 1)], pt[:, m % 2, :]).then_inc(copied, 1)
                act.wait_ge(contrib, 1)
                act.wait_ge(cs_made, 1)
                for b in range(6):
                    n = min(12, G5 - 12 * b)
                    nc.scalar.copy(cc[:, b * 12 * NCH:(b * 12 + n) * NCH], pc[:, b, 0:n * NCH])


def s5_scan_phase(k, s, zT):
    nc = k.nc
    V = nc.vector
    NC2 = G5 * NCH
    with k.phase() as ctx:
        def sb(name, shape, dt=F32):
            return k.sb(ctx, name, shape, dt)

        cc = s["work"][:, 0:NC2].rearrange("p (g q) -> p g q", q=NCH)
        icc = s["u"][:].rearrange("p g q -> p (g q)")
        icv = icc.rearrange("p (g q) -> p g q", q=NCH)
        pad = s["fs"]
        kk = s["e"][:].rearrange("p (t j n) -> p t j n", t=KC, j=CH)
        yc = s["fs"][0:NCH, 0:CH * D]
        v3 = sb("s5_v3", [P, 2, 3, G5])
        t1, t2, t3 = sb("s5_t1", [P, 2, G5]), sb("s5_t2", [P, 2, G5]), sb("s5_t3", [P, 2, G5])
        ai2 = sb("s5_ai2", [P, 2, G5])
        fin = sb("s5_fin", [P, NSEQ + 1, G5])
        fout = s["work"][0:G5, 2560:2560 + (NSEQ + 1) * P].rearrange("g (n p) -> g n p", p=P)
        f1 = sb("s5_f1", [P, NSEQ, G5])
        yt = sb("s5_yt", [P, 2, NTOK])
        ps_b = k.ps(ctx, "s5s_b", [P, 8, 512])
        swapped, icc_ok, padded, kk_ps, kk_ok = (k.sem("q_" + n) for n in "swapped icc_ok padded kk_ps kk_ok".split())
        zeroed, own_s, state, saved, xs_ok = (k.sem("q_" + n) for n in "zeroed own state saved xs_ok".split())
        cross, cross_ok, y_ps, y_ok, gelu_ok = (k.sem("q_" + n) for n in "cross cross_ok y_ps y_ok gelu_ok".split())
        fin_ok, fin_ps, fout_ok, out_s, act_s = (k.sem("q_" + n) for n in "fin_ok fin_ps fout_ok out act".split())
        with nc.Block() as block:
            @block.gpsimd
            def _(pool):
                G = nc.gpsimd
                G.memset(pad[:], 0.0).then_inc(zeroed, 1)
                pool.wait_ge(zeroed, 1)
                for t in range(KC):
                    G.tensor_copy(pad[:, 1024 * t:1024 * t + 8 * 144].rearrange("p (i x) -> p i x", x=144)[:, :, 0:C5],
                                  s["pb"][:, 0, :, 8 * t:8 * t + 8].rearrange("p c g -> p g c")).then_inc(padded, 1)

            @block.tensor
            def _(pe):
                for b in range(5):
                    nc.tensor.matmul(ps_b[:, b, :], s["sw"][:], s["work"][:, 512 * b:512 * (b + 1)], start=True, stop=True
                                     ).then_inc(swapped, 1)
                pe.wait_ge(padded, KC)
                pe.wait_ge(icc_ok, 5)
                for t in range(KC):
                    if t >= 2:
                        pe.wait_ge(kk_ok, t - 1)
                    for i in range(8):
                        g = 8 * t + i
                        for half in range(2):
                            out = ps_b[:, 2 * (t % 2) + half, :].rearrange("p (j n) -> p j n", j=4)[:, :, C5 * i:C5 * (i + 1)]
                            last = nc.tensor.matmul(out, pad[:, g * P:(g + 1) * P], s["cs"][:, g, 4 * half:4 * half + 4, :],
                                                    start=True, stop=True)
                    last.then_inc(kk_ps, 1)
                pe.wait_ge(xs_ok, 1)
                for m in range(16):
                    if m >= 4:
                        pe.wait_ge(cross_ok, m - 3)
                    for i in range(4):
                        g = 4 * m + i
                        last = nc.tensor.matmul(ps_b[0:NCH, 4 + m % 4, i * P:(i + 1) * P], s["xs"][:, g, 0:NCH],
                                                s["cs"][:, g, 1:CH + 1, :].rearrange("p s c -> p (s c)"), start=True, stop=True)
                    last.then_inc(cross, 1)
                pe.wait_ge(cross_ok, 16)
                pe.wait_ge(kk_ok, KC)
                for t in range(KC):
                    if t >= 2:
                        pe.wait_ge(y_ok, t - 1)
                    y = ps_b[:, t % 2, 0:NTOK].rearrange("p (q s) -> p q s", s=CH)
                    u = k.xT[:, t, :].rearrange("p (q s) -> p q s", s=CH)
                    for j in range(CH):
                        nc.tensor.matmul(y[:, :, j:CH], kk[:, t, j, :], u[:, :, 0:CH - j], start=j == 0, stop=False)
                    for i in range(CH):
                        last = nc.tensor.matmul(y[:, :, i], yc[:, i * D + t * P:i * D + (t + 1) * P], k.ident[0:NCH, 0:NCH],
                                                start=False, stop=i == CH - 1)
                    last.then_inc(y_ps, 1)
                pe.wait_ge(fin_ok, 1)
                for n in range(NSEQ + 1):
                    last = nc.tensor.transpose(ps_b[0:G5, 4 + n // 4, (n % 4) * P:(n % 4 + 1) * P], fin[:, n, :], k.ident[:])
                last.then_inc(fin_ps, 1)

            @block.scalar
            def _(act):
                S = nc.scalar
                for b in range(5):
                    act.wait_ge(swapped, b + 1)
                    S.copy(icc[:, 512 * b:512 * (b + 1)], ps_b[:, b, :]).then_inc(icc_ok, 1)
                for t in range(KC):
                    act.wait_ge(kk_ps, t + 1)
                    S.copy(kk[:, t].rearrange("p j n -> p (j n)"), ps_b[:, 2 * (t % 2):2 * (t % 2) + 2, :].rearrange("p a b -> p (a b)")
                           ).then_inc(kk_ok, 1)
                for m in range(16):
                    act.wait_ge(cross, m + 1)
                    S.copy(yc.rearrange("q (s g c) -> q g s c", s=CH, c=C5)[:, 4 * m:4 * m + 4],
                           ps_b[0:NCH, 4 + m % 4, :].rearrange("q (g s c) -> q g s c", g=4, c=C5)).then_inc(cross_ok, 1)
                for t in range(KC):
                    act.wait_ge(y_ok, t + 1)
                    S.activation(zT[:, t, :], yt[:, t % 2, :], ACT.Gelu_apprx_tanh).then_inc(gelu_ok, 1)
                act.wait_ge(fin_ps, 1)
                S.copy(fout.rearrange("g n p -> g (n p)"), ps_b[0:G5, 4:7, :].rearrange("g a b -> g (a b)")[:, 0:(NSEQ + 1) * P]
                       ).then_inc(fout_ok, 1)
                act.wait_ge(fout_ok, 1)
                for i, n in enumerate(("re", "im")):
                    act.dma_start(k.o[f"s5_{n}_prompt"][0, 0], fout[:, 0, i * S5:(i + 1) * S5]).then_inc(out_s, 16)
                    act.dma_start(k.o[f"s5_{n}_sample"][0].rearrange("n g p -> g n p"), fout[:, 1:, i * S5:(i + 1) * S5]
                                  ).then_inc(out_s, 16)
                act.wait_ge(out_s, 64)

            @block.vector
            def _(dve):
                own = Own(dve, own_s)
                tt = V.tensor_tensor
                ar8 = s["ar"][:, CH]
                ar2 = ar8.unsqueeze(1).broadcast_to([P, 2, G5])
                own.inc(V.memset(v3[:, 0], 0.0))
                own.inc(V.tensor_copy(ai2[:, 0], s["ai"][:, CH]))
                own.inc(V.tensor_scalar(ai2[:, 1], s["ai"][:, CH], -1.0, None, ALU.mult))
                own.inc(V.memset(s["xs"][:, :, 0], 0.0))
                own.inc(V.tensor_copy(s["xs"][:, :, PCH:NCH].rearrange("p g n -> p n g"), s["s0"][:, 0]))
                own.sync()
                dve.wait_ge(icc_ok, 5)
                for q in range(PCH):
                    a, b = v3[:, q % 2], v3[:, (q + 1) % 2]
                    own.inc(tt(t1[:], a[:, 0:2], ar2, ALU.mult))
                    own.do(tt(t2[:], a[:, 1:3], ai2[:], ALU.mult))
                    own.inc(tt(t1[:, 0], t1[:, 0], cc[:, :, q], ALU.add))
                    own.do(tt(t1[:, 1], t1[:, 1], icv[:, :, q], ALU.add))
                    own.inc(tt(b[:, 0:2], t1[:], t2[:], ALU.add))
                    own.inc(tt(b[:, 2], t1[:, 0], t2[:, 0], ALU.add))
                    dst = s["xs"][:, :, q + 1] if q + 1 < PCH else fin[:, 0]
                    own.do(tt(dst, t1[:, 0], t2[:, 0], ALU.add))
                dve.sem_inc(xs_ok, 1)
                ai8 = s["ai"][:, CH]
                own.inc(tt(f1[:], s["s0"][:, 0], ar8.unsqueeze(1).broadcast_to([P, NSEQ, G5]), ALU.mult))
                own.do(tt(fin[:, 1:], s["s0"][:, 1], ai8.unsqueeze(1).broadcast_to([P, NSEQ, G5]), ALU.mult))
                own.do(tt(f1[:], f1[:], fin[:, 1:], ALU.add))
                own.do(tt(fin[:, 1:], f1[:], cc[:, :, PCH:NCH].rearrange("p g n -> p n g"), ALU.add))
                dve.sem_inc(fin_ok, 1)
                for t in range(KC):
                    dve.wait_ge(y_ps, t + 1)
                    if t >= 2:
                        dve.wait_ge(gelu_ok, t - 1)
                    V.scalar_tensor_tensor(out=yt[:, t % 2, :], in0=k.xT[:, t, :], scalar=s["d"][:, t:t + 1],
                                           in1=ps_b[:, t % 2, 0:NTOK], op0=ALU.mult, op1=ALU.add).then_inc(y_ok, 1)


def glu_phase(k, zT):
    nc = k.nc
    V = nc.vector
    w = k.i["s5_w_glu"][0].rearrange("(c p) n -> p c n", p=P)
    with k.phase() as ctx:
        wg = k.sb(ctx, "wg", [P, KC, 2 * D])
        bias = k.sb(ctx, "bglu", [P, 2 * D])
        a = k.sb(ctx, "glu_a", [P, 2, 512])
        b = k.sb(ctx, "glu_b", [P, 2, 512])
        acc = k.ps(ctx, "glu_ps", [P, 4, 2, 512])
        ready = [k.sem(f"glu_w{n}") for n in range(4)]
        bias_in, done, linear, sig, own_s = (k.sem("glu_" + n) for n in "bias done linear sig own".split())
        units = [(t, half) for half in range(2) for t in range(TILES)]
        with nc.Block() as block:
            @block.sync
            def _(sp):
                for n, col in enumerate((0, 1024, 512, 1536)):
                    sp.dma_start(wg[:, :, col:col + 512], w[:, :, col:col + 512]).then_inc(ready[n], 16)
                sp.dma_start(bias[:], k.i["s5_b_glu"][0].partition_broadcast(P)).then_inc(bias_in, 16)

            @block.tensor
            def _(pe):
                for m, (t, half) in enumerate(units):
                    if m >= 4:
                        pe.wait_ge(linear, m - 3)
                    for part in range(2):
                        pe.wait_ge(ready[2 * half + part], 16)
                        col = part * D + half * 512
                        if t == 2:
                            continue
                        for c in range(KC):
                            last = nc.tensor.matmul(acc[:, m % 4, part, :], zT[:, c, P * t:P * (t + 1)],
                                                    wg[:, c, col:col + 512], start=c == 0, stop=c == KC - 1)
                    if t == 2:
                        for c in range(KC):
                            for part in range(2):
                                col = part * D + half * 512
                                last = nc.tensor.matmul(acc[64 * part:64 * part + 64, m % 4, 0, :], zT[:, c, 256:320],
                                                        wg[:, c, col:col + 512], start=c == 0, stop=c == KC - 1)
                    last.then_inc(done, 1)

            @block.scalar
            def _(act):
                for m, (t, half) in enumerate(units):
                    act.wait_ge(linear, m + 1)
                    nc.scalar.activation(b[0:ROWS[t], m % 2, :], b[0:ROWS[t], m % 2, :], ACT.Sigmoid).then_inc(sig, 1)

            @block.vector
            def _(dve):
                own = Own(dve, own_s)
                dve.wait_ge(bias_in, 16)

                def gate(m):
                    t, half = units[m]
                    r = ROWS[t]
                    dve.wait_ge(sig, m + 1)
                    own.do(V.tensor_tensor(a[0:r, m % 2], a[0:r, m % 2], b[0:r, m % 2], ALU.mult))
                    h = k.h[0:r, t, half * 512:(half + 1) * 512]
                    own.do(V.tensor_tensor(h, h, a[0:r, m % 2], ALU.add))

                for m, (t, half) in enumerate(units):
                    r = ROWS[t]
                    dve.wait_ge(done, m + 1)
                    own.do(V.tensor_tensor(a[0:r, m % 2], acc[0:r, m % 4, 0], bias[0:r, half * 512:(half + 1) * 512], ALU.add))
                    b_ps = acc[64:128, m % 4, 0] if t == 2 else acc[0:r, m % 4, 1]
                    V.tensor_tensor(b[0:r, m % 2], b_ps, bias[0:r, D + half * 512:D + (half + 1) * 512],
                                    ALU.add).then_inc(linear, 1)
                    if m:
                        gate(m - 1)
                gate(len(units) - 1)


def final_norm(k):
    yp = k.o["y_prompt"].rearrange("b (t p) d -> t p (b d)", p=P)
    norm_phase(k, "nf", k.i["norm_f"], None, [yp[0], yp[1], k.o["y_sample"].rearrange("n t d -> (n t) d")])


def program(nc, ins, outs, consts, scratch):
    k = Core(nc, ins, outs, consts, scratch)
    with ExitStack() as ctx:
        k.software_dma_semaphores(ctx)
        k.h = k.sb(ctx, "h", [P, TILES, D])
        k.ident = k.sb(ctx, "ident", [P, P])
        rows = [scratch["xn"][P * t:P * t + ROWS[t], :] for t in range(TILES)]
        with ExitStack() as zc:
            z = k.sb(zc, "z", [P, TILES, IN_W])
            with ExitStack() as xc:
                k.xT = k.sb(xc, "xT0", [P, KC, NTOK])
                in_proj_phases(k, z, ins["norm1"][0])
            mix = k.sb(zc, "mix", [P, TILES, MIX_W])
            even_mixer_phase(k, z, mix)
            out_proj_phase(k, mix)
        moe_layer(k, 0, rows)
        with ExitStack() as zc:
            zT = k.sb(zc, "zT", [P, KC, NTOK])
            with ExitStack() as xc:
                k.xT = k.sb(xc, "xT1", [P, KC, NTOK])
                norm_phase(k, "n11", ins["norm1"][1], "cp", rows)
                s5_layer(k, zT)
            glu_phase(k, zT)
        moe_layer(k, 1, rows)
        final_norm(k)


INPUTS = ("x_prompt", "x_sample", "cache_k", "cache_v", "state_ret", "state_s5_re", "state_s5_im", "page_table",
          "norm1", "norm2", "norm_f", "w_in_even", "w_out_even", "s5_lam_re", "s5_lam_im", "s5_log_dt", "s5_b_re",
          "s5_b_im", "s5_c_re", "s5_c_im", "s5_d", "s5_w_glu", "s5_b_glu", "moe_w_group", "moe_b_group",
          "moe_w_expert", "moe_b_expert", "moe_w13", "moe_w2")
OUTPUTS = (("y_prompt", (1, 256, D)), ("y_sample", (NSEQ, DSEQ, D)),
           ("k_prompt", (1, 1, 2, PAGE, H, HD)), ("v_prompt", (1, 1, 2, PAGE, H, HD)),
           ("k_sample", (1, NSEQ, DSEQ, H, HD)), ("v_sample", (1, NSEQ, DSEQ, H, HD)),
           ("ret_prompt", (1, 1, H, DK, DV)), ("ret_sample", (1, NSEQ, H, DK, DV)),
           ("s5_re_prompt", (1, 1, G5, S5)), ("s5_im_prompt", (1, 1, G5, S5)),
           ("s5_re_sample", (1, NSEQ, G5, S5)), ("s5_im_sample", (1, NSEQ, G5, S5)))
SCRATCH = (("xn", (NTOK, D)), ("smix", (NSEQ // 2, P, HD)), ("yblk", ((NBLK - BUFS) * SLOT, D)))


def kernel(**inputs):
    from concourse import bacc
    from concourse.bass_utils import run_bass_kernel_spmd

    nc = bacc.Bacc("TRN2", target_bir_lowering=False, num_devices=1)
    arrays, ins, consts = {}, {}, {}
    for name in INPUTS:
        a = np.ascontiguousarray(inputs[name])
        arrays["in_" + name] = a
        ins[name] = nc.dram_tensor("in_" + name, a.shape, mybir.dt.from_np(a.dtype), kind="ExternalInput").ap()
    for name, a in constants().items():
        arrays["table_" + name] = np.ascontiguousarray(a)
        consts[name] = nc.dram_tensor("table_" + name, a.shape, F32, kind="ExternalInput").ap()
    outs = {n: nc.dram_tensor("out_" + n, s, F32, kind="ExternalOutput").ap() for n, s in OUTPUTS}
    scratch = {n: nc.dram_tensor("scratch_" + n, s, F32).ap() for n, s in SCRATCH}
    program(nc, ins, outs, consts, scratch)
    r = run_bass_kernel_spmd(nc, [arrays], core_ids=[0])
    return tuple(r.results[0]["out_" + n] for n, _ in OUTPUTS)
```

```python
from contextlib import ExitStack, contextmanager

import concourse.bass as bass
import numpy as np
from concourse import mybir

F32 = mybir.dt.float32
I32 = mybir.dt.int32
U32 = mybir.dt.uint32
ALU = mybir.AluOpType
ACT = mybir.ActivationFunctionType
X = mybir.AxisListType.X

P = 128
D = 1024
KC = D // P
TILES = 3
ROWS = (128, 128, 64)
NTOK = sum(ROWS)
NSEQ, DSEQ = 8, 8
NS = NSEQ * DSEQ
H, HD = 8, 64
ROT = 8
DK, DV = 64, 128
PAGE = 128
IN_W = 4608
MIX_W = 1536
KM = MIX_W // P
QA, KA, VA, QR, KR, VR, GR = 0, 512, 1024, 1536, 2048, 2560, 3584
NEG = -1e30
EPS = 1e-6
GROUPS, PER, NE = 4, 8, 32
DE = 512
SLOT = 32
MAXB = NE + (2 * NTOK - NE) // SLOT
MINB = 2 * NTOK // SLOT
BUFS = 3
NBLK = -(-(MAXB + BUFS) // BUFS) * BUFS
G5, C5, S5 = 64, 16, 64
CH = 8
NCH = NTOK // CH
PCH = 256 // CH


def constants():
    f = np.float32
    pos = np.concatenate([np.arange(256), 256 + np.arange(NS) % DSEQ]).astype(f)
    out = {}

    def tiles(a):
        b = np.zeros((P, TILES) + a.shape[1:], f)
        b[:, 0], b[:, 1], b[:NS, 2] = a[:128], a[128:256], a[256:]
        return b

    inv = (f(500000.0) ** (-np.arange(ROT, dtype=f) / f(ROT))).astype(f)
    ang = pos[:, None] * inv[None]
    out["rope"] = tiles(np.stack([np.cos(ang), np.sin(ang)], 1).astype(f))
    inv = (f(1.0) / (f(10000.0) ** np.linspace(0.0, 1.0, DK // 2, dtype=f))).astype(f)
    ang = pos[:, None] * inv[None]
    cs = np.stack([np.cos(ang), np.sin(ang)], 1).astype(f)
    out["xpos"] = tiles(np.stack([cs, cs * f(DK ** -0.5)], 2))
    lg = np.log(f(1.0) - f(2.0) ** (f(-5.0) - np.arange(H, dtype=f))).astype(f)

    def decay(c):
        i = np.arange(c, dtype=f)
        diff = i[None, :] - i[:, None]
        return np.where(diff[:, None] >= 0, np.exp(np.maximum(diff, 0)[:, None] * lg[None, :, None]), 0).astype(f)

    order = [0, 2, 4, 6, 1, 3, 5, 7]
    out["dmat"] = decay(128)[:, order]
    same = (np.arange(NS)[:, None] // DSEQ == np.arange(NS)[None] // DSEQ)
    small = decay(DSEQ)
    i = np.arange(NS) % DSEQ
    out["dmat_s"] = (small[i][:, :, i] * same[:, None])[:, order].astype(f)
    i = np.concatenate([np.arange(256) % 128, np.arange(NS) % DSEQ]).astype(f)
    out["dq"] = tiles(np.exp((i + 1)[:, None] * lg[None]).astype(f))
    j = np.arange(128, dtype=f)
    out["dk"] = np.exp((127 - j)[:, None] * lg[None]).astype(f)
    j = (np.arange(NS) % DSEQ).astype(f)
    dks = np.exp((DSEQ - 1 - j)[:, None] * lg[None]).astype(f)
    seq = (np.arange(NS)[:, None] // DSEQ == np.arange(NSEQ)[None]).astype(f)
    out["dk_s"] = (dks[:, None, :] * seq[:, :, None]).astype(f)
    head = 2 * np.arange(4)[None] + np.arange(P)[:, None] // 64
    out["dc"] = np.stack([np.exp(f(128) * lg)[head], np.exp(f(DSEQ) * lg)[head]], 1).astype(f)
    q, k = np.arange(128)[:, None], np.arange(256)[None]
    out["causal"] = np.stack([np.where(k <= q, 0, NEG), np.where(k <= q + 128, 0, NEG)], 1).astype(f)
    t = np.arange(NS)[:, None, None] % DSEQ
    n, kk = np.arange(NSEQ)[None, :, None], np.arange(NS)[None, None]
    own = np.where((kk // DSEQ == n) & (kk % DSEQ <= t), 0, NEG).astype(f)
    out["own"] = own.reshape(NS, NSEQ // 2, 2, NS).transpose(2, 0, 1, 3).reshape(P, NSEQ // 2, NS)
    out["ident"] = np.eye(P, dtype=f)
    out["before"] = np.triu(np.ones((P, P), f), 1)
    sw = np.zeros((P, P), f)
    for p in range(S5):
        sw[S5 + p, p], sw[p, S5 + p] = -1, 1
    out["swap"] = sw
    tok = np.arange(P, dtype=f)[:, None] + 128 * np.arange(TILES, dtype=f)[None]
    out["token"] = tok.astype(f)
    out["heads"] = np.broadcast_to((np.arange(P)[:, None] % NS // DSEQ == np.arange(H)[None])[:, :, None],
                                   (P, H, HD)).astype(f)
    return out


class Own:

    def __init__(self, eng, sem):
        self.eng, self.sem, self.n = eng, sem, 0

    def inc(self, ins):
        ins.then_inc(self.sem, 1)
        self.n += 1

    def sync(self):
        self.eng.wait_ge(self.sem, self.n)

    def do(self, ins):
        self.inc(ins)
        self.sync()


class Core:

    def __init__(self, nc, ins, outs, consts, scratch):
        self.nc, self.i, self.o, self.c, self.d = nc, ins, outs, consts, scratch
        self.h = self.ident = self.xT = None
        self.nest, self.ctx, self.dirty = [], [], []

    def lasting_semaphores(self, ctx):
        def sem(name):
            return ctx.enter_context(self.nc.semaphore(name))

        self.cleared = sem("yblk_cleared")
        self.gathered = [[sem(f"gathered{li}{b}") for b in range(BUFS)] for li in range(2)]
        self.combined = [sem(f"yg_got{m}") for m in range(2 * TILES)]
        self.w13_ready = [[sem(f"w13_ready{li}{b}") for b in range(BUFS)] for li in range(2)]
        self.w2_ready = [[sem(f"w2_ready{li}{b}") for b in range(BUFS)] for li in range(2)]

    @contextmanager
    def phase(self):
        self.nest.append([])
        with ExitStack() as ctx:
            self.ctx.append(ctx)
            yield ctx
            self.ctx.pop()
        self.dirty += self.nest.pop()

    def clear(self):
        runs = []
        for n in sorted(self.dirty):
            if runs and n == runs[-1][1] + 1:
                runs[-1][1] = n
            else:
                runs.append([n, n])
        self.dirty = []
        with self.nc.Block() as block:
            @block.gpsimd
            def _(pool):
                for lo, hi in runs:
                    pool.sem_clear(range(lo, hi + 1))

    def sem(self, name):
        s = self.ctx[-1].enter_context(self.nc.semaphore(name))
        assert s.num not in self.dirty, "too few clean semaphores"
        self.nest[-1].append(s.num)
        return s

    def sb(self, ctx, name, shape, dt=F32):
        return ctx.enter_context(self.nc.sbuf_tensor(name, shape, dt))

    def ps(self, ctx, name, shape):
        return ctx.enter_context(self.nc.psum_tensor(name, shape, F32))


def norm_phase(k, tag, gain, chunks, store, ahead=None, later=None, behind=None, gain_at=None, combine=None):
    nc = k.nc
    with k.phase() as ctx:
        xn = later[0] if later else k.sb(ctx, f"xn_{tag}", [P, TILES, D])
        g = gain_at if gain_at is not None else k.sb(ctx, f"gain_{tag}", [P, D])
        ss = k.sb(ctx, f"ss_{tag}", [P, 4])
        ms = k.sb(ctx, f"ms_{tag}", [P, 4])
        rstd = k.sb(ctx, f"rstd_{tag}", [P, 4])
        turned_ps = k.ps(ctx, f"turned_ps_{tag}", [P, TILES, D])
        loaded, squares, cleared = k.sem(f"loaded_{tag}"), k.sem(f"squares_{tag}"), k.sem(f"cleared_{tag}")
        own, inv, root = k.sem(f"own_{tag}"), k.sem(f"inv_{tag}"), k.sem(f"root_{tag}")
        normed, turned = k.sem(f"normed_{tag}"), k.sem(f"turned_{tag}")
        stored = later[1] if later else k.sem(f"stored_{tag}")
        first = tag == "n10"
        added, warm = k.sem(f"added_{tag}"), k.sem(f"warm_{tag}")
        if first:
            s_h, s_ident = [k.sem(f"h_ready{t}") for t in range(TILES)], k.sem("ident_ready")
        with nc.Block() as block:
            @block.sync
            def _(sp):
                if first:
                    for t in range(2):
                        sp.dma_start(k.h[:, t, :], k.i["x_prompt"][0, P * t:P * (t + 1), :]).then_inc(s_h[t], 16)
                    sp.dma_start(k.h[0:NS, 2, :], k.i["x_sample"].rearrange("b t d -> (b t) d")).then_inc(s_h[2], 16)
                    sp.dma_start(k.ident[:], k.c["ident"]).then_inc(s_ident, 16)
                sp.dma_start(g[:], gain.partition_broadcast(P)).then_inc(loaded, 16)
                if ahead:
                    ahead(sp)
                for t in range(TILES if store else 0):
                    sp.wait_ge(normed, t + 1)
                    sp.dma_start(store[t], xn[0:ROWS[t], t, :]).then_inc(stored, 16)
                if behind:
                    behind(sp)
                if store and not later:
                    sp.wait_ge(stored, 16 * TILES)

            if combine:
                @block.gpsimd
                def _(pool):
                    combine.gather(pool)

            @block.scalar
            def _(act):
                act.wait_ge(cleared, 1)
                nc.scalar.activation(rstd[:], ss[:], ACT.Sqrt).then_inc(warm, 1)
                act.wait_ge(warm, 1)
                for t in range(TILES):
                    r = ROWS[t]
                    if first:
                        act.wait_ge(s_h[t], 16)
                    if combine:
                        act.wait_ge(added, t + 1)
                    nc.scalar.activation(xn[0:r, t, :], k.h[0:r, t, :], ACT.Square,
                                         accum_out=ss[0:r, t:t + 1]).then_inc(squares, 1)
                act.wait_ge(inv, 1)
                nc.scalar.activation(rstd[:], ms[:], ACT.Sqrt).then_inc(root, 1)
                if chunks:
                    for t in range(TILES):
                        act.wait_ge(turned, 2 * t + 1)
                        nc.scalar.activation(k.xT[:, 0:4, P * t:P * t + ROWS[t]],
                                             turned_ps[:, t, 0:512].rearrange("p (c n) -> p c n", c=4)[:, :, 0:ROWS[t]],
                                             ACT.Copy)

            @block.vector
            def _(dve):
                nc.vector.memset(ss[:], 1.0).then_inc(cleared, 1)
                o = Own(dve, own)
                if combine:
                    for t in range(TILES):
                        combine.add(o, t)
                        dve.sem_inc(added, 1)
                dve.wait_ge(squares, TILES)
                if first:
                    for t in range(TILES):
                        dve.wait_ge(s_h[t], 16)
                o.do(nc.vector.tensor_scalar(ss[:], ss[:], 1.0 / D, EPS, ALU.mult, ALU.add))
                nc.vector.reciprocal(ms[:], ss[:]).then_inc(inv, 1)
                dve.wait_ge(root, 1)
                dve.wait_ge(loaded, 16)
                for t in range(TILES):
                    r = ROWS[t]
                    nc.vector.scalar_tensor_tensor(out=xn[0:r, t, :], in0=k.h[0:r, t, :], scalar=rstd[0:r, t:t + 1],
                                                   in1=g[0:r, :], op0=ALU.mult, op1=ALU.mult).then_inc(normed, 1)
                if chunks:
                    for t in range(TILES):
                        dve.wait_ge(turned, 2 * t + 2)
                        nc.vector.tensor_copy(k.xT[:, 4:8, P * t:P * t + ROWS[t]],
                                              turned_ps[:, t, 512:1024].rearrange("p (c n) -> p c n", c=4)[:, :, 0:ROWS[t]])

            @block.tensor
            def _(pe):
                if not chunks:
                    return
                if first:
                    pe.wait_ge(s_ident, 16)
                for t in range(TILES):
                    r = ROWS[t]
                    pe.wait_ge(normed, t + 1)
                    for c in range(KC):
                        src = xn[0:r, t, c:D:KC] if chunks == "pc" else xn[0:r, t, c * P:(c + 1) * P]
                        last = nc.tensor.transpose(turned_ps[:, t, c * P:c * P + r], src, k.ident[0:r, 0:r])
                        if c % 4 == 3:
                            last.then_inc(turned, 1)


def in_proj_phases(k, z, gain, mix, qt, load_later):
    nc = k.nc
    NB, RING = 384, 4
    BLOCKS = IN_W // NB
    w = k.i["w_in_even"].rearrange("e (p c) n -> p (e c) n", c=KC)
    with k.phase() as ctx:
        def sb(name, shape, dt=F32):
            return k.sb(ctx, name, shape, dt)

        wr = sb("win_ring", [P, RING, KC, NB])
        rope = sb("rope", [P, TILES, 2, ROT])
        xpos = sb("xpos", [P, TILES, 2, 2, DK // 2])
        causal = sb("causal", [P, 2, 256])
        ra, rb = sb("ra", [P, 4, 16, ROT]), sb("rb", [P, 4, 256])
        sc, pr, prt = sb("sc", [P, 4, 256]), sb("pr", [P, 4, 256]), sb("prt", [P, 8, P])
        mx, sm, rs = sb("mx", [P, 4]), sb("sm", [P, 4]), sb("rs", [P, 4])
        w_ready = [k.sem(f"win_ready{r}") for r in range(RING)]
        tables = k.sem("turn_tables")

        def ahead(sp):
            for r in range(RING):
                sp.dma_start(wr[:, r], w[:, :, r * NB:(r + 1) * NB]).then_inc(w_ready[r], 16)
            for t, name in ((rope, "rope"), (xpos, "xpos"), (causal, "causal")):
                sp.dma_start(t[:], k.c[name]).then_inc(tables, 16)
            load_later(sp)

        norm_phase(k, "n10", gain, "pc", None, ahead, (mix[:, :, 0:D], None), gain_at=sc[:].rearrange("p h n -> p (h n)"))
        zp = k.ps(ctx, "z_ps", [P, 2, 2, 512])
        zs = k.ps(ctx, "z_ps_s", [P, 512])
        ps = k.ps(ctx, "attn_ps", [P, 2, 512])
        pt = k.ps(ctx, "attn_pt", [P, 512])
        zero = sb("zero_rows", [P, D])
        zeroed, cleared = k.sem("zero_made"), k.cleared
        done = [k.sem(f"z_done{t}") for t in range(TILES)]
        copied = [k.sem(f"z_copied{t}") for t in range(TILES)]
        S = {n: k.sem("at_" + n) for n in "roped pool own qt_turned qt_copied scores scaled probs p_turned p_copied pv mixed".split()}

        units = [(t, hg) for t in range(2) for hg in range(2)]
        steps = [("turn_qk", t) for t in range(TILES)]
        for u, (t, hg) in enumerate(units):
            steps += [("scores", u)] + [("turn_probs", u, part) for part in range(t + 1)] + [("values", u)]
        slots = [(n, t) for n in range((VA + 512) // NB, BLOCKS) for t in range(2 + n % 2)][1:]
        plan = dict(zip(slots, steps))
        assert len(steps) <= len(slots)

        def z_there(eng, columns):
            n = -(-columns // NB)
            eng.wait_ge(copied[0], n)
            eng.wait_ge(copied[1], n)
            eng.wait_ge(copied[2], 2 * -(-n // 2))

        def turn_count(u, part):
            return sum(units[v][0] + 1 for v in range(u)) + part + 1

        with nc.Block() as block:
            @block.sync
            def _(sp):
                for n in range(RING, BLOCKS):
                    sp.wait_ge(done[2], n // 2 - 1)
                    sp.dma_start(wr[:, n % RING], w[:, :, n * NB:(n + 1) * NB]).then_inc(w_ready[n % RING], 16)

            @block.gpsimd
            def _(pool):
                nc.gpsimd.memset(zero[:], 0.0).then_inc(zeroed, 1)
                pool.wait_ge(zeroed, 1)
                rows = k.d["yblk"].shape[0] - MINB * SLOT
                LOTS = 8
                assert rows % LOTS == 0 and rows // LOTS <= P
                lots = k.d["yblk"][MINB * SLOT:].rearrange("(n p) d -> n p d", n=LOTS)
                for n in range(LOTS):
                    pool.dma_start(lots[n], zero[0:rows // LOTS]).then_inc(cleared, 16)
                own = Own(pool, S["pool"])
                pool.wait_ge(tables, 48)
                z_there(pool, VA)
                for t in range(TILES):
                    r = ROWS[t]
                    qk = z[0:r, t, QA:VA].rearrange("p (h d) -> p h d", d=HD)
                    x1, x2 = qk[:, :, 0:ROT], qk[:, :, ROT:2 * ROT]
                    co, si = (rope[0:r, t, i].unsqueeze(1).broadcast_to([r, 16, ROT]) for i in range(2))
                    for i, (a, b) in enumerate(((x1, co), (x2, si), (x2, co), (x1, si))):
                        own.inc(nc.gpsimd.tensor_tensor(ra[0:r, i], a, b, ALU.mult))
                    own.sync()
                    own.inc(nc.gpsimd.tensor_tensor(x1, ra[0:r, 0], ra[0:r, 1], ALU.subtract))
                    own.do(nc.gpsimd.tensor_tensor(x2, ra[0:r, 2], ra[0:r, 3], ALU.add))
                    pool.sem_inc(S["roped"], 1)
                pool.wait_ge(cleared, 16 * LOTS)

            @block.tensor
            def _(pe):
                def q_of(base, h, lo, n):
                    b = 64 * (h % 2)
                    return qt[b:b + 64, base + h // 2, lo:lo + n]

                def turn_qk(t):
                    r = ROWS[t]
                    pe.wait_ge(S["roped"], t + 1)
                    if t:
                        pe.wait_ge(S["qt_copied"], 2 * t)
                    for g in range(2):
                        for i in range(4):
                            col = (4 * g + i) * P
                            last = nc.tensor.transpose(ps[:, g, i * P:i * P + r], z[0:r, t, col:col + P], k.ident[0:r, 0:r])
                    last.then_inc(S["qt_turned"], 1)

                def scores(u):
                    t, hg = units[u]
                    pe.wait_ge(S["qt_copied"], 2 * TILES)
                    if u:
                        pe.wait_ge(S["mixed"], u)
                    for i in range(4):
                        h = 4 * hg + i
                        last = nc.tensor.matmul(ps[:, i % 2, (i // 2) * 256:(i // 2) * 256 + P * (t + 1)],
                                                q_of(0, h, P * t, P), q_of(4, h, 0, P * (t + 1)), start=True, stop=True)
                    last.then_inc(S["scores"], 1)

                def turn_probs(u, part):
                    t, hg = units[u]
                    pe.wait_ge(S["probs"], u + 1)
                    if turn_count(u, part) > 1:
                        pe.wait_ge(S["p_copied"], turn_count(u, part) - 1)
                    for j in range(4):
                        s = 4 * part + j
                        i, b = s // (t + 1), s % (t + 1)
                        last = nc.tensor.transpose(pt[:, j * P:(j + 1) * P], pr[:, 2 * (i % 2) + i // 2, b * P:(b + 1) * P], k.ident[:])
                    last.then_inc(S["p_turned"], 1)

                def values(u):
                    t, hg = units[u]
                    pe.wait_ge(S["p_copied"], turn_count(u, t))
                    for i in range(4):
                        h = 4 * hg + i
                        for b in range(t + 1):
                            last = nc.tensor.matmul(ps[:, 0, i * HD:(i + 1) * HD], prt[:, i * (t + 1) + b, :],
                                                    z[:, b, VA + h * HD:VA + (h + 1) * HD], start=b == 0, stop=b == t)
                    last.then_inc(S["pv"], 1)

                take = {"turn_qk": turn_qk, "scores": scores, "turn_probs": turn_probs, "values": values}

                def step(slot):
                    if slot in plan:
                        take[plan[slot][0]](*plan[slot][1:])

                for n in range(BLOCKS):
                    r = n % RING
                    pe.wait_ge(w_ready[r], 16 * (n // RING) + 16)
                    for t in range(2):
                        if n >= 2:
                            pe.wait_ge(copied[t], n - 1)
                        for c in range(KC):
                            last = nc.tensor.matmul(zp[:, t, n % 2, 0:NB], k.xT[:, c, P * t:P * (t + 1)],
                                                    wr[:, r, c, :], start=c == 0, stop=c == KC - 1)
                        last.then_inc(done[t], 1)
                        step((n, t))
                    if n % 2:
                        if n > 1:
                            pe.wait_ge(copied[2], 2 * (n // 2))
                        for c in range(KC):
                            for half in range(2):
                                last = nc.tensor.matmul(zs[64 * half:64 * half + 64, 0:NB], k.xT[:, c, 256:320],
                                                        wr[:, r - 1 + half, c, :], start=c == 0, stop=c == KC - 1)
                        last.then_inc(done[2], 1)
                        step((n, 2))

            @block.scalar
            def _(act):
                def turn_qk(t):
                    act.wait_ge(S["qt_turned"], t + 1)
                    for g in range(2):
                        nc.scalar.copy(qt[:, 4 * g:4 * g + 4, P * t:P * t + ROWS[t]],
                                       ps[:, g].rearrange("p (c n) -> p c n", c=4)[:, :, 0:ROWS[t]]).then_inc(S["qt_copied"], 1)

                def scores(u):
                    t, hg = units[u]
                    act.wait_ge(S["scaled"], u + 1)
                    if u:
                        act.wait_ge(S["p_turned"], turn_count(u, -1))
                    nc.scalar.activation(pr[:, :, 0:P * (t + 1)], sc[:, :, 0:P * (t + 1)], ACT.Exp).then_inc(S["probs"], 1)

                def turn_probs(u, part):
                    act.wait_ge(S["p_turned"], turn_count(u, part))
                    if u:
                        act.wait_ge(S["pv"], u)
                    nc.scalar.copy(prt[:, 4 * part:4 * part + 4, :].rearrange("p a n -> p (a n)"), pt[:]).then_inc(S["p_copied"], 1)

                take = {"turn_qk": turn_qk, "scores": scores, "turn_probs": turn_probs}
                for n in range(BLOCKS):
                    act.wait_ge(done[0], n + 1)
                    nc.scalar.copy(z[:, 0, n * NB:(n + 1) * NB], zp[:, 0, n % 2, 0:NB]).then_inc(copied[0], 1)
                    for t in range(TILES):
                        step = plan.get((n, t))
                        if step and step[0] in take:
                            take[step[0]](*step[1:])

            @block.vector
            def _(dve):
                own = Own(dve, S["own"])
                V = nc.vector

                def scores(u):
                    t, hg = units[u]
                    n_k = P * (t + 1)
                    s4 = ps[:].rearrange("p a (b n) -> p (a b) n", n=256)[:, :, 0:n_k]
                    dve.wait_ge(S["scores"], u + 1)
                    if u:
                        dve.wait_ge(S["probs"], u)
                    own.do(V.scalar_tensor_tensor(out=sc[:, :, 0:n_k], in0=s4, scalar=HD ** -0.5,
                                                  in1=causal[:, t, 0:n_k].unsqueeze(1).broadcast_to([P, 4, n_k]),
                                                  op0=ALU.mult, op1=ALU.add))
                    own.do(V.tensor_reduce(mx[:], sc[:, :, 0:n_k], X, ALU.max))
                    V.tensor_tensor(sc[:, :, 0:n_k], sc[:, :, 0:n_k], mx[:].unsqueeze(2).broadcast_to([P, 4, n_k]),
                                    ALU.subtract).then_inc(S["scaled"], 1)

                def turn_probs(u, part):
                    if part == 0:
                        dve.wait_ge(S["probs"], u + 1)
                        own.do(V.tensor_reduce(sm[:], pr[:, :, 0:P * (units[u][0] + 1)], X, ALU.add))
                        own.do(V.reciprocal(rs[:], sm[:]))

                def values(u):
                    t, hg = units[u]
                    dve.wait_ge(S["pv"], u + 1)
                    V.tensor_tensor(mix[:, t, hg * 256:(hg + 1) * 256].rearrange("p (j b d) -> p j b d", b=2, d=HD),
                                    ps[:, 0, 0:256].rearrange("p (j b d) -> p j b d", b=2, d=HD),
                                    rs[:].rearrange("p (b j) -> p j b", b=2).unsqueeze(3).broadcast_to([P, 2, 2, HD]), ALU.mult
                                    ).then_inc(S["mixed"], 1)

                def rotate(t):
                    r = ROWS[t]
                    for part in range(2):
                        qk = z[0:r, t, QR + 512 * part:QR + 512 * (part + 1)].rearrange("p (h n e) -> p h n e", h=H, e=2)
                        xe, xo = qk[:, :, :, 0], qk[:, :, :, 1]
                        f = [rb[0:r, i].rearrange("p (h n) -> p h n", h=H) for i in range(4)]
                        co, si = (xpos[0:r, t, i, part].unsqueeze(1).broadcast_to([r, H, 32]) for i in range(2))
                        for i, (a, b) in enumerate(((xe, co), (xo, si), (xo, co), (xe, si))):
                            own.inc(V.tensor_tensor(f[i], a, b, ALU.mult))
                        own.sync()
                        own.inc(V.tensor_tensor(xe, f[0], f[1], ALU.subtract))
                        own.do(V.tensor_tensor(xo, f[2], f[3], ALU.add))

                take = {"scores": scores, "turn_probs": turn_probs, "values": values}

                def step(slot):
                    if slot in plan and plan[slot][0] in take:
                        take[plan[slot][0]](*plan[slot][1:])

                dve.wait_ge(tables, 48)
                for n in range(BLOCKS):
                    step((n, 0))
                    dve.wait_ge(done[1], n + 1)
                    V.tensor_copy(z[:, 1, n * NB:(n + 1) * NB], zp[:, 1, n % 2, 0:NB]).then_inc(copied[1], 1)
                    step((n, 1))
                    if n % 2:
                        dve.wait_ge(done[2], n // 2 + 1)
                        for half in range(2):
                            V.tensor_copy(z[0:NS, 2, (n - 1 + half) * NB:(n + half) * NB],
                                          zs[64 * half:64 * half + 64, 0:NB]).then_inc(copied[2], 1)
                        step((n, 2))
                    t = n - (BLOCKS - 1 - TILES)
                    if 0 <= t < TILES:
                        z_there(dve, VR)
                        rotate(t)


def mixer_tables(k, ctx):
    places = {"dmat": [P, H, P], "dmat_s": [NS, H, NS], "dq": [P, TILES, H], "dk": [P, H], "dk_s": [NS, NSEQ, H],
              "dc": [P, 2, 4], "own": [P, NSEQ // 2, NS], "heads": [P, H, HD]}
    tables = {name: k.sb(ctx, "mixer_" + name, shape) for name, shape in places.items()}
    ready = k.sem("mixer_tables")

    def load(sp):
        for name, t in tables.items():
            sp.dma_start(t[:], k.c[name]).then_inc(ready, 16)

    return tables, ready, load


def even_mixer_phase(k, z, mix, qt, tables, tables_ready):
    nc, c = k.nc, k.c
    PAIRS = NSEQ // 2
    with k.phase() as ctx:
        def sb(name, shape, dt=F32):
            return k.sb(ctx, name, shape, dt)

        dmat, dmat_s, dq, dk, dk_s, dc, own_mask = (tables[n] for n in "dmat dmat_s dq dk dk_s dc own".split())
        heads = tables["heads"][:].rearrange("p h d -> p (h d)")
        pages = sb("pages", [1, 16], I32)
        big = sb("big", [P, 2112])
        soft = sb("soft", [P, 4096])
        km = soft[0:NS, :]
        attkd = sb("attkd", [P, 2 * H * P])
        att = attkd[:, 0:H * P]
        kd = attkd[:, H * P:].rearrange("p (t x) -> p t x", t=2)
        sq = sb("sq", [P, 2, 4 * DV])
        st = sb("st", [P, 4, DV])
        st_out = sb("st_out", [P, 4, DV])
        ss = sb("ss_state", [P, NSEQ, 4, DV])
        tmp = sb("tmp_o", [P, H * DV])
        nrm, nrm2 = sb("nrm", [P, TILES, H]), sb("nrm2", [P, TILES, H])
        qb = sb("qb", [P, NSEQ, 320])
        kv01 = sb("kv", [P, 2, 2, 2, 512])
        whole = [(a[:, 0:512], a[:, 512:1024]) for a in (
            kv01[:, 0, 0].rearrange("p v x -> p (v x)"), kv01[:, 0, 1].rearrange("p v x -> p (v x)"),
            kv01[:, 1, 0].rearrange("p v x -> p (v x)"), kv01[:, 1, 1].rearrange("p v x -> p (v x)"),
            attkd[:, 0:1024], attkd[:, 1024:2048], big[:, 0:1024], big[:, 1024:2048],
            z[:, 0, QR:VR], z[:, 1, QR:VR], z[:, 2, QR:VR])] + [(z[:, 0, QA:KA], z[:, 1, QA:KA])]
        SLOTS = len(whole) // 2

        def kv(n, page, v):
            return whole[2 * (n % SLOTS) + page][v]

        kT = soft[:, 0:2048].rearrange("p (j c n) -> p j c n", j=2, c=4)
        scs = soft[:, 2048:2688].rearrange("p (a n) -> p a n", a=2)
        prs = soft[:, 2688:3328].rearrange("p (a n) -> p a n", a=2)
        prst = soft[:, 3328:4096].rearrange("p (a b n) -> p a b n", a=2, b=3)
        so = sb("so", [P, PAIRS, HD])
        sml = sb("sml", [P, 3, PAIRS])
        msk = tmp[:].rearrange("p (a b) -> p a b", a=2)

        pt = k.ps(ctx, "mix_pt", [P, 2, 512])
        ps = k.ps(ctx, "mix_ps", [P, 2, 512])
        po = k.ps(ctx, "mix_po", [P, 2, 512])
        pd = k.ps(ctx, "mix_pd", [P, 2, 512])

        S = {n: k.sem("mx_" + n) for n in (
            "pages states own qt_turned qt_copied kv_out "
            "ss_new "
            "att decayed ocross orr kd state st_copied st_final st_stored kvm qm "
            "qb kt_turned kt_copied s_scores s_scaled s_probs ps_turned ps_copied s_pv s_out s_stored s_loaded "
            "s_masked o_ready squares osq root osil gated squared zeroed ss_stored actown").split()}
        kv_ready = [k.sem(f"mx_kv_ready{m}") for m in range(PAIRS)]
        flat_state = "h d e -> (h d) e"

        with nc.Block() as block:
            @block.sync
            def _(sp):
                sp.dma_start(pages[:], k.i["page_table"].rearrange("(a n) p -> a (n p)", a=1)).then_inc(S["pages"], 16)
                sp.dma_start(ss[:], k.i["state_ret"][0].rearrange("n h d e -> n (h d) e")
                             .rearrange("n (c p) e -> p n c e", p=P)).then_inc(S["states"], 16)
                sp.wait_ge(S["pages"], 16)

                def attention_leaves(m):
                    sp.wait_ge(S["s_out"], m + 1)
                    sp.dma_start(k.d["smix"][m], so[:, m]).then_inc(S["s_stored"], 16)
                    sp.wait_ge(S["s_stored"], 16 * (m + 1))
                    for j in range(2):
                        n = 2 * m + j
                        sp.dma_start(mix[DSEQ * n:DSEQ * (n + 1), 2, 0:512].rearrange("t (h e) -> t h e", h=H),
                                     k.d["smix"][m, NS * j:NS * (j + 1)].rearrange("(h t) e -> t h e", t=DSEQ)
                                     ).then_inc(S["s_loaded"], 16)

                for m in (0, 2, 1, 3):
                    if m == 2:
                        sp.wait_ge(S["qt_copied"], 6)
                        sp.wait_ge(S["kd"], 2)
                        sp.wait_ge(S["kvm"], 1)
                    elif m == 1:
                        sp.wait_ge(S["o_ready"], 3)
                    elif m == 3:
                        sp.wait_ge(S["ss_new"], NSEQ)
                        sp.dma_start(k.o["ret_sample"][0].rearrange("n h d e -> n (h d) e")
                                     .rearrange("n (c p) e -> p n c e", p=P), ss[:]).then_inc(S["ss_stored"], 16)
                        sp.wait_ge(S["s_pv"], 1)
                    for j in range(2):
                        n = 2 * m + j
                        for g in range(2):
                            page = sp.value_load(pages[0:1, 2 * n + g:2 * n + g + 1], min_val=0, max_val=19)
                            for v, cache in enumerate(("cache_k", "cache_v")):
                                sp.dma_start(kv(n, g, v),
                                             k.i[cache][0].rearrange("n s h d -> n s (h d)")[bass.ds(page, 1)]
                                             .rearrange("a s f -> s (a f)")).then_inc(kv_ready[m], 16)
                for m in range(PAIRS):
                    attention_leaves(m)
                sp.wait_ge(S["s_loaded"], 32 * PAIRS)
                sp.wait_ge(S["ss_stored"], 16)

            @block.gpsimd
            def _(pool):
                nc.gpsimd.memset(qb[:], 0.0).then_inc(S["zeroed"], 1)
                pool.wait_ge(tables_ready, 16 * 8)
                for t in range(2):
                    nc.gpsimd.tensor_tensor(kd[:, t].rearrange("p (h d) -> p h d", d=DK),
                                            z[:, t, KR:VR].rearrange("p (h d) -> p h d", d=DK),
                                            dk[:].unsqueeze(2).broadcast_to([P, H, DK]), ALU.mult).then_inc(S["kd"], 1)
                for t in range(TILES):
                    r = ROWS[t]
                    pool.wait_ge(S["osil"], t + 1)
                    pool.wait_ge(S["squared"], t + 1)
                    nc.gpsimd.tensor_tensor(mix[0:r, t, 512:MIX_W], mix[0:r, t, 512:MIX_W], z[0:r, t, GR:], ALU.mult
                                            ).then_inc(S["gated"], 1)

            @block.tensor
            def _(pe):
                for m in range(6):
                    t, g = m // 2, m % 2
                    r = ROWS[t]
                    if m >= 2:
                        pe.wait_ge(S["qt_copied"], m - 1)
                    for i in range(4):
                        col = QR + (4 * g + i) * P
                        last = nc.tensor.transpose(pt[:, m % 2, i * P:i * P + r], z[0:r, t, col:col + P], k.ident[0:r, 0:r])
                    last.then_inc(S["qt_turned"], 1)
                pe.wait_ge(S["qt_copied"], 6)

                def q_of(base, h, lo, n):
                    b = 64 * (h % 2)
                    return qt[b:b + 64, base + h // 2, lo:lo + n]

                pe.wait_ge(S["kd"], 2)
                for t in range(TILES):
                    r = ROWS[t]
                    if t:
                        pe.wait_ge(S["decayed"], t)
                    for h in range(H):
                        last = nc.tensor.matmul(ps[0:r, h % 2, (h // 2) * r:(h // 2 + 1) * r],
                                                q_of(12, h, P * t, r), q_of(8, h, P * t, r), start=True, stop=True)
                    last.then_inc(S["att"], 1)
                    if t < 2:
                        if t:
                            pe.wait_ge(S["st_copied"], 1)
                        for h in range(H):
                            last = nc.tensor.matmul(pt[64 * (h % 2):64 * (h % 2) + 64, 0, (h // 2) * DV:(h // 2 + 1) * DV],
                                                    kd[:, t, h * DK:(h + 1) * DK], z[:, t, VR + h * DV:VR + (h + 1) * DV],
                                                    start=True, stop=True)
                        last.then_inc(S["state"], 1)
                    if t:
                        pe.wait_ge(S["orr"], t)
                    if t == 1:
                        for h in range(H):
                            b = 64 * (h % 2)
                            last = nc.tensor.matmul(pd[:, h % 2, (h // 2) * DV:(h // 2 + 1) * DV], q_of(8, h, P, P),
                                                    st[b:b + 64, h // 2, :], start=True, stop=True)
                    if t == 2:
                        pe.wait_ge(S["qm"], 1)
                        pe.wait_ge(S["states"], 16)
                        for h, n in [(4 * i + j, n) for i in range(2) for n in range(NSEQ) for j in range(4)]:
                            b = 64 * (h % 2)
                            lo = n * 256 + (h // 2) * 64
                            at = NS * (h // 2 % 2)
                            last = nc.tensor.matmul(pd[at:at + NS, h % 2, (h // 4) * DV:(h // 4 + 1) * DV],
                                                    big[b:b + 64, lo:lo + 64], ss[b:b + 64, n, h // 2, :],
                                                    start=n == 0, stop=n == NSEQ - 1)
                    if t:
                        last.then_inc(S["ocross"], 1)
                    pe.wait_ge(S["decayed"], t + 1)
                    for h in range(H):
                        last = nc.tensor.matmul(po[0:r, h // 4, (h % 4) * DV:(h % 4 + 1) * DV], att[0:r, (4 * (h % 2) + h // 2) * r:(4 * (h % 2) + h // 2 + 1) * r],
                                                z[0:r, t, VR + h * DV:VR + (h + 1) * DV], start=True, stop=True)
                    last.then_inc(S["o_ready"], 1)
                pe.wait_ge(S["st_final"], 1)
                pe.wait_ge(S["kvm"], 1)
                for n in range(NSEQ):
                    if n >= 2:
                        pe.wait_ge(S["ss_new"], n - 1)
                    for h in range(H):
                        last = nc.tensor.matmul(pt[64 * (h % 2):64 * (h % 2) + 64, n % 2, (h // 2) * DV:(h // 2 + 1) * DV],
                                                km[:, n * 512 + h * DK:n * 512 + (h + 1) * DK],
                                                z[0:NS, 2, VR + h * DV:VR + (h + 1) * DV], start=True, stop=True)
                    last.then_inc(S["state"], 1)
                pe.wait_ge(S["ss_new"], NSEQ)
                pe.wait_ge(S["qb"], 1)
                pe.wait_ge(S["orr"], 3)

                def keys(n):
                    if n % 2 == 0:
                        pe.wait_ge(kv_ready[n // 2], 128)
                    if n:
                        pe.wait_ge(S["kt_copied"], 2 * n)
                    for ch in range(4):
                        for g in range(2):
                            last = nc.tensor.transpose(pt[:, ch // 2, ((ch % 2) * 2 + g) * P:((ch % 2) * 2 + g + 1) * P],
                                                       kv(n, g, 0)[:, ch * P:(ch + 1) * P], k.ident[:])
                    last.then_inc(S["kt_turned"], 1)

                def pair_scores(m):
                    pe.wait_ge(S["kt_copied"], 4 * (m + 1))
                    if m >= 2:
                        pe.wait_ge(S["s_scaled"], m - 1)
                    for lo, n_k in ((0, 256), (256, 64)):
                        for ch in range(4):
                            for j in range(2):
                                rhs = kT[:, j, ch, :] if lo == 0 else qt[:, 4 + ch, 256:320]
                                last = nc.tensor.matmul(ps[NS * j:NS * (j + 1), m % 2, lo:lo + n_k],
                                                        qb[:, 2 * m + j, ch * 64:(ch + 1) * 64], rhs, start=ch == 0, stop=ch == 3)
                    last.then_inc(S["s_scores"], 1)

                def turn_probs(m):
                    pe.wait_ge(S["s_probs"], m + 1)
                    if m >= 2:
                        pe.wait_ge(S["ps_copied"], m - 1)
                    for b in range(3):
                        w = (P, P, NS)[b]
                        last = nc.tensor.transpose(pd[0:w, m % 2, b * P:(b + 1) * P], prs[:, m % 2, b * P:b * P + w], k.ident[:])
                    last.then_inc(S["ps_turned"], 1)

                def values(m):
                    pe.wait_ge(S["ps_copied"], m + 1)
                    if m >= 2:
                        pe.wait_ge(S["s_masked"], m - 1)
                    for b in range(3):
                        w = (P, P, NS)[b]
                        for j in range(2):
                            rhs = kv(2 * m + j, b, 1) if b < 2 else z[0:NS, 2, VA:VA + 512]
                            last = nc.tensor.matmul(po[NS * j:NS * (j + 1), m % 2, :], prst[0:w, m % 2, b, NS * j:NS * (j + 1)],
                                                    rhs, start=b == 0, stop=b == 2)
                    last.then_inc(S["s_pv"], 1)

                keys(0)
                keys(1)
                pair_scores(0)
                for m in range(PAIRS):
                    if m + 1 < PAIRS:
                        keys(2 * m + 2)
                    turn_probs(m)
                    if m + 1 < PAIRS:
                        keys(2 * m + 3)
                    values(m)
                    if m + 1 < PAIRS:
                        pair_scores(m + 1)

            @block.scalar
            def _(act):
                own = Own(act, S["actown"])
                for name, col in (("k", KA), ("v", VA)):
                    act.dma_start(k.o[name + "_prompt"].rearrange("e b g p h d -> p (e b g) (h d)"), z[:, 0:2, col:col + 512]
                                  ).then_inc(S["kv_out"], 16)
                    act.dma_start(k.o[name + "_sample"].rearrange("e n t h d -> (e n t) (h d)"), z[0:NS, 2, col:col + 512]
                                  ).then_inc(S["kv_out"], 16)
                for m in range(6):
                    t, g = m // 2, m % 2
                    act.wait_ge(S["qt_turned"], m + 1)
                    nc.scalar.copy(qt[:, 8 + 4 * g:12 + 4 * g, P * t:P * t + ROWS[t]],
                                   pt[:, m % 2].rearrange("p (c n) -> p c n", c=4)[:, :, 0:ROWS[t]]).then_inc(S["qt_copied"], 1)
                for t in range(TILES):
                    nc.scalar.activation(z[0:ROWS[t], t, GR:], z[0:ROWS[t], t, GR:], ACT.Silu).then_inc(S["osil"], 1)
                act.wait_ge(S["st_final"], 1)
                act.dma_start(k.o["ret_prompt"][0, 0].rearrange("h d e -> (h d) e").rearrange("(c p) e -> p c e", p=P),
                              st_out[:]).then_inc(S["st_stored"], 16)

                def keys_copy(n):
                    act.wait_ge(S["kt_turned"], n + 1)
                    if n >= 2:
                        act.wait_ge(S["s_scores"], n // 2)
                    nc.scalar.copy(kT[:, n % 2, 0:2].rearrange("p c n -> p (c n)"), pt[:, 0]).then_inc(S["kt_copied"], 1)

                def probs_copy(m):
                    act.wait_ge(S["ps_turned"], m + 1)
                    if m >= 2:
                        act.wait_ge(S["s_pv"], m - 1)
                    own.inc(nc.scalar.copy(prst[:, m % 2, 0:2, :], pd[:, m % 2, 0:2 * P].rearrange("p (a b) -> p a b", b=P)))
                    own.do(nc.scalar.copy(prst[0:NS, m % 2, 2, :], pd[0:NS, m % 2, 2 * P:3 * P]))
                    act.sem_inc(S["ps_copied"], 1)

                keys_copy(0)
                keys_copy(1)
                for m in range(PAIRS):
                    act.wait_ge(S["s_scaled"], m + 1)
                    if m >= 2:
                        act.wait_ge(S["ps_turned"], m - 1)
                    nc.scalar.activation(prs[:, m % 2, :], scs[:, m % 2, :], ACT.Exp, bias=sml[:, 0, m:m + 1],
                                         accum_out=sml[:, 1, m:m + 1]).then_inc(S["s_probs"], 1)
                    if m + 1 < PAIRS:
                        keys_copy(2 * m + 2)
                    probs_copy(m)
                    if m + 1 < PAIRS:
                        keys_copy(2 * m + 3)
                act.wait_ge(S["osq"], 1)
                nc.scalar.activation(nrm2[:], nrm[:], ACT.Sqrt).then_inc(S["root"], 1)
                act.wait_ge(S["kv_out"], 64)
                act.wait_ge(S["st_stored"], 16)

            @block.vector
            def _(dve):
                own = Own(dve, S["own"])
                V = nc.vector
                own.do(V.memset(big[:], 0.0))
                dve.wait_ge(S["zeroed"], 1)
                for b in range(2):
                    own.inc(V.tensor_copy(qb[64 * b:64 * b + 64].rearrange("p n (c x) -> p n c x", x=80)
                                          [:, :, :, b * DSEQ:(b + 1) * DSEQ],
                                          qt[64 * b:64 * b + 64, 0:4, 256:320].rearrange("p c (n t) -> p n c t", t=DSEQ)))
                own.sync()
                dve.sem_inc(S["qb"], 1)
                dve.wait_ge(tables_ready, 16 * 8)
                for n in range(NSEQ):
                    own.inc(V.tensor_tensor(km[:, n * 512:(n + 1) * 512].rearrange("p (h d) -> p h d", h=H),
                                            z[0:NS, 2, KR:VR].rearrange("p (h d) -> p h d", h=H),
                                            dk_s[:, n].unsqueeze(2).broadcast_to([NS, H, DK]), ALU.mult))
                own.sync()
                dve.sem_inc(S["kvm"], 1)
                for t in range(TILES):
                    if t == 1:
                        own.do(V.tensor_copy(big[:].rearrange("p (n x) -> p n x", x=264)[:, :, 0:256]
                                             .rearrange("p n (c y) -> p n c y", y=64)[:, :, :, 0:DSEQ],
                                             qt[:, 8:12, 256:320].rearrange("p c (n t) -> p n c t", t=DSEQ)))
                        dve.sem_inc(S["qm"], 1)
                    r = ROWS[t]
                    dve.wait_ge(S["att"], t + 1)
                    if t:
                        dve.wait_ge(S["o_ready"], t)
                    table = (dmat if t < 2 else dmat_s)[:].rearrange("p (a h) n -> p a (h n)", a=2)
                    V.tensor_tensor(att[0:r, 0:H * r].rearrange("p (a n) -> p a n", a=2), ps[0:r, :, 0:4 * r], table, ALU.mult
                                    ).then_inc(S["decayed"], 1)
                    if t < 2:
                        dve.wait_ge(S["state"], t + 1)
                        s_ps = pt[:, 0].rearrange("p (c e) -> p c e", e=DV)
                        if t == 0:
                            own.do(V.tensor_copy(st[:], s_ps))
                            dve.sem_inc(S["st_copied"], 1)
                        else:
                            own.do(V.tensor_tensor(st_out[:], st[:], dc[:, 0].unsqueeze(2).broadcast_to([P, 4, DV]), ALU.mult))
                            own.do(V.tensor_tensor(st_out[:], s_ps, st_out[:], ALU.add))
                            dve.sem_inc(S["st_final"], 1)
                    o_dst = mix[0:r, t, 512:MIX_W]
                    o_ps = po[0:r].rearrange("p a b -> p (a b)")
                    if t == 0:
                        dve.wait_ge(S["o_ready"], 1)
                        V.tensor_copy(o_dst, o_ps).then_inc(S["orr"], 1)
                    else:
                        dve.wait_ge(S["ocross"], t)
                        lots = [(pd[0:r], slice(0, 4))] if t == 1 else [(pd[NS * q:NS * q + NS, :, 0:2 * DV], slice(q, 4, 2))
                                                                        for q in range(2)]
                        for src, j in lots:
                            cols = len(range(4)[j])
                            own.inc(V.tensor_tensor(tmp[0:r].rearrange("p (j b e) -> p b j e", b=2, e=DV)[:, :, j],
                                                    src.rearrange("p b (j e) -> p b j e", e=DV),
                                                    dq[0:r, t].rearrange("p (j b) -> p b j", b=2)[:, :, j].unsqueeze(3)
                                                    .broadcast_to([r, 2, cols, DV]), ALU.mult))
                        own.sync()
                        dve.wait_ge(S["o_ready"], t + 1)
                        V.tensor_tensor(o_dst, o_ps, tmp[0:r], ALU.add).then_inc(S["orr"], 1)
                dve.wait_ge(S["orr"], 3)
                dve.wait_ge(S["states"], 16)
                for n in range(NSEQ):
                    dve.wait_ge(S["state"], n + 3)
                    for ch in range(4):
                        last = V.scalar_tensor_tensor(out=ss[:, n, ch], in0=ss[:, n, ch], scalar=dc[:, 1, ch:ch + 1],
                                                      in1=pt[:, n % 2, ch * DV:(ch + 1) * DV], op0=ALU.mult, op1=ALU.add)
                        own.inc(last)
                    own.sync()
                    dve.sem_inc(S["ss_new"], 1)

                def keys_copy(n):
                    dve.wait_ge(S["kt_turned"], n + 1)
                    if n >= 2:
                        dve.wait_ge(S["s_scores"], n // 2)
                    V.tensor_copy(kT[:, n % 2, 2:4].rearrange("p c n -> p (c n)"), pt[:, 1]).then_inc(S["kt_copied"], 1)

                def softmax_in(m):
                    dve.wait_ge(S["s_scores"], m + 1)
                    if m >= 2:
                        dve.wait_ge(S["s_probs"], m - 1)
                    own.inc(V.tensor_scalar(scs[:, m % 2, 0:256], ps[:, m % 2, 0:256], HD ** -0.5, None, ALU.mult))
                    own.do(V.scalar_tensor_tensor(out=scs[:, m % 2, 256:320], in0=ps[:, m % 2, 256:320], scalar=HD ** -0.5,
                                                  in1=own_mask[:, m, :], op0=ALU.mult, op1=ALU.add))
                    own.do(V.tensor_reduce(sml[:, 2, m:m + 1], scs[:, m % 2, :], X, ALU.max))
                    V.tensor_scalar(sml[:, 0, m:m + 1], sml[:, 2, m:m + 1], -1.0, None, ALU.mult).then_inc(S["s_scaled"], 1)

                def place(m):
                    dve.wait_ge(S["s_pv"], m + 1)
                    own.do(V.reciprocal(sml[:, 2, m:m + 1], sml[:, 1, m:m + 1]))
                    V.scalar_tensor_tensor(out=msk[:, m % 2, :], in0=po[:, m % 2, :], scalar=sml[:, 2, m:m + 1],
                                           in1=heads, op0=ALU.mult, op1=ALU.mult).then_inc(S["s_masked"], 1)
                    dve.wait_ge(S["s_masked"], m + 1)
                    V.tensor_reduce(so[:, m, :], msk[:, m % 2, :].rearrange("p (h e) -> p e h", h=H), X, ALU.add
                                    ).then_inc(S["s_out"], 1)

                def squares(t):
                    r = ROWS[t]
                    for half in range(2):
                        o = mix[0:r, t, 512 + 512 * half:1024 + 512 * half]
                        own.do(V.tensor_tensor(sq[0:r, half], o, o, ALU.mult))
                    for half in range(2):
                        own.inc(V.tensor_reduce(nrm2[0:r, t, 4 * half:4 * half + 4],
                                                sq[0:r, half].rearrange("p (h e) -> p h e", e=DV), X, ALU.add))
                    own.sync()
                    dve.sem_inc(S["squared"], 1)

                own.do(V.memset(nrm2[:], 1.0))
                keys_copy(0)
                keys_copy(1)
                for m in range(PAIRS):
                    softmax_in(m)
                    if m + 1 < PAIRS:
                        keys_copy(2 * m + 2)
                        keys_copy(2 * m + 3)
                    if m < TILES:
                        squares(m)
                    else:
                        own.do(V.tensor_scalar(nrm2[:], nrm2[:], 1.0 / DV, EPS, ALU.mult, ALU.add))
                        V.reciprocal(nrm[:], nrm2[:]).then_inc(S["osq"], 1)
                    place(m)
                dve.wait_ge(S["root"], 1)
                for t in range(TILES):
                    r = ROWS[t]
                    dve.wait_ge(S["gated"], t + 1)
                    o = mix[0:r, t, 512:MIX_W].rearrange("p (h e) -> p h e", e=DV)
                    own.inc(V.tensor_tensor(o, o, nrm2[0:r, t].unsqueeze(2).broadcast_to([r, H, DV]), ALU.mult))


def out_proj_phase(k, mix, behind):
    nc = k.nc
    w = k.i["w_out_even"].rearrange("e (p c) n -> p (e c) n", c=KM)
    LOTS = 4
    with k.phase() as ctx:
        wo = k.sb(ctx, "wo", [P, KM, D])
        mixT = k.sb(ctx, "mixT", [P, KM, NTOK])
        pt = k.ps(ctx, "op_pt", [P, 2, 512])
        acc = k.ps(ctx, "op_acc", [P, TILES, 2, 512])
        w_ready = [k.sem(f"wo_ready{n}") for n in range(LOTS)]
        turned, copied, done = k.sem("mix_turned"), k.sem("mix_copied"), k.sem("op_done")
        with nc.Block() as block:
            @block.sync
            def _(sp):
                for n in range(LOTS):
                    s = slice(n * KM // LOTS, (n + 1) * KM // LOTS)
                    sp.dma_start(wo[:, s], w[:, s]).then_inc(w_ready[n], 16)
                behind(sp)

            @block.tensor
            def _(pe):
                def product(t, c):
                    for half in range(2):
                        out = acc[64 * half:64 * half + 64, 2, 0, :] if t == 2 else acc[:, t, half, :]
                        last = nc.tensor.matmul(out, mixT[:, c, P * t:P * t + ROWS[t]],
                                                wo[:, c, half * 512:(half + 1) * 512], start=c == 0, stop=c == KM - 1)
                    return last

                for m in range(9):
                    t, g = m // 3, m % 3
                    r = ROWS[t]
                    if m >= 2:
                        pe.wait_ge(copied, m - 1)
                    for i in range(4):
                        last = nc.tensor.transpose(pt[:, m % 2, i * P:i * P + r], mix[0:r, t, 4 * g + i:MIX_W:KM],
                                                   k.ident[0:r, 0:r])
                    last.then_inc(turned, 1)
                pe.wait_ge(copied, 9)
                for n in range(LOTS - 1):
                    pe.wait_ge(w_ready[n], 16)
                    for c in range(KM // LOTS * n, KM // LOTS * (n + 1)):
                        for t in range(TILES):
                            product(t, c)
                pe.wait_ge(w_ready[LOTS - 1], 16)
                for t in range(TILES):
                    for c in range(KM // LOTS * (LOTS - 1), KM):
                        last = product(t, c)
                    last.then_inc(done, 1)

            @block.scalar
            def _(act):
                for m in range(9):
                    t, g = m // 3, m % 3
                    act.wait_ge(turned, m + 1)
                    nc.scalar.copy(mixT[:, 4 * g:4 * g + 4, P * t:P * t + ROWS[t]],
                                   pt[:, m % 2].rearrange("p (c n) -> p c n", c=4)[:, :, 0:ROWS[t]]).then_inc(copied, 1)

            @block.vector
            def _(dve):
                for t in range(2):
                    dve.wait_ge(done, t + 1)
                    nc.vector.tensor_tensor(k.h[:, t, :], acc[:, t].rearrange("p a b -> p (a b)"), k.h[:, t, :], ALU.add)
                dve.wait_ge(done, 3)
                for half in range(2):
                    h = k.h[0:NS, 2, half * 512:(half + 1) * 512]
                    nc.vector.tensor_tensor(h, acc[64 * half:64 * half + 64, 2, 0, :], h, ALU.add)


def moe_route(k, ctx, li):
    return {
        "slot_tok": k.sb(ctx, f"slot_tok{li}", [SLOT, NBLK], U32),
        "dest": k.sb(ctx, f"dest{li}", [P, TILES, 2], U32),
        "weight": k.sb(ctx, f"weight{li}", [P, TILES, 2]),
        "experts": k.sb(ctx, f"experts{li}", [1, NBLK], I32),
        "total": k.sb(ctx, f"total{li}", [1, 1], I32),
    }


class ExpertWeights:

    def __init__(self, k, li, w13_last=None):
        self.k, self.li = k, li
        self.w13, self.w2 = [None] * BUFS, [None] * BUFS
        self.w13[-1] = w13_last
        self.started = set()

    def place(self, ctx, *names):
        for which, b in names:
            shape = [P, KC, 2 * DE] if which == "w13" else [P, 4, D]
            self.of(which)[b] = self.k.sb(ctx, f"{which}_{self.li}{b}", shape)

    def place_rest(self, ctx):
        self.place(ctx, *((which, b) for b in range(BUFS) for which in ("w13", "w2") if self.of(which)[b] is None))

    def of(self, which):
        return self.w13 if which == "w13" else self.w2

    def start(self, sp, *names):
        for which, b in names:
            self.load(sp, which, b, b)
            self.started.add((which, b))

    def start_rest(self, sp):
        self.start(sp, *((which, b) for b in range(BUFS) for which in ("w13", "w2") if (which, b) not in self.started))

    def load(self, sp, which, e, b, halves=range(2)):
        k = self.k
        w = k.i["moe_" + which][self.li].rearrange("e (p c) n -> e p (c n)", p=P)[bass.ds(e, 1)]
        to = self.of(which)[b][:].rearrange("p c n -> p (c n)")
        if which == "w2":
            sp.dma_start(to, w.rearrange("e p n -> p (e n)")).then_inc(k.w2_ready[self.li][b], 16)
            return
        for half in halves:
            part = slice(KC * DE * half, KC * DE * (half + 1))
            sp.dma_start(to[:, part], w[:, :, part].rearrange("e p n -> p (e n)")).then_inc(k.w13_ready[self.li][b], 16)


class TokenRows:

    def __init__(self, k, ctx, li):
        self.all = k.sb(ctx, f"token_rows{li}", [P, TILES * D + KC * NTOK])
        self.xT = self.all[:, 0:KC * NTOK].rearrange("p (c n) -> p c n", c=KC)
        self.xn = self.all[:, KC * NTOK:].rearrange("p (t d) -> p t d", t=TILES)
        self.mix = self.all[:, 0:TILES * MIX_W].rearrange("p (t d) -> p t d", t=TILES)


def moe_layer(k, li, rows, route, weights, place):
    with k.phase() as wc:
        weights.place_rest(wc)
        with ExitStack() as xc:
            k.xT, xn = place.xT, place.xn
            stored = k.sem(f"xn_stored{li}")
            r = {
                "w": k.sb(xc, f"wr{li}", [P, KC, GROUPS + NE]), "bias": k.sb(xc, f"br{li}", [P, GROUPS + NE]),
                "before": k.sb(xc, f"before{li}", [P, P]), "token": k.sb(xc, f"token{li}", [P, TILES]),
                "loaded": k.sem(f"router_loaded{li}"),
            }

            def ahead(sp):
                for dst, src in (
                        (r["w"][:, :, 0:GROUPS], k.i["moe_w_group"][li].rearrange("(p c) n -> p c n", c=KC)),
                        (r["w"][:, :, GROUPS:], k.i["moe_w_expert"][li].rearrange("(p c) n -> p c n", c=KC)),
                        (r["bias"][:, 0:GROUPS], k.i["moe_b_group"][li].partition_broadcast(P)),
                        (r["bias"][:, GROUPS:], k.i["moe_b_expert"][li].partition_broadcast(P)),
                        (r["before"][:], k.c["before"]), (r["token"][:], k.c["token"])):
                    sp.dma_start(dst, src).then_inc(r["loaded"], 16)

            norm_phase(k, f"n2{li}", k.i["norm2"][li], "pc", rows, ahead, (xn, stored), weights.start_rest)
            routing_phase(k, li, route, r, stored)
        experts_phase(k, li, route, weights)


def routing_phase(k, li, route, r, stored):
    nc = k.nc
    V = nc.vector
    NL = GROUPS + NE
    MOST = NTOK // SLOT
    with k.phase() as ctx:
        def sb(name, shape, dt=F32):
            return k.sb(ctx, f"{name}_r{li}", shape, dt)

        w, bias, before, token, loaded = (r[n] for n in "w bias before token loaded".split())
        ones = sb("ones", [P, P])
        count_up = sb("count_up", [P, 64])
        lg = sb("lg", [P, TILES, NL])
        g8 = sb("g8", [P, TILES, 8])
        gmax, gidx = sb("gmax", [P, TILES, 8]), sb("gidx", [P, TILES, 8], U32)
        gf = sb("gf", [P, TILES])
        ge, gs, wg = sb("ge", [P, TILES, GROUPS]), sb("gs", [P, TILES]), sb("wg", [P, TILES])
        goh = sb("goh", [P, TILES, GROUPS])
        leg = sb("leg", [P, TILES, PER, GROUPS])
        le8, emax, eidx = sb("le8", [P, TILES, PER]), sb("emax", [P, TILES, 8]), sb("eidx", [P, TILES, 8], U32)
        ef = sb("ef", [P, TILES, 2])
        dd, ee, w0 = sb("dd", [P, TILES]), sb("ee", [P, TILES]), sb("w0", [P, TILES])
        oh = sb("oh", [P, TILES, 2, NE])
        both = sb("both", [P, TILES, NE])
        cnt, cmp = sb("cnt", [P, NE]), sb("cmp", [P, NE, MOST])
        limits = sb("limits", [P, MOST])
        nblk, incl, first = sb("nblk", [P, NE]), sb("incl", [P, NE]), sb("first", [P, NE])
        rank, blk, sel = sb("rank", [P, TILES, 2]), sb("blk", [P, TILES, 2]), sb("sel", [P, TILES, 2, NE])
        ahead = sb("ahead", [P, TILES, NE])
        qc, q = sb("qc", [P, TILES, 2, MOST - 1]), sb("q", [P, TILES, 2])
        slot, destf = sb("slot", [P, TILES, 2]), sb("destf", [P, TILES, 2])
        ohs, ohb = sb("ohs", [P, TILES, 2, SLOT]), sb("ohb", [P, TILES, 2, NBLK])
        ended, bexp = sb("ended", [P, NE]), sb("bexp", [P, 1])
        total = sb("total_f", [1, 1])
        lps = k.ps(ctx, f"lps{li}", [P, TILES, 512])
        cps = k.ps(ctx, f"cps{li}", [P, TILES, 512])
        tps = k.ps(ctx, f"tps{li}", [P, 512])
        aps = k.ps(ctx, f"aps{li}", [P, 512])
        own_s, made = k.sem("r_own"), k.sem("r_made")
        logits, shifted, exps, delta = k.sem("r_logits"), k.sem("r_shifted"), k.sem("r_exps"), k.sem("r_delta")
        chosen, counted, placed, listed = k.sem("r_chosen"), k.sem("r_counted"), k.sem("r_placed"), k.sem("r_listed")
        with nc.Block() as block:
            @block.sync
            def _(sp):
                sp.wait_ge(stored, 16 * TILES)
            @block.gpsimd
            def _(pool):
                nc.gpsimd.iota(count_up[:], pattern=[[1, 64]], base=0, channel_multiplier=0,
                               allow_small_or_imprecise_dtypes=True).then_inc(made, 1)
                nc.gpsimd.iota(limits[:], pattern=[[SLOT, MOST]], base=0, channel_multiplier=0,
                               allow_small_or_imprecise_dtypes=True).then_inc(made, 1)
                nc.gpsimd.memset(ones[:], 1.0).then_inc(made, 1)

            @block.tensor
            def _(pe):
                pe.wait_ge(loaded, 96)
                for t in range(TILES):
                    for c in range(KC):
                        last = nc.tensor.matmul(lps[0:ROWS[t], t, 0:NL], k.xT[:, c, P * t:P * t + ROWS[t]], w[:, c, :],
                                                start=c == 0, stop=c == KC - 1)
                last.then_inc(logits, 1)
                pe.wait_ge(chosen, 1)
                pe.wait_ge(made, 3)
                for t in range(TILES):
                    for s in range(t + 1):
                        r = ROWS[s]
                        lhs = before[0:r, 0:ROWS[t]] if s == t else ones[0:r, 0:ROWS[t]]
                        last = nc.tensor.matmul(cps[0:ROWS[t], t, 0:NE], lhs, both[0:r, s, :], start=s == 0, stop=s == t)
                for s in range(TILES):
                    last = nc.tensor.matmul(aps[:, 0:NE], ones[0:ROWS[s], :], both[0:ROWS[s], s, :], start=s == 0, stop=s == TILES - 1)
                last.then_inc(counted, 1)
                pe.wait_ge(placed, 1)
                for m in range(2 * TILES):
                    t, j = m // 2, m % 2
                    last = nc.tensor.matmul(tps[0:SLOT, 0:NBLK], ohs[0:ROWS[t], t, j, :], ohb[0:ROWS[t], t, j, :],
                                            start=m == 0, stop=m == 2 * TILES - 1)
                nc.tensor.matmul(aps[0:1, 0:NBLK], bexp[:], k.ident[:, 0:NBLK], start=True, stop=True).then_inc(listed, 1)

            @block.scalar
            def _(act):
                act.wait_ge(shifted, 1)
                nc.scalar.activation(ge[:], goh[:], ACT.Exp).then_inc(exps, 1)
                act.wait_ge(delta, 1)
                nc.scalar.activation(ee[:], dd[:], ACT.Exp).then_inc(exps, 1)

            @block.vector
            def _(dve):
                own = Own(dve, own_s)
                own.inc(V.memset(g8[:], NEG))
                own.inc(V.memset(lg[:], 0.0))
                own.do(V.memset(both[:], 0.0))
                dve.wait_ge(loaded, 96)
                dve.wait_ge(made, 3)
                dve.wait_ge(logits, 1)
                for t in range(TILES):
                    own.inc(V.tensor_tensor(lg[0:ROWS[t], t], lps[0:ROWS[t], t, 0:NL], bias[0:ROWS[t]], ALU.add))
                own.sync()
                own.do(V.tensor_copy(g8[:, :, 0:GROUPS], lg[:, :, 0:GROUPS]))
                for t in range(TILES):
                    own.do(V.max(gmax[:, t], g8[:, t]))
                    own.do(V.max_index(gidx[:, t], gmax[:, t], g8[:, t]))
                own.inc(V.tensor_copy(gf[:], gidx[:, :, 0]))
                V.tensor_tensor(goh[:], lg[:, :, 0:GROUPS], gmax[:, :, 0:1].broadcast_to([P, TILES, GROUPS]),
                                ALU.subtract).then_inc(shifted, 1)
                dve.wait_ge(exps, 1)
                own.do(V.tensor_reduce(gs[:], ge[:], X, ALU.add))
                own.do(V.reciprocal(wg[:], gs[:]))
                own.do(V.tensor_tensor(goh[:], count_up[:, 0:GROUPS].unsqueeze(1).broadcast_to([P, TILES, GROUPS]),
                                       gf[:].unsqueeze(2).broadcast_to([P, TILES, GROUPS]), ALU.is_equal))
                for t in range(TILES):
                    own.inc(V.tensor_tensor(leg[:, t], lg[:, t, GROUPS:NL].rearrange("p (g e) -> p e g", g=GROUPS),
                                            goh[:, t].unsqueeze(1).broadcast_to([P, PER, GROUPS]), ALU.mult))
                own.sync()
                own.do(V.tensor_reduce(le8[:], leg[:], X, ALU.add))
                for t in range(TILES):
                    own.do(V.max(emax[:, t], le8[:, t]))
                    own.do(V.max_index(eidx[:, t], emax[:, t], le8[:, t]))
                own.inc(V.tensor_copy(ef[:], eidx[:, :, 0:2]))
                V.tensor_tensor(dd[:], emax[:, :, 1], emax[:, :, 0], ALU.subtract).then_inc(delta, 1)
                own.sync()
                for j in range(2):
                    own.do(V.scalar_tensor_tensor(out=ef[:, :, j], in0=gf[:], scalar=float(PER), in1=ef[:, :, j],
                                                  op0=ALU.mult, op1=ALU.add))
                for t in range(TILES):
                    own.inc(V.tensor_tensor(oh[:, t], count_up[:, 0:NE].unsqueeze(1).broadcast_to([P, 2, NE]),
                                            ef[:, t].unsqueeze(2).broadcast_to([P, 2, NE]), ALU.is_equal))
                own.sync()
                V.tensor_tensor(both[:], oh[:, :, 0, :], oh[:, :, 1, :], ALU.add).then_inc(chosen, 1)
                dve.wait_ge(exps, 2)
                own.do(V.tensor_scalar(w0[:], ee[:], 1.0, None, ALU.add))
                own.do(V.reciprocal(w0[:], w0[:]))
                own.do(V.tensor_tensor(w0[:], w0[:], wg[:], ALU.mult))
                own.inc(V.tensor_copy(route["weight"][:, :, 0], w0[:]))
                own.inc(V.tensor_tensor(route["weight"][:, :, 1], w0[:], ee[:], ALU.mult))
                dve.wait_ge(counted, 1)
                own.do(V.tensor_copy(cnt[:], aps[:, 0:NE]))
                own.do(V.tensor_tensor(cmp[:], cnt[:].unsqueeze(2).broadcast_to([P, NE, MOST]),
                                       limits[:].unsqueeze(1).broadcast_to([P, NE, MOST]), ALU.is_gt))
                own.do(V.tensor_reduce(nblk[:], cmp[:], X, ALU.add))
                own.do(V.tensor_scalar(nblk[:, 0:BUFS], nblk[:, 0:BUFS], -1.0, 0.0, ALU.add, ALU.max))
                own.do(V.tensor_tensor_scan(incl[:], ones[:, 0:NE], nblk[:], 0.0, ALU.mult, ALU.add))
                own.do(V.tensor_tensor(first[:], incl[:], nblk[:], ALU.subtract))
                own.do(V.tensor_scalar(first[:], first[:], float(BUFS), None, ALU.add))
                own.do(V.tensor_scalar(first[:, 0:BUFS], first[:, 0:BUFS], -1.0, None, ALU.add))
                own.do(V.tensor_scalar(total[:], incl[0:1, NE - 1:NE], float(BUFS), None, ALU.add))
                own.inc(V.tensor_copy(route["total"][:], total[:]))
                own.do(V.tensor_scalar(ended[:], incl[:], token[:, 0:1], None, ALU.is_le))
                own.do(V.tensor_reduce(bexp[:], ended[:], X, ALU.add))
                own.do(V.tensor_scalar(bexp[:], bexp[:], float(NE - 1), None, ALU.min))
                own.inc(V.memset(ahead[:], 0.0))
                own.sync()
                for t in range(TILES):
                    own.inc(V.tensor_copy(ahead[0:ROWS[t], t], cps[0:ROWS[t], t, 0:NE]))
                own.sync()
                for src, dst in ((ahead, rank), (first, blk)):
                    for t in range(TILES):
                        v = (src[:, t] if src is ahead else src[:]).unsqueeze(1).broadcast_to([P, 2, NE])
                        own.inc(V.tensor_tensor(sel[:, t], oh[:, t], v, ALU.mult))
                    own.sync()
                    own.do(V.tensor_reduce(dst[:], sel[:], X, ALU.add))
                for j in range(2):
                    own.inc(V.tensor_tensor(qc[:, :, j], rank[:, :, j].unsqueeze(2).broadcast_to([P, TILES, MOST - 1]),
                                            limits[:, 1:].unsqueeze(1).broadcast_to([P, TILES, MOST - 1]), ALU.is_ge))
                own.sync()
                own.do(V.tensor_reduce(q[:], qc[:], X, ALU.add))
                own.do(V.scalar_tensor_tensor(out=slot[:], in0=q[:], scalar=-float(SLOT), in1=rank[:], op0=ALU.mult, op1=ALU.add))
                own.do(V.tensor_tensor(blk[:], blk[:], q[:], ALU.add))
                own.inc(V.tensor_scalar(sel[:, :, :, 0], ef[:], float(BUFS) - 0.5, None, ALU.is_le))
                own.inc(V.tensor_scalar(sel[:, :, :, 1], q[:], 0.5, None, ALU.is_le))
                own.inc(V.tensor_tensor(sel[:, :, :, 2], ef[:], blk[:], ALU.subtract))
                own.sync()
                own.do(V.tensor_tensor(sel[:, :, :, 0], sel[:, :, :, 0], sel[:, :, :, 1], ALU.mult))
                own.do(V.tensor_tensor(sel[:, :, :, 0], sel[:, :, :, 0], sel[:, :, :, 2], ALU.mult))
                own.do(V.tensor_tensor(blk[:], blk[:], sel[:, :, :, 0], ALU.add))
                own.do(V.scalar_tensor_tensor(out=destf[:], in0=blk[:], scalar=float(SLOT), in1=slot[:], op0=ALU.mult, op1=ALU.add))
                own.inc(V.tensor_copy(route["dest"][:], destf[:]))
                for t in range(TILES):
                    own.inc(V.tensor_tensor(ohs[:, t], count_up[:, 0:SLOT].unsqueeze(1).broadcast_to([P, 2, SLOT]),
                                            slot[:, t].unsqueeze(2).broadcast_to([P, 2, SLOT]), ALU.is_equal))
                    own.inc(V.tensor_tensor(ohb[:, t], count_up[:, 0:NBLK].unsqueeze(1).broadcast_to([P, 2, NBLK]),
                                            blk[:, t].unsqueeze(2).broadcast_to([P, 2, NBLK]), ALU.is_equal))
                own.sync()
                for t in range(TILES):
                    own.inc(V.tensor_scalar(ohb[:, t], ohb[:, t], token[:, t:t + 1], None, ALU.mult))
                own.sync()
                dve.sem_inc(placed, 1)
                dve.wait_ge(listed, 1)
                V.tensor_copy(route["slot_tok"][:], tps[0:SLOT, 0:NBLK])
                V.tensor_copy(route["experts"][:], aps[0:1, 0:NBLK])


def experts_phase(k, li, route, weights):
    nc = k.nc
    ROUNDS = NBLK // BUFS
    yblk = k.d["yblk"].rearrange("(b s) d -> b s d", s=SLOT)
    HALF = (slice(0, SLOT), slice(64, 64 + SLOT))
    HI = HALF[1]
    with k.phase() as ctx:
        def sb(name, shape, dt=F32):
            return k.sb(ctx, f"{name}_e{li}", shape, dt)

        wa, wb = weights.w13, weights.w2
        xg = [sb(f"xg{b}", [SLOT, D]) for b in range(BUFS)]
        idx = [sb(f"idx{b}", [SLOT, 1], U32) for b in range(BUFS)]
        xgT = [sb(f"xgT{b}", [P, KC, SLOT]) for b in range(BUFS)]
        act_g = sb("act_g", [P, DE])
        hid = sb("hid", [P, DE])
        hidT = sb("hidT", [P, 4, SLOT])
        y = [sb(f"y{b}", [P, D // 2]) for b in range(BUFS)]
        xps = k.ps(ctx, f"xps{li}", [P, KC, SLOT])
        gu = [k.ps(ctx, f"gu{li}{b}", [P, DE]) for b in range(BUFS)]
        hps = k.ps(ctx, f"hps{li}", [P, 2, 4 * SLOT])
        yps = [k.ps(ctx, f"yps{li}{b}", [P, D // 2]) for b in range(BUFS)]
        w13_ready, w2_ready = k.w13_ready[li], k.w2_ready[li]
        gathered = k.gathered[li]
        stored = [k.sem(f"y_stored{b}") for b in range(BUFS)]
        w13_used, w2_used, idx_copied = k.sem("w13_used"), k.sem("w2_used"), k.sem("idx_copied")
        passed = k.sem("passed")
        x_turned, x_copied, gate_up = k.sem("x_turned"), k.sem("x_copied"), k.sem("gate_up")
        silu, hidden, h_turned, h_copied = k.sem("silu"), k.sem("hidden"), k.sem("h_turned"), k.sem("h_copied")
        y_copied = k.sem("y_copied")

        def blocks(eng, body):
            total = eng.value_load(route["total"][:], min_val=1, max_val=MAXB)
            with eng.Fori(0, ROUNDS) as i:
                with eng.If(BUFS * i < total):
                    for p in range(BUFS):
                        with eng.If(BUFS * i + p < total):
                            body(i, p, BUFS * i + p)

        with nc.Block() as block:
            @block.sync
            def _(sp):
                total = sp.value_load(route["total"][:], min_val=1, max_val=MAXB)
                with sp.Fori(1, ROUNDS) as i:
                    with sp.If(BUFS * (i - 1) < total):
                        for p in range(BUFS):
                            b = BUFS * i + p
                            with sp.If(b < total):
                                e = sp.value_load(route["experts"][0:1, bass.ds(b - BUFS, 1)], min_val=0, max_val=NE - 1)
                                for half in range(2):
                                    sp.wait_ge(w13_used, 2 * (b - BUFS) + 1 + half)
                                    weights.load(sp, "w13", e, p, [half])
                                sp.wait_ge(w2_used, b - BUFS + 1)
                                weights.load(sp, "w2", e, p)
                            with sp.If(b < total + BUFS):
                                sp.wait_ge(y_copied, 2 * (b - BUFS + 1))
                                for half in range(2):
                                    sp.dma_start(yblk[bass.ds(b - BUFS, 1), :, half * 512:(half + 1) * 512].rearrange("b s d -> s (b d)"),
                                                 y[p][HALF[half], :]).then_inc(stored[p], 16)
                for p in range(BUFS):
                    sp.wait_ge(stored[p], 32 * ((total + BUFS - 1 - p) // BUFS))
                sp.sem_inc(passed, 1)

            @block.gpsimd
            def _(pool):
                def gather(i, p, b):
                    pool.wait_ge(x_turned, b + 1)
                    nc.gpsimd.tensor_copy(idx[p][:], route["slot_tok"][:, bass.ds(b, 1)]).then_inc(idx_copied, 1)
                    pool.wait_ge(idx_copied, b + 1)
                    pool.sem_inc(passed, 1)
                    nc.gpsimd.indirect_dma_start(xg[p][:], None, k.d["xn"], bass.IndirectOffsetOnAxis(ap=idx[p][:], axis=0)
                                                 ).then_inc(gathered[p], 16)

                blocks(pool, gather)

            @block.tensor
            def _(pe):
                pe.sem_inc(x_turned, BUFS)

                def expert(i, p, b):
                    pe.wait_ge(gathered[p], 16 * i + 16)
                    pe.wait_ge(x_copied, b + 1)
                    pe.sem_inc(passed, 1)
                    for c in range(KC):
                        last = nc.tensor.transpose(xps[:, c, :], xg[p][:, c:D:KC], k.ident[0:SLOT, 0:SLOT])
                    last.then_inc(x_turned, 1)
                    pe.wait_ge(x_copied, b + 2)
                    pe.wait_ge(w13_ready[p], 32 * i + 32)
                    for c in range(KC):
                        for half in range(2):
                            last = nc.tensor.matmul(gu[p][HALF[half], :], xgT[p][:, c, :],
                                                    wa[p][:, c, half * DE:(half + 1) * DE], start=c == 0, stop=c == KC - 1)
                        if c == KC // 2 - 1:
                            last.then_inc(w13_used, 1)
                    last.then_inc(gate_up, 1)
                    pe.wait_ge(gate_up, b + 1)
                    pe.sem_inc(w13_used, 1)
                    pe.wait_ge(hidden, b + 1)
                    pe.sem_inc(passed, 1)
                    for j in range(4):
                        last = nc.tensor.transpose(hps[:, 0, j * SLOT:(j + 1) * SLOT], hid[HI, j:DE:4], k.ident[HI, HI])
                    last.then_inc(h_turned, 1)
                    pe.wait_ge(h_copied, b + 1)
                    pe.wait_ge(w2_ready[p], 16 * i + 16)
                    for j in range(4):
                        for half in range(2):
                            last = nc.tensor.matmul(yps[p][HALF[half], :], hidT[:, j, :],
                                                    wb[p][:, j, half * 512:(half + 1) * 512], start=j == 0, stop=j == 3)
                    last.then_inc(w2_used, 1)

                blocks(pe, expert)

            @block.scalar
            def _(act):
                def step(i, p, b):
                    act.wait_ge(gate_up, b + 1)
                    nc.scalar.activation(act_g[HI, :], gu[p][0:SLOT, :], ACT.Silu).then_inc(silu, 1)

                blocks(act, step)

            @block.vector
            def _(dve):
                dve.sem_inc(x_copied, 1)

                def step(i, p, b):
                    dve.wait_ge(x_turned, b + BUFS + 1)
                    nc.vector.tensor_copy(xgT[p][:], xps[:]).then_inc(x_copied, 1)
                    dve.wait_ge(silu, b + 1)
                    nc.vector.tensor_tensor(hid[HI, :], gu[p][HI, :], act_g[HI, :], ALU.mult).then_inc(hidden, 1)
                    dve.wait_ge(h_turned, b + 1)
                    nc.vector.tensor_copy(hidT[:].rearrange("p j n -> p (j n)"), hps[:, 0, :]).then_inc(h_copied, 1)
                    dve.wait_ge(w2_used, b + 1)
                    dve.wait_ge(stored[p], 32 * i)
                    for half in range(2):
                        nc.vector.tensor_copy(y[p][HALF[half], :], yps[p][HALF[half], :]).then_inc(y_copied, 1)

                blocks(dve, step)


class Combination:

    def __init__(self, k, li, route, yg):
        self.k, self.li, self.route, self.yg = k, li, route, yg

    def gather(self, pool):
        for m in range(2 * TILES):
            t, j = m // 2, m % 2
            r = ROWS[t]
            self.k.nc.gpsimd.indirect_dma_start(self.yg[0:r, t, j, :], None, self.k.d["yblk"],
                                                bass.IndirectOffsetOnAxis(ap=self.route["dest"][0:r, t, j:j + 1], axis=0)
                                                ).then_inc(self.k.combined[m], 16)

    def add(self, own, t):
        h = self.k.h[0:ROWS[t], t, :]
        for j in range(2):
            own.eng.wait_ge(self.k.combined[2 * t + j], 16 * (self.li + 1))
            own.do(self.k.nc.vector.scalar_tensor_tensor(out=h, in0=self.yg[0:ROWS[t], t, j, :],
                                                         scalar=self.route["weight"][0:ROWS[t], t, j:j + 1],
                                                         in1=h, op0=ALU.mult, op1=ALU.add))


def s5_layer(k, zT, gain, rows, glu, route, room):
    with k.phase() as sc:
        def sb(name, shape, dt=F32):
            return k.sb(sc, name, shape, dt)

        s = {
            "uw": sb("s5_uw", [P, G5 * NCH + 4096]),
            "cs": sb("s5_cs", [P, G5, CH + 1, C5]),
            "fs": sb("s5_fs", [P, G5 * P]),
            "e": glu["first"],
            "x": sb("s5_x", [P, NCH, 2, G5]),
            "pb": room[:, 0:2 * C5 * G5].rearrange("p (a c g) -> p a c g", a=2, c=C5),
            "pc": sb("s5_pc", [P, 2, C5, G5]),
            "ar": room[:, 2 * C5 * G5:(2 * C5 + CH + 1) * G5].rearrange("p (j g) -> p j g", g=G5),
            "ai": sb("s5_ai", [P, CH + 1, G5]),
            "d": sb("s5_dcol", [P, KC]),
            "sw": room[:, TILES * D - P:],
        }
        s["work"] = s["uw"][:, G5 * NCH:]
        s["u"] = s["uw"][:, 0:G5 * NCH].rearrange("p (g q) -> p g q", q=NCH)
        spare = s["cs"][:].rearrange("p g j c -> p (g j c)")
        s["spare"] = spare
        s["s0raw"] = spare[0:G5, 3072:3072 + NSEQ * P].rearrange("g (n a p) -> g n a p", n=NSEQ, a=2)
        xf = s["x"][:].rearrange("p q a g -> p (q a g)")
        s["lam"] = xf[0:G5, 0:2 * S5].rearrange("g (a p) -> g a p", a=2)
        s["ldt"] = xf[:, 2 * S5:2 * S5 + G5]
        raw = s["raw"] = s["work"][0:G5, :].rearrange("g (a n) -> g a n", a=4)
        loaded, s0_loaded, stored = k.sem("p_loaded"), k.sem("p_s0"), k.sem("p_stored")
        raws = [k.sem(f"p_raw{i}") for i in range(4)]

        def ahead(sp):
            sp.wait_ge(k.combined[2 * TILES - 1], 16)
            for dst, src in ((s["ldt"], k.i["s5_log_dt"][0].partition_broadcast(P)), (s["lam"][:, 0], k.i["s5_lam_re"][0]),
                             (s["lam"][:, 1], k.i["s5_lam_im"][0]), (s["sw"][:], k.c["swap"])):
                sp.dma_start(dst, src).then_inc(loaded, 16)
            sp.dma_start(s["d"][:], k.i["s5_d"][0].rearrange("(c p) -> p c", p=P), allow_slow_non_contiguous=True
                         ).then_inc(loaded, 16)
            for i, n in enumerate(("s5_b_re", "s5_b_im")):
                sp.dma_start(raw[:, i], k.i[n][0].rearrange("g p c -> g (p c)")).then_inc(raws[i], 16)
            for i, n in enumerate(("s5_c_re", "s5_c_im")):
                sp.dma_start(raw[:, 2 + i], k.i[n][0].rearrange("g c p -> g (c p)")).then_inc(raws[2 + i], 16)
            for i, n in enumerate(("state_s5_re", "state_s5_im")):
                sp.dma_start(s["s0raw"][:, :, i, :], k.i[n][0].rearrange("n g p -> g n p")).then_inc(s0_loaded, 16)

        xn = spare[:, 4096:4096 + TILES * D].rearrange("p (t d) -> p t d", t=TILES)
        yg = s["fs"][:, 0:TILES * 2 * D].rearrange("p (t j d) -> p t j d", t=TILES, j=2)
        norm_phase(k, "n11", gain, "cp", rows, ahead, (xn, stored), gain_at=s["e"][:, 0:D],
                   combine=Combination(k, 0, route, yg))
        s5_prepare_phase(k, s, loaded, raws, s0_loaded, stored)
        s5_scan_phase(k, s, zT, glu)


def s5_prepare_phase(k, s, loaded, raws, s0_loaded, stored):
    nc = k.nc
    V = nc.vector
    with k.phase() as ctx:
        def sb(name, shape, dt=F32):
            return k.sb(ctx, name, shape, dt)

        xc = s["e"][0:NCH, :]
        xg = s["fs"][0:NCH, 0:CH * D]
        raw, lam, ldt, spare, s0raw = (s[n] for n in "raw lam ldt spare s0raw".split())
        names = "lr li dt x ang mag kf a1 a2 sn sh cs den rden nr t1 t2 cor coi ek er eq ep".split()
        e_int = sb("s5_eint", [P, G5], I32)
        v = {n: spare[:, G5 * i:G5 * (i + 1)] for i, n in enumerate(names)}
        pp = spare[:, 2048:2560].rearrange("p (a m g) -> p a m g", a=2, m=4)
        pb = k.ps(ctx, "s5p", [P, 8, 512])
        chunks, zeroed = k.sem("p_chunks"), k.sem("p_zeroed")
        sorted_, turned, copied = k.sem("p_sorted"), k.sem("p_turned"), k.sem("p_copied")
        lam_ps, lam_got, b_ps, c_re_ps, c_im_ps = (k.sem("p_" + n) for n in "lam_ps lam_got b_ps c_re_ps c_im_ps".split())
        SORTS = ((0, 1), (2, 3, 4, 5, 6, 7))
        own_s, e2, a_ok, b_done, c_done, b_used, s0_ps, s0_got = (k.sem("p_" + n) for n in
            "own e2 a_ok b_done c_done b_used s0_ps s0_got".split())
        lo, hi = slice(0, 64), slice(64, 128)

        def bank(i):
            return pb[:, i:i + 2, :].rearrange("p a b -> p (a b)")

        with nc.Block() as block:
            @block.sync
            def _(sp):
                sp.wait_ge(stored, 16 * TILES)
                sp.dma_start(xc, k.d["xn"].rearrange("(q s) d -> q (s d)", s=CH)).then_inc(chunks, 16)

            @block.gpsimd
            def _(pool):
                pool.wait_ge(chunks, 16)
                for i in SORTS[0]:
                    nc.gpsimd.tensor_copy(xg.rearrange("q (g s c) -> q g s c", s=CH, c=C5)[:, :, i, :],
                                          xc[:, i * D:(i + 1) * D].rearrange("q (g c) -> q g c", c=C5)).then_inc(sorted_, 1)
                pool.wait_ge(sorted_, len(SORTS[0]))
                pool.wait_ge(b_done, len(SORTS[1]))
                nc.gpsimd.memset(s["e"][:, G5 * P // 2:], 0.0)

            @block.scalar
            def _(act):
                act.wait_ge(a_ok, 1)
                nc.scalar.activation(v["sn"], v["a2"], ACT.Sin).then_inc(e2, 1)
                nc.scalar.activation(v["sh"], v["a2"], ACT.Sin, scale=0.5).then_inc(e2, 1)
                act.wait_ge(chunks, 16)
                for i in SORTS[1]:
                    nc.scalar.copy(xg.rearrange("q (g s c) -> q g s c", s=CH, c=C5)[:, :, i, :],
                                   xc[:, i * D:(i + 1) * D].rearrange("q (g c) -> q g c", c=C5)).then_inc(b_done, 1)
                pc = s["pc"]
                for made, dst, src, sign in ((c_re_ps, pc[lo, 0], bank(6)[lo], 1.0), (c_re_ps, pc[hi, 1], bank(6)[hi], -1.0),
                                             (c_im_ps, pc[hi, 0], bank(0)[hi], -1.0), (c_im_ps, pc[lo, 1], bank(0)[lo], -1.0)):
                    act.wait_ge(made, 1)
                    nc.scalar.activation(dst.rearrange("p c g -> p (c g)"), src, ACT.Copy, scale=sign).then_inc(c_done, 1)
                for m in range(8):
                    act.wait_ge(turned, m + 1)
                    nc.scalar.copy(s["u"][:, 8 * m:8 * m + 8, :].rearrange("p g q -> p (g q)"), pb[:, 6 + m % 2, 0:8 * NCH]
                                   ).then_inc(copied, 1)
                act.wait_ge(s0_ps, 1)
                nc.scalar.copy(s["x"][:, PCH:, 0], pb[:, 2, :].rearrange("p (n g) -> p n g", g=G5)).then_inc(s0_got, 1)
                act.wait_ge(s0_ps, 2)
                nc.scalar.copy(s["x"][:, PCH:, 1], pb[:, 3, :].rearrange("p (n g) -> p n g", g=G5)).then_inc(s0_got, 1)

            @block.tensor
            def _(pe):
                def both_halves(src, stop_bank, col):
                    last = None
                    for half in range(2):
                        last = nc.tensor.matmul(pb[64 * half:64 * half + 64, stop_bank, col:col + G5], src, k.ident[0:G5, 0:G5],
                                                start=True, stop=True)
                    return last

                pe.wait_ge(loaded, 80)
                for i in range(2):
                    last = both_halves(lam[:, i, :], 0, i * G5)
                last.then_inc(lam_ps, 1)
                for i in range(2):
                    pe.wait_ge(raws[i], 16)
                    for c in range(C5):
                        last = both_halves(raw[:, i, c:1024:C5], 2 + 2 * i + c // 8, (c % 8) * G5)
                last.then_inc(b_ps, 1)
                pe.wait_ge(raws[2], 16)
                for c in range(C5):
                    last = both_halves(raw[:, 2, c * S5:(c + 1) * S5], 6 + c // 8, (c % 8) * G5)
                last.then_inc(c_re_ps, 1)
                pe.wait_ge(raws[3], 16)
                pe.wait_ge(lam_got, 1)
                for c in range(C5):
                    last = both_halves(raw[:, 3, c * S5:(c + 1) * S5], c // 8, (c % 8) * G5)
                last.then_inc(c_im_ps, 1)
                pe.wait_ge(c_done, 2)
                pe.wait_ge(sorted_, len(SORTS[0]))
                pe.wait_ge(b_done, len(SORTS[1]))
                for m in range(8):
                    if m >= 2:
                        pe.wait_ge(copied, m - 1)
                    for i in range(8):
                        g = 8 * m + i
                        last = nc.tensor.transpose(pb[:, 6 + m % 2, i * NCH:(i + 1) * NCH], xg[:, g * P:(g + 1) * P], k.ident[0:NCH, 0:NCH])
                    last.then_inc(turned, 1)
                pe.wait_ge(s0_loaded, 32)
                pe.wait_ge(b_used, 1)
                for n in range(NSEQ):
                    last = nc.tensor.transpose(pb[:, 2, n * G5:(n + 1) * G5], s0raw[:, n].rearrange("g a p -> g (a p)"),
                                               k.ident[0:G5, 0:G5])
                last.then_inc(s0_ps, 1)
                pe.wait_ge(s0_got, 1)
                nc.tensor.matmul(pb[:, 3, :], s["sw"][:], s["x"][:, PCH:, 0], start=True, stop=True
                                 ).then_inc(s0_ps, 1)

            @block.vector
            def _(dve):
                own = Own(dve, own_s)
                tt = V.tensor_tensor

                def st(o, a, scalar, b, op0=ALU.mult, op1=ALU.add):
                    own.do(V.scalar_tensor_tensor(out=v[o], in0=v[a], scalar=scalar, in1=v[b] if b else e_int[:].bitcast(F32),
                                                  op0=op0, op1=op1))

                def do(o, a, b, op):
                    own.do(tt(v[o], v[a], v[b], op))

                def exp(o, x):
                    own.do(V.tensor_scalar(v["ek"], x, 1.0 / np.log(2.0), None, ALU.mult))
                    own.do(V.tensor_scalar(v["ek"], v["ek"], big, None, ALU.add))
                    own.do(V.tensor_scalar(v["ek"], v["ek"], -big, None, ALU.add))
                    own.do(V.tensor_scalar(v["ek"], v["ek"], 127.0, -126.0, ALU.min, ALU.max))
                    own.do(V.scalar_tensor_tensor(out=v["er"], in0=v["ek"], scalar=-0.693359375, in1=x, op0=ALU.mult, op1=ALU.add))
                    st("er", "ek", 2.12194440e-4, "er")
                    own.do(V.tensor_scalar(v["eq"], v["er"], 1.0 / 5040, None, ALU.mult))
                    for f in (720, 120, 24, 6, 2, 1):
                        st("eq", "eq", 1.0 / f, "er", ALU.add, ALU.mult)
                    own.do(V.tensor_scalar(v["ep"], v["ek"], 127.0, None, ALU.add))
                    own.do(V.tensor_copy(e_int[:], v["ep"]))
                    own.do(V.tensor_scalar(e_int[:], e_int[:], 23, None, ALU.logical_shift_left))
                    st(o, "eq", 1.0, None, ALU.add, ALU.mult)

                big = 12582912.0
                dve.wait_ge(loaded, 80)
                exp("dt", ldt[:])
                dve.wait_ge(lam_ps, 1)
                own.inc(V.tensor_copy(v["lr"], pb[:, 0, 0:G5]))
                own.do(V.tensor_copy(v["li"], pb[:, 0, G5:2 * G5]))
                dve.sem_inc(lam_got, 1)
                do("x", "lr", "dt", ALU.mult)
                exp("mag", v["x"])
                do("ang", "li", "dt", ALU.mult)
                own.do(V.tensor_scalar(v["kf"], v["ang"], 1.0 / (2 * np.pi), None, ALU.mult))
                own.do(V.tensor_scalar(v["kf"], v["kf"], big, None, ALU.add))
                own.do(V.tensor_scalar(v["kf"], v["kf"], -big, None, ALU.add))
                st("a1", "kf", -6.28125, "ang")
                st("a2", "kf", -(2 * np.pi - 6.28125), "a1")
                V.tensor_scalar(v["a2"], v["a2"], 3.1415925, -3.1415925, ALU.min, ALU.max).then_inc(a_ok, 1)
                dve.wait_ge(e2, 2)
                do("cs", "sh", "sh", ALU.mult)
                own.do(V.tensor_scalar(v["cs"], v["cs"], -2.0, 1.0, ALU.mult, ALU.add))
                ar, ai = s["ar"], s["ai"]
                own.inc(V.memset(ar[:, 0], 1.0))
                own.inc(V.memset(ai[:, 0], 0.0))
                own.inc(tt(ar[:, 1], v["mag"], v["cs"], ALU.mult))
                own.do(tt(ai[:, 1], v["mag"], v["sn"], ALU.mult))
                for m in (1, 2, 4):
                    r, i = ar[:, 1:1 + m], ai[:, 1:1 + m]
                    br, bi = (a[:, m].unsqueeze(1).broadcast_to([P, m, G5]) for a in (ar, ai))
                    f = [pp[:, j, 0:m] for j in range(2)]
                    own.inc(tt(f[0], r, br, ALU.mult))
                    own.do(tt(f[1], i, bi, ALU.mult))
                    own.do(tt(ar[:, 1 + m:1 + 2 * m], f[0], f[1], ALU.subtract))
                    own.inc(tt(f[0], r, bi, ALU.mult))
                    own.do(tt(f[1], i, br, ALU.mult))
                    own.do(tt(ai[:, 1 + m:1 + 2 * m], f[0], f[1], ALU.add))
                do("t1", "lr", "lr", ALU.mult)
                do("t2", "li", "li", ALU.mult)
                do("den", "t1", "t2", ALU.add)
                own.inc(V.reciprocal(v["rden"], v["den"]))
                own.do(V.tensor_scalar(v["nr"], ar[:, 1], -1.0, None, ALU.add))
                do("t1", "nr", "lr", ALU.mult)
                own.do(tt(v["t2"], ai[:, 1], v["li"], ALU.mult))
                do("t1", "t1", "t2", ALU.add)
                do("cor", "t1", "rden", ALU.mult)
                own.do(tt(v["t1"], ai[:, 1], v["lr"], ALU.mult))
                do("t2", "nr", "li", ALU.mult)
                do("t1", "t1", "t2", ALU.subtract)
                do("coi", "t1", "rden", ALU.mult)
                for made in (b_ps, c_re_ps, c_im_ps):
                    dve.wait_ge(made, 1)
                pbk = s["pb"]
                w = s["work"].rearrange("p (a c g) -> p a c g", a=4, c=C5)
                cor, coi = (v[n].unsqueeze(1).broadcast_to([P, C5, G5]) for n in ("cor", "coi"))
                b_re, b_im = (bank(i).rearrange("p (c g) -> p c g", c=C5) for i in (2, 4))
                for j, (a, b) in enumerate(((b_re, cor), (b_im, coi), (b_im, cor), (b_re, coi))):
                    own.inc(tt(w[:, j], a, b, ALU.mult))
                own.sync()
                dve.sem_inc(b_used, 1)
                own.inc(tt(pbk[lo, 0], w[lo, 0], w[lo, 1], ALU.subtract))
                own.inc(tt(pbk[hi, 0], w[hi, 2], w[hi, 3], ALU.add))
                own.inc(tt(pbk[hi, 1], w[hi, 0], w[hi, 1], ALU.subtract))
                own.do(V.scalar_tensor_tensor(out=pbk[lo, 1], in0=w[lo, 2], scalar=-1.0, in1=w[lo, 3],
                                              op0=ALU.mult, op1=ALU.subtract))


def s5_scan_phase(k, s, zT, glu):
    nc = k.nc
    V, G = nc.vector, nc.gpsimd
    NC2 = G5 * NCH
    with k.phase() as ctx:
        fs = s["fs"][:].rearrange("p (g s c) -> p g s c", s=CH, c=C5)
        prod = s["work"].rearrange("p (a c g) -> p a c g", a=4, c=C5)
        turned_fs = zT[:].rearrange("p c n -> p (c n)")[:, 0:2048].rearrange("p (r n) -> p r n", r=4)
        cc = s["uw"][:, 0:2 * NC2]
        cv = cc.rearrange("p (a g q) -> p a g q", a=2, q=NCH)
        x = s["x"]
        kk = s["e"][:, 0:4096].rearrange("p (t j n) -> p t j n", t=KC, j=CH)
        pad = s["e"][:, 4096:]
        yc = s["fs"][0:NCH, 0:CH * D]
        free = s["uw"][:, 2 * NC2:]
        fin = free[:, 0:576].rearrange("p (n g) -> p n g", g=G5)
        t0 = free[:, 576:704].rearrange("p (a g) -> p a g", a=2)
        t1 = free[:, 704:832].rearrange("p (a g) -> p a g", a=2)
        nai = free[:, 832:896]
        f1 = free[:, 896:1408].rearrange("p (n g) -> p n g", g=G5)
        dd = k.sb(ctx, "s5_dd", [P, KC, 64])
        fout = s["pb"][0:G5].rearrange("g a c n -> g (a c n)")[:, 0:(NSEQ + 1) * P].rearrange("g (n p) -> g n p", p=P)
        ps = k.ps(ctx, "s5_ps", [P, 8, 512])
        fs_v, fs_g, fs_a, cs_v, cs_g, cs_a = (k.sem("q_" + n) for n in "fs_v fs_g fs_a cs_v cs_g cs_a".split())
        own_s, pool_s, padded, skip = (k.sem("q_" + n) for n in "own pool padded skip".split())
        turned, copied, contrib, cc_ok = (k.sem("q_" + n) for n in "turned copied contrib cc_ok".split())
        swapped, icc_ok, kk_ps, kk_ok = (k.sem("q_" + n) for n in "swapped icc_ok kk_ps kk_ok".split())
        own_ps, own_ok, states = (k.sem("q_" + n) for n in "own_ps own_ok states".split())
        cross, cross_ok, y_ps, y_ok = (k.sem("q_" + n) for n in "cross cross_ok y_ps y_ok".split())
        fin_ok, fin_ps, fout_ok, out_s = (k.sem("q_" + n) for n in "fin_ok fin_ps fout_ok out".split())

        def lot(b):
            return 12 * b * NCH, min(12, G5 - 12 * b) * NCH

        def power(eng, own, out, base, j, buf, g):
            n = g.stop - g.start
            t = [prod[:, buf + i, :, g] for i in range(2)]
            for i, a in enumerate((s["ar"], s["ai"])):
                own.inc(eng.tensor_tensor(t[i], base[:, i, :, g], a[:, j, g].unsqueeze(1).broadcast_to([P, C5, n]), ALU.mult))
            own.sync()
            own.do(eng.tensor_tensor(out[:, g].rearrange("p g c -> p c g"), t[0], t[1], ALU.add))

        def powers(eng, own, buf, tokens, steps, fs_sem, cs_sem):
            for quarter in range(4):
                for i in tokens:
                    power(eng, own, fs[:, :, i, :], s["pb"], CH - 1 - i, buf, slice(quarter * G5 // 4, (quarter + 1) * G5 // 4))
                eng.sem_inc(fs_sem, 1)
            for j in steps:
                power(eng, own, s["cs"][:, :, j, :], s["pc"], j, buf, slice(0, G5))
            eng.sem_inc(cs_sem, 1)

        with nc.Block() as block:
            @block.sync
            def _(sp):
                sp.wait_ge(own_ps, KC)
                for n in range(2):
                    load_glu(k, glu, sp, n)

            @block.gpsimd
            def _(pool):
                own = Own(pool, pool_s)
                powers(G, own, 0, (5, 6), (6, 7, 8), fs_g, cs_g)
                for i in range(4):
                    G.tensor_copy(pad.rearrange("p (T n) -> p T n", n=256)[:, :, 80 * i:80 * i + C5],
                                  s["pb"][:, 0].rearrange("p c (T i) -> p T i c", i=4)[:, :, i]).then_inc(padded, 1)
                halves = [k.ident[:, 64 * h:64 * h + 64].unsqueeze(1).broadcast_to([P, KC, 64]) for h in range(2)]
                own.do(G.tensor_tensor(dd[:], halves[0], halves[1], ALU.add))
                own.do(G.tensor_tensor(dd[:], dd[:], s["d"][:].unsqueeze(2).broadcast_to([P, KC, 64]), ALU.mult))
                for t in range(KC):
                    pool.wait_ge(kk_ok, 2 * t + 2)
                    G.tensor_tensor(kk[:, t, 0, :], kk[:, t, 0, :], dd[:, t], ALU.add).then_inc(skip, 1)

            @block.tensor
            def _(pe):
                def turn(m):
                    quarter = m // 4
                    for made in (fs_v, fs_g, fs_a):
                        pe.wait_ge(made, quarter + 1)
                    if m >= 2:
                        pe.wait_ge(copied, m - 1)
                    for i in range(4):
                        g = 4 * m + i
                        last = nc.tensor.transpose(ps[:, m % 2, i * P:(i + 1) * P], s["fs"][:, g * P:(g + 1) * P], k.ident[:])
                    last.then_inc(turned, 1)

                def contributions(m):
                    pe.wait_ge(copied, m + 1)
                    for i in range(4):
                        g = 4 * m + i
                        for h in range(2):
                            last = nc.tensor.matmul(ps[64 * h:64 * h + 64, 2 + g // 12, (g % 12) * NCH:(g % 12 + 1) * NCH],
                                                    turned_fs[:, m % 4, i * P + 64 * h:i * P + 64 * h + 64], s["u"][:, g, :],
                                                    start=True, stop=True)
                    last.then_inc(contrib, 1)

                def swap(b):
                    pe.wait_ge(cc_ok, b + 1)
                    lo, n = lot(b)
                    nc.tensor.matmul(ps[:, 2 + b, 0:n], s["sw"][:], cc[:, lo:lo + n], start=True, stop=True).then_inc(swapped, 1)

                turn(0)
                for m in range(16):
                    if m + 1 < 16:
                        turn(m + 1)
                    contributions(m)
                    if m >= 5 and (m - 5) % 3 == 0:
                        swap((m - 5) // 3)
                swap(4)
                swap(5)
                pe.wait_ge(padded, 4)
                pe.wait_ge(icc_ok, 5)
                for made in (cs_v, cs_g, cs_a):
                    pe.wait_ge(made, 1)
                for t in range(KC):
                    if t >= 2:
                        pe.wait_ge(kk_ok, 2 * t - 2)
                    for i in range(4):
                        for h in range(2):
                            g = 8 * t + 4 * h + i
                            last = nc.tensor.matmul(ps[64 * h:64 * h + 64, 5 + t % 2, i * P:(i + 1) * P], pad[:, 64 * g:64 * g + 64],
                                                    s["cs"][:, g, 0:CH, :].rearrange("p j c -> p (j c)"), start=True, stop=True)
                    last.then_inc(kk_ps, 1)
                pe.wait_ge(icc_ok, 6)
                for t in range(KC):
                    pe.wait_ge(skip, t + 1)
                    if t >= 2:
                        pe.wait_ge(own_ok, 2 * t - 2)
                    for j in range(CH):
                        for h in range(2):
                            r = slice(64 * h, 64 * h + 64)
                            y = ps[r, 2 * (t % 2) + h, 0:NTOK].rearrange("p (q s) -> p q s", s=CH)
                            u = k.xT[r, t, :].rearrange("p (q s) -> p q s", s=CH)
                            last = nc.tensor.matmul(y[:, :, j:CH], kk[r, t, j, :], u[:, :, 0:CH - j], start=j == 0, stop=j == CH - 1)
                    last.then_inc(own_ps, 1)
                pe.wait_ge(states, 1)
                pe.wait_ge(kk_ok, 2 * KC)
                for m in range(16):
                    if m >= 4:
                        pe.wait_ge(cross_ok, m - 3)
                    for i in range(4):
                        g = 4 * m + i
                        last = nc.tensor.matmul(ps[0:NCH, 4 + m % 4, i * P:(i + 1) * P], x[:, :, 0, g],
                                                s["cs"][:, g, 1:CH + 1, :].rearrange("p s c -> p (s c)"), start=True, stop=True)
                    last.then_inc(cross, 1)
                pe.wait_ge(cross_ok, 16)
                pe.wait_ge(own_ok, 2 * KC)
                pe.wait_ge(fin_ok, 1)
                for n in range(NSEQ + 1):
                    last = nc.tensor.transpose(ps[0:G5, 4 + n // 4, (n % 4) * P:(n % 4 + 1) * P], fin[:, n, :], k.ident[:])
                last.then_inc(fin_ps, 1)
                for t in range(KC):
                    if t >= 2:
                        pe.wait_ge(y_ok, t - 1)
                    for i in range(CH):
                        last = nc.tensor.transpose(ps[:, t % 2, i * NCH:(i + 1) * NCH], yc[:, i * D + t * P:i * D + (t + 1) * P],
                                                   k.ident[0:NCH, 0:NCH])
                    last.then_inc(y_ps, 1)

            @block.scalar
            def _(act):
                S = nc.scalar
                S.copy(fs[:, :, CH - 1, :], s["pb"][:, 0].rearrange("p c g -> p g c")).then_inc(fs_a, 4)
                S.copy(s["cs"][:, :, 0, :], s["pc"][:, 0].rearrange("p c g -> p g c")).then_inc(cs_a, 1)

                def leave(b):
                    act.wait_ge(contrib, min(3 * b + 3, 16))
                    lo, n = lot(b)
                    S.copy(cc[:, lo:lo + n], ps[:, 2 + b, 0:n]).then_inc(cc_ok, 1)

                for m in range(16):
                    act.wait_ge(turned, m + 1)
                    if m >= 4:
                        act.wait_ge(contrib, m - 3)
                    S.copy(turned_fs[:, m % 4], ps[:, m % 2, :]).then_inc(copied, 1)
                    if m >= 4 and (m - 4) % 3 == 0:
                        leave((m - 4) // 3)
                leave(4)
                leave(5)
                act.wait_ge(cs_v, 1)
                act.wait_ge(cs_g, 1)
                for b in range(6):
                    act.wait_ge(swapped, b + 1)
                    lo, n = lot(b)
                    S.copy(cc[:, NC2 + lo:NC2 + lo + n], ps[:, 2 + b, 0:n]).then_inc(icc_ok, 1)
                for t in range(KC):
                    act.wait_ge(kk_ps, t + 1)
                    for h in range(2):
                        r = slice(64 * h, 64 * h + 64)
                        S.copy(kk[r, t].rearrange("p j (i c) -> p i j c", c=C5),
                               ps[r, 5 + t % 2, :].rearrange("p (i j c) -> p i j c", i=4, c=C5)).then_inc(kk_ok, 1)
                for t in range(KC):
                    act.wait_ge(own_ps, t + 1)
                    for h in range(2):
                        r = slice(64 * h, 64 * h + 64)
                        S.copy(zT[r, t, :], ps[r, 2 * (t % 2) + h, 0:NTOK]).then_inc(own_ok, 1)
                for m in range(16):
                    act.wait_ge(cross, m + 1)
                    S.copy(yc.rearrange("q (s g c) -> q g s c", s=CH, c=C5)[:, 4 * m:4 * m + 4],
                           ps[0:NCH, 4 + m % 4, :].rearrange("q (g s c) -> q g s c", g=4, c=C5)).then_inc(cross_ok, 1)
                act.wait_ge(fin_ps, 1)
                S.copy(fout.rearrange("g n p -> g (n p)"), ps[0:G5, 4:7, :].rearrange("g a b -> g (a b)")[:, 0:(NSEQ + 1) * P]
                       ).then_inc(fout_ok, 1)
                act.wait_ge(fout_ok, 1)
                for i, n in enumerate(("re", "im")):
                    act.dma_start(k.o[f"s5_{n}_prompt"][0, 0], fout[:, 0, i * S5:(i + 1) * S5]).then_inc(out_s, 16)
                    act.dma_start(k.o[f"s5_{n}_sample"][0].rearrange("n g p -> g n p"), fout[:, 1:, i * S5:(i + 1) * S5]
                                  ).then_inc(out_s, 16)
                for t in range(KC):
                    act.wait_ge(y_ok, t + 1)
                    S.activation(zT[:, t, :], zT[:, t, :], ACT.Gelu_apprx_tanh)
                act.wait_ge(out_s, 64)

            @block.vector
            def _(dve):
                own = Own(dve, own_s)
                tt = V.tensor_tensor
                powers(V, own, 2, range(5), range(1, 6), fs_v, cs_v)
                ar8, ai8 = s["ar"][:, CH], s["ai"][:, CH]
                ar2 = ar8.unsqueeze(1).broadcast_to([P, 2, G5])
                own.inc(V.tensor_scalar(nai, ai8, -1.0, None, ALU.mult))
                own.do(V.memset(x[:, 0], 0.0))
                dve.wait_ge(icc_ok, 6)
                for q in range(PCH):
                    own.inc(tt(t0, x[:, q], ar2, ALU.mult))
                    own.inc(tt(t1[:, 0], x[:, q, 1], ai8, ALU.mult))
                    own.inc(tt(t1[:, 1], x[:, q, 0], nai, ALU.mult))
                    dve.wait_ge(own_s, own.n - 2)
                    own.do(tt(t0, t0, cv[:, :, :, q], ALU.add))
                    if q + 1 < PCH:
                        own.do(tt(x[:, q + 1], t0, t1, ALU.add))
                    else:
                        own.do(tt(fin[:, 0], t0[:, 0], t1[:, 0], ALU.add))
                dve.sem_inc(states, 1)
                own.inc(tt(f1, x[:, PCH:, 0], ar8.unsqueeze(1).broadcast_to([P, NSEQ, G5]), ALU.mult))
                own.do(tt(fin[:, 1:], x[:, PCH:, 1], ai8.unsqueeze(1).broadcast_to([P, NSEQ, G5]), ALU.mult))
                own.do(tt(f1, f1, fin[:, 1:], ALU.add))
                own.do(tt(fin[:, 1:], f1, cv[:, 0, :, PCH:NCH].rearrange("p g n -> p n g"), ALU.add))
                dve.sem_inc(fin_ok, 1)
                dve.wait_ge(own_ok, 2 * KC)
                for t in range(KC):
                    dve.wait_ge(y_ps, t + 1)
                    z = zT[:, t, :].rearrange("p (q s) -> p q s", s=CH)
                    tt(z, ps[:, t % 2, 0:NTOK].rearrange("p (s q) -> p q s", q=NCH), z, ALU.add).then_inc(y_ok, 1)


def load_glu(k, glu, sp, n):
    col = (0, 1024, 512, 1536)[n]
    w = k.i["s5_w_glu"][0].rearrange("(c p) n -> p c n", p=P)
    sp.dma_start(glu["blocks"][n], w[:, :, col:col + 512]).then_inc(glu["ready"][n], 16)


def glu_phase(k, zT, glu, behind):
    nc = k.nc
    V = nc.vector
    with k.phase() as ctx:
        rest = k.sb(ctx, "wg_rest", [P, 2, KC, 512])
        glu["blocks"] += [rest[:, 0], rest[:, 1]]
        wg, ready = glu["blocks"], glu["ready"]
        bias = k.sb(ctx, "bglu", [P, 2 * D])
        a = k.sb(ctx, "glu_a", [P, 2, 512])
        b = k.sb(ctx, "glu_b", [P, 2, 512])
        acc = k.ps(ctx, "glu_ps", [P, 4, 2, 512])
        bias_in, done, linear, sig, own_s = (k.sem("glu_" + n) for n in "bias done linear sig own".split())
        units = [(t, half) for half in range(2) for t in range(TILES)]
        with nc.Block() as block:
            @block.sync
            def _(sp):
                sp.dma_start(bias[:], k.i["s5_b_glu"][0].partition_broadcast(P)).then_inc(bias_in, 16)
                for n in range(2, 4):
                    load_glu(k, glu, sp, n)
                behind(sp)

            @block.tensor
            def _(pe):
                for m, (t, half) in enumerate(units):
                    if m >= 4:
                        pe.wait_ge(linear, m - 3)
                    for part in range(2):
                        pe.wait_ge(ready[2 * half + part], 16)
                        if t == 2:
                            continue
                        for c in range(KC):
                            last = nc.tensor.matmul(acc[:, m % 4, part, :], zT[:, c, P * t:P * (t + 1)],
                                                    wg[2 * half + part][:, c, :], start=c == 0, stop=c == KC - 1)
                    if t == 2:
                        for c in range(KC):
                            for part in range(2):
                                last = nc.tensor.matmul(acc[64 * part:64 * part + 64, m % 4, 0, :], zT[:, c, 256:320],
                                                        wg[2 * half + part][:, c, :], start=c == 0, stop=c == KC - 1)
                    last.then_inc(done, 1)

            @block.scalar
            def _(act):
                for m, (t, half) in enumerate(units):
                    act.wait_ge(linear, m + 1)
                    nc.scalar.activation(b[0:ROWS[t], m % 2, :], b[0:ROWS[t], m % 2, :], ACT.Sigmoid).then_inc(sig, 1)

            @block.vector
            def _(dve):
                own = Own(dve, own_s)
                dve.wait_ge(bias_in, 16)

                def gate(m):
                    t, half = units[m]
                    r = ROWS[t]
                    dve.wait_ge(sig, m + 1)
                    own.do(V.tensor_tensor(a[0:r, m % 2], a[0:r, m % 2], b[0:r, m % 2], ALU.mult))
                    h = k.h[0:r, t, half * 512:(half + 1) * 512]
                    own.do(V.tensor_tensor(h, h, a[0:r, m % 2], ALU.add))

                for m, (t, half) in enumerate(units):
                    r = ROWS[t]
                    dve.wait_ge(done, m + 1)
                    own.do(V.tensor_tensor(a[0:r, m % 2], acc[0:r, m % 4, 0], bias[0:r, half * 512:(half + 1) * 512], ALU.add))
                    b_ps = acc[64:128, m % 4, 0] if t == 2 else acc[0:r, m % 4, 1]
                    V.tensor_tensor(b[0:r, m % 2], b_ps, bias[0:r, D + half * 512:D + (half + 1) * 512],
                                    ALU.add).then_inc(linear, 1)
                    if m:
                        gate(m - 1)
                gate(len(units) - 1)


def final_norm(k, route):
    yp = k.o["y_prompt"].rearrange("b (t p) d -> t p (b d)", p=P)
    with ExitStack() as ctx:
        yg = k.sb(ctx, "yg", [P, TILES, 2, D])
        norm_phase(k, "nf", k.i["norm_f"], None, [yp[0], yp[1], k.o["y_sample"].rearrange("n t d -> (n t) d")],
                   combine=Combination(k, 1, route, yg))


def program(nc, ins, outs, consts, scratch):
    k = Core(nc, ins, outs, consts, scratch)
    with ExitStack() as ctx:
        k.lasting_semaphores(ctx)
        k.h = k.sb(ctx, "h", [P, TILES, D])
        k.ident = k.sb(ctx, "ident", [P, P])
        rows = [scratch["xn"][P * t:P * t + ROWS[t], :] for t in range(TILES)]
        routes = [moe_route(k, ctx, li) for li in range(2)]
        with ExitStack() as memory:
            place = TokenRows(k, memory, 0)
            mix = place.mix
            with k.phase() as qc:
                z = k.sb(qc, "z", [P, TILES, IN_W])
                qt = k.sb(qc, "qt", [P, 16, NTOK])
                tables, tables_ready, load_tables = mixer_tables(k, qc)
                with ExitStack() as xc:
                    k.xT = k.sb(xc, "xT0", [P, KC, NTOK])
                    in_proj_phases(k, z, ins["norm1"][0], mix, qt, load_tables)
                even_mixer_phase(k, z, mix, qt, tables, tables_ready)
            weights = ExpertWeights(k, 0)
            early = [(which, b) for b in range(2) for which in ("w13", "w2")]
            weights.place(memory, *early)
            out_proj_phase(k, mix, lambda sp: weights.start(sp, *early))
            moe_layer(k, 0, rows, routes[0], weights, place)
        k.clear()
        with ExitStack() as memory:
            place = TokenRows(k, memory, 1)
            first = k.sb(memory, "wg_first", [P, KC, 2 * DE])
            with k.phase():
                zT = place.xT
                flat = first[:].rearrange("p c n -> p (c n)")
                glu = {"first": flat, "blocks": [flat[:, 4096 * n:4096 * (n + 1)].rearrange("p (c n) -> p c n", c=KC) for n in range(2)],
                       "ready": [k.sem(f"glu_w{n}") for n in range(4)]}
                with ExitStack() as xc:
                    k.xT = k.sb(xc, "xT1", [P, KC, NTOK])
                    s5_layer(k, zT, ins["norm1"][1], rows, glu, routes[0],
                             place.all[:, KC * NTOK:])
                weights = ExpertWeights(k, 1, first)
                early = [("w13", 0), ("w2", 0), ("w13", 1)]
                weights.place(memory, *early)
                glu_phase(k, zT, glu, lambda sp: weights.start(sp, *early))
            moe_layer(k, 1, rows, routes[1], weights, place)
        final_norm(k, routes[1])


INPUTS = ("x_prompt", "x_sample", "cache_k", "cache_v", "state_ret", "state_s5_re", "state_s5_im", "page_table",
          "norm1", "norm2", "norm_f", "w_in_even", "w_out_even", "s5_lam_re", "s5_lam_im", "s5_log_dt", "s5_b_re",
          "s5_b_im", "s5_c_re", "s5_c_im", "s5_d", "s5_w_glu", "s5_b_glu", "moe_w_group", "moe_b_group",
          "moe_w_expert", "moe_b_expert", "moe_w13", "moe_w2")
OUTPUTS = (("y_prompt", (1, 256, D)), ("y_sample", (NSEQ, DSEQ, D)),
           ("k_prompt", (1, 1, 2, PAGE, H, HD)), ("v_prompt", (1, 1, 2, PAGE, H, HD)),
           ("k_sample", (1, NSEQ, DSEQ, H, HD)), ("v_sample", (1, NSEQ, DSEQ, H, HD)),
           ("ret_prompt", (1, 1, H, DK, DV)), ("ret_sample", (1, NSEQ, H, DK, DV)),
           ("s5_re_prompt", (1, 1, G5, S5)), ("s5_im_prompt", (1, 1, G5, S5)),
           ("s5_re_sample", (1, NSEQ, G5, S5)), ("s5_im_sample", (1, NSEQ, G5, S5)))
SCRATCH = (("xn", (NTOK, D)), ("smix", (NSEQ // 2, P, HD)), ("yblk", ((NBLK - BUFS) * SLOT, D)))


def kernel(**inputs):
    from concourse import bacc
    from concourse.bass_utils import run_bass_kernel_spmd

    nc = bacc.Bacc("TRN2", target_bir_lowering=False, num_devices=1)
    arrays, ins, consts = {}, {}, {}
    for name in INPUTS:
        a = np.ascontiguousarray(inputs[name])
        arrays["in_" + name] = a
        ins[name] = nc.dram_tensor("in_" + name, a.shape, mybir.dt.from_np(a.dtype), kind="ExternalInput").ap()
    for name, a in constants().items():
        arrays["table_" + name] = np.ascontiguousarray(a)
        consts[name] = nc.dram_tensor("table_" + name, a.shape, F32, kind="ExternalInput").ap()
    outs = {n: nc.dram_tensor("out_" + n, s, F32, kind="ExternalOutput").ap() for n, s in OUTPUTS}
    scratch = {n: nc.dram_tensor("scratch_" + n, s, F32).ap() for n, s in SCRATCH}
    program(nc, ins, outs, consts, scratch)
    r = run_bass_kernel_spmd(nc, [arrays], core_ids=[0])
    return tuple(r.results[0]["out_" + n] for n, _ in OUTPUTS)
```
